# Optimizing a Trainium2 kernel written in Bass

```python
import math
import jax, jax.numpy as jnp
from jax import lax
import numpy as np

D_MODEL = 1024
BATCH = 1
SEQ = 512
DEPTH = 2

CHUNK = 64
Q_BLOCK = 128
N_A_LAYERS = DEPTH // 2
N_B_LAYERS = DEPTH - N_A_LAYERS
HEAD_DIM = 64
FOX_HEADS = D_MODEL // HEAD_DIM
DIFF_HEADS = D_MODEL // (2 * HEAD_DIM)
DIFF_V_DIM = 2 * HEAD_DIM
D_FF = 2816
CONV_WIDTH = 3
ROPE_THETA = 10000.0
LN_EPS = 1e-5
RMS_EPS = 1e-5
DN_ALPHA = (2 * DEPTH) ** 0.25
DN_BETA = (8 * DEPTH) ** -0.25


def _layer_norm(x, g, b):
    xf = x.astype(jnp.float32)
    mu = jnp.mean(xf, axis=-1, keepdims=True)
    var = jnp.mean(jnp.square(xf - mu), axis=-1, keepdims=True)
    y = (xf - mu) * lax.rsqrt(var + LN_EPS)
    return (y * g.astype(jnp.float32) + b.astype(jnp.float32)).astype(x.dtype)

def _rope_tables(seq_len):
    inv_freq = 1.0 / (ROPE_THETA ** (jnp.arange(0, HEAD_DIM, 2, dtype=jnp.float32) / HEAD_DIM))
    ang = jnp.arange(seq_len, dtype=jnp.float32)[:, None] * inv_freq[None, :]
    return jnp.cos(ang), jnp.sin(ang)

def _apply_rope(t, cos, sin):
    half = t.shape[-1] // 2
    t1, t2 = t[..., :half], t[..., half:]
    c = cos.astype(t.dtype)
    s = sin.astype(t.dtype)
    return jnp.concatenate([t1 * c - t2 * s, t2 * c + t1 * s], axis=-1)

def _heads(t, n_heads, d):
    b, s, _ = t.shape
    return t.reshape(b, s, n_heads, d).transpose(0, 2, 1, 3)

def _merge_blocks(o):
    nb, b, h, qb, dv = o.shape
    return o.transpose(1, 0, 3, 2, 4).reshape(b, nb * qb, h * dv)

def _fox_attention(x, w_in, b_f, w_out):
    b, s, d = x.shape
    proj = x @ w_in
    q = _heads(proj[..., :d], FOX_HEADS, HEAD_DIM)
    k = _heads(proj[..., d:2 * d], FOX_HEADS, HEAD_DIM)
    v = _heads(proj[..., 2 * d:3 * d], FOX_HEADS, HEAD_DIM)
    f_logit = proj[..., 3 * d:].astype(jnp.float32) + b_f.astype(jnp.float32)
    c = jnp.cumsum(jax.nn.log_sigmoid(f_logit), axis=1).transpose(0, 2, 1)
    scale = HEAD_DIM ** -0.5
    kpos = jnp.arange(s)

    def block(i):
        start = i * Q_BLOCK
        qb = lax.dynamic_slice_in_dim(q, start, Q_BLOCK, axis=2)
        cb = lax.dynamic_slice_in_dim(c, start, Q_BLOCK, axis=2)
        logits = jnp.einsum('bhqd,bhkd->bhqk', qb, k).astype(jnp.float32) * scale
        logits = logits + cb[..., :, None] - c[..., None, :]
        qpos = start + jnp.arange(Q_BLOCK)
        mask = kpos[None, :] <= qpos[:, None]
        p = jax.nn.softmax(jnp.where(mask, logits, -jnp.inf), axis=-1).astype(v.dtype)
        return jnp.einsum('bhqk,bhkd->bhqd', p, v)

    o = lax.map(block, jnp.arange(s // Q_BLOCK))
    return _merge_blocks(o) @ w_out

def _shared_kv(x, w_kv, cos, sin):
    b, s, _ = x.shape
    kw = 2 * DIFF_HEADS * HEAD_DIM
    proj = x @ w_kv
    k = proj[..., :kw].reshape(b, s, 2, DIFF_HEADS, HEAD_DIM).transpose(2, 0, 3, 1, 4)
    k1 = _apply_rope(k[0], cos, sin)
    k2 = _apply_rope(k[1], cos, sin)
    v = _heads(proj[..., kw:], DIFF_HEADS, DIFF_V_DIM)
    return k1, k2, v

def _diff_attention(x, k1, k2, v, w_q, lam_p, subln_g, w_out, lambda_init, cos, sin):
    b, s, _ = x.shape
    qp = (x @ w_q).reshape(b, s, 2, DIFF_HEADS, HEAD_DIM).transpose(2, 0, 3, 1, 4)
    q1 = _apply_rope(qp[0], cos, sin)
    q2 = _apply_rope(qp[1], cos, sin)
    lp = lam_p.astype(jnp.float32)
    lam = jnp.exp(jnp.sum(lp[0] * lp[1])) - jnp.exp(jnp.sum(lp[2] * lp[3])) + lambda_init
    scale = HEAD_DIM ** -0.5
    kpos = jnp.arange(s)

    def block(i):
        start = i * Q_BLOCK
        qb1 = lax.dynamic_slice_in_dim(q1, start, Q_BLOCK, axis=2)
        qb2 = lax.dynamic_slice_in_dim(q2, start, Q_BLOCK, axis=2)
        qpos = start + jnp.arange(Q_BLOCK)
        mask = kpos[None, :] < ((qpos // CHUNK) + 1)[:, None] * CHUNK
        s1 = jnp.einsum('bhqd,bhkd->bhqk', qb1, k1).astype(jnp.float32) * scale
        s2 = jnp.einsum('bhqd,bhkd->bhqk', qb2, k2).astype(jnp.float32) * scale
        p1 = jax.nn.softmax(jnp.where(mask, s1, -jnp.inf), axis=-1)
        p2 = jax.nn.softmax(jnp.where(mask, s2, -jnp.inf), axis=-1)
        a = (p1 - lam * p2).astype(v.dtype)
        return jnp.einsum('bhqk,bhkd->bhqd', a, v)

    o = lax.map(block, jnp.arange(s // Q_BLOCK)).astype(jnp.float32)
    o = o * lax.rsqrt(jnp.mean(jnp.square(o), axis=-1, keepdims=True) + RMS_EPS)
    o = (o * subln_g.astype(jnp.float32) * (1.0 - lambda_init)).astype(x.dtype)
    return _merge_blocks(o) @ w_out

def _conv_ffn(x, w_in, conv_w, conv_b, w_out):
    s = x.shape[1]
    u = x @ w_in
    up = jnp.pad(u, ((0, 0), (CONV_WIDTH - 1, 0), (0, 0)))
    u = sum(conv_w[j] * up[:, j:j + s] for j in range(CONV_WIDTH)) + conv_b
    g, val = u[..., :D_FF], u[..., D_FF:]
    return (jax.nn.silu(g) * val) @ w_out

def first_inputs(seed: int = 0) -> dict:
    key = jax.random.key(seed)
    ks = jax.random.split(key, 20)
    d = D_MODEL
    f32 = jnp.float32
    nrm = lambda k, shape, sc: jax.random.normal(k, shape, f32) * sc
    return {
        'x': jax.random.normal(ks[0], (BATCH, SEQ, d), f32),
        'a_w_in': nrm(ks[1], (N_A_LAYERS, d, 3 * d + FOX_HEADS), d ** -0.5),
        'a_b_f': jax.random.uniform(ks[2], (N_A_LAYERS, FOX_HEADS), f32, 1.0, 6.0),
        'a_w_out': nrm(ks[3], (N_A_LAYERS, d, d), DN_BETA * d ** -0.5),
        'kv_w': nrm(ks[4], (d, 2 * DIFF_HEADS * HEAD_DIM + DIFF_HEADS * DIFF_V_DIM), d ** -0.5),
        'b_w_q': nrm(ks[5], (N_B_LAYERS, d, 2 * DIFF_HEADS * HEAD_DIM), d ** -0.5),
        'b_lambda': nrm(ks[6], (N_B_LAYERS, 4, HEAD_DIM), 0.1),
        'b_subln_g': 1.0 + nrm(ks[7], (N_B_LAYERS, DIFF_V_DIM), 0.02),
        'b_w_out': nrm(ks[8], (N_B_LAYERS, DIFF_HEADS * DIFF_V_DIM, d), DN_BETA * d ** -0.5),
        'ffn_w_in': nrm(ks[9], (DEPTH, d, 2 * D_FF), d ** -0.5),
        'ffn_conv_w': nrm(ks[10], (DEPTH, CONV_WIDTH, 2 * D_FF), CONV_WIDTH ** -0.5),
        'ffn_conv_b': nrm(ks[11], (DEPTH, 2 * D_FF), 0.02),
        'ffn_w_out': nrm(ks[12], (DEPTH, D_FF, d), DN_BETA * D_FF ** -0.5),
        'ln_attn_g': 1.0 + nrm(ks[13], (DEPTH, d), 0.02),
        'ln_attn_b': nrm(ks[14], (DEPTH, d), 0.02),
        'ln_ffn_g': 1.0 + nrm(ks[15], (DEPTH, d), 0.02),
        'ln_ffn_b': nrm(ks[16], (DEPTH, d), 0.02),
    }

def first_block(x, a_w_in, a_b_f, a_w_out, kv_w, b_w_q, b_lambda, b_subln_g, b_w_out,
              ffn_w_in, ffn_conv_w, ffn_conv_b, ffn_w_out,
              ln_attn_g, ln_attn_b, ln_ffn_g, ln_ffn_b):
    cos, sin = _rope_tables(x.shape[1])
    k1 = k2 = v = None
    for layer in range(DEPTH):
        if layer < N_A_LAYERS:
            h = _fox_attention(x, a_w_in[layer], a_b_f[layer], a_w_out[layer])
        else:
            j = layer - N_A_LAYERS
            lambda_init = 0.8 - 0.6 * math.exp(-0.3 * layer)
            h = _diff_attention(x, k1, k2, v, b_w_q[j], b_lambda[j], b_subln_g[j], b_w_out[j],
                                lambda_init, cos, sin)
        x = _layer_norm(DN_ALPHA * x + h, ln_attn_g[layer], ln_attn_b[layer])
        f = _conv_ffn(x, ffn_w_in[layer], ffn_conv_w[layer], ffn_conv_b[layer], ffn_w_out[layer])
        x = _layer_norm(DN_ALPHA * x + f, ln_ffn_g[layer], ln_ffn_b[layer])
        if layer == N_A_LAYERS - 1:
            k1, k2, v = _shared_kv(x, kv_w, cos, sin)
    return x


DEPTH_2 = 1

GRID_W = 64
N_Q_HEADS = 8
N_KV_HEADS = 2
Q_PER_KV = N_Q_HEADS // N_KV_HEADS
ATTN_WIDTH = N_Q_HEADS * HEAD_DIM
KV_WIDTH = N_KV_HEADS * HEAD_DIM
AXIAL_DIM = HEAD_DIM // 2
SSD_D_INNER = D_MODEL
SSD_HEADDIM = 64
SSD_HEADS = SSD_D_INNER // SSD_HEADDIM
SSD_GROUPS = 2
SSD_HEADS_PER_GROUP = SSD_HEADS // SSD_GROUPS
SSD_STATE = 128
CONV_K = 5
CHUNK_2 = 128
CONV_CH = SSD_D_INNER + 2 * SSD_GROUPS * SSD_STATE
N_BRANCH = 2
D_FF_2 = ((8 * D_MODEL // 3 + 255) // 256) * 256
EPS = 1e-6
IN_SPLITS = (ATTN_WIDTH, KV_WIDTH, KV_WIDTH, SSD_D_INNER, CONV_CH, 2 * SSD_HEADS, N_BRANCH * D_MODEL)
D_IN_PROJ = sum(IN_SPLITS)


def rms_norm(x, g):
    xf = x.astype(jnp.float32)
    xf = xf * lax.rsqrt(jnp.mean(xf * xf, axis=-1, keepdims=True) + EPS)
    return (xf * g.astype(jnp.float32)).astype(x.dtype)

def split_cols(h, sizes):
    idx = np.cumsum(np.array(sizes[:-1]))
    return jnp.split(h, [int(i) for i in idx], axis=-1)

def axial_angles(seq_len):
    rows = seq_len // GRID_W
    row_idx = jnp.repeat(jnp.arange(rows, dtype=jnp.float32), GRID_W)
    col_idx = jnp.tile(jnp.arange(GRID_W, dtype=jnp.float32), rows)
    inv_freq = ROPE_THETA ** (-jnp.arange(0, AXIAL_DIM, 2, dtype=jnp.float32) / AXIAL_DIM)
    ang_row = row_idx[:, None] * inv_freq[None, :]
    ang_col = col_idx[:, None] * inv_freq[None, :]
    return ang_row, ang_col

def rotate(xh, ang):
    half = xh.shape[-1] // 2
    x1, x2 = xh[..., :half], xh[..., half:]
    cos, sin = jnp.cos(ang).astype(xh.dtype), jnp.sin(ang).astype(xh.dtype)
    return jnp.concatenate([x1 * cos - x2 * sin, x2 * cos + x1 * sin], axis=-1)

def axial_rope(x, ang_row, ang_col):
    shp = (1, x.shape[1]) + (1,) * (x.ndim - 3) + (AXIAL_DIM // 2,)
    xr = rotate(x[..., :AXIAL_DIM], ang_row.reshape(shp))
    xc = rotate(x[..., AXIAL_DIM:], ang_col.reshape(shp))
    return jnp.concatenate([xr, xc], axis=-1)

def gqa_attention(q, k, v):
    b, s = q.shape[0], q.shape[1]
    nblk = s // Q_BLOCK
    scale = 1.0 / math.sqrt(HEAD_DIM)
    qb = jnp.moveaxis(q.reshape(b, nblk, Q_BLOCK, N_KV_HEADS, Q_PER_KV, HEAD_DIM), 1, 0)

    def block(q_blk):
        sc = jnp.einsum("bqkgd,bskd->bkgqs", q_blk, k).astype(jnp.float32) * scale
        p = jax.nn.softmax(sc, axis=-1).astype(v.dtype)
        return jnp.einsum("bkgqs,bskd->bqkgd", p, v)

    out = lax.map(block, qb)
    return jnp.moveaxis(out, 0, 1).reshape(b, s, ATTN_WIDTH)

def ssd_chunked(xs, dt, a, bm, cm):
    b, l, g, r, p = xs.shape
    n = bm.shape[-1]
    c = l // CHUNK_2
    xd = (xs * dt[..., None]).reshape(b, c, CHUNK_2, g, r, p)
    adt = jnp.moveaxis((dt * a).reshape(b, c, CHUNK_2, g, r), 2, -1)
    bc = bm.reshape(b, c, CHUNK_2, g, n)
    cc = cm.reshape(b, c, CHUNK_2, g, n)
    a_cs = jnp.cumsum(adt, axis=-1)
    tri = jnp.tril(jnp.ones((CHUNK_2, CHUNK_2), dtype=bool))
    seg = a_cs[..., :, None] - a_cs[..., None, :]
    decay_in = jnp.exp(jnp.where(tri, seg, -jnp.inf))
    cb = jnp.einsum("bclgn,bcsgn->bcgls", cc, bc)
    y_diag = jnp.einsum("bcgls,bcgrls,bcsgrp->bclgrp", cb, decay_in, xd)
    decay_states = jnp.exp(a_cs[..., -1:] - a_cs)
    states = jnp.einsum("bclgn,bcgrl,bclgrp->bcgrpn", bc, decay_states, xd)
    chunk_decay = jnp.exp(a_cs[..., -1])

    def step(h, inp):
        st, dec = inp
        return h * dec[..., None, None] + st, h

    h0 = jnp.zeros((b, g, r, p, n), dtype=xs.dtype)
    _, prev = lax.scan(step, h0, (jnp.moveaxis(states, 1, 0), jnp.moveaxis(chunk_decay, 1, 0)))
    prev = jnp.moveaxis(prev, 0, 1)
    y_off = jnp.einsum("bclgn,bcgrpn,bcgrl->bclgrp", cc, prev, jnp.exp(a_cs))
    return (y_diag + y_off).reshape(b, l, g, r, p)

def centred_depthwise_conv(u, w, bias):
    pad = (CONV_K - 1) // 2
    out = lax.conv_general_dilated(
        u, w[:, None, :].astype(u.dtype), window_strides=(1,), padding=[(pad, pad)],
        dimension_numbers=("NWC", "WIO", "NWC"), feature_group_count=u.shape[-1])
    return out + bias

def ssd_branch(z, xbc, dt_raw, conv_w, conv_b, dt_bias_f, dt_bias_b, a_log_f, a_log_b, d_skip, ssd_norm):
    b, l, _ = z.shape
    xbc = jax.nn.silu(centred_depthwise_conv(xbc, conv_w, conv_b))
    xs, bm, cm = split_cols(xbc, (SSD_D_INNER, SSD_GROUPS * SSD_STATE, SSD_GROUPS * SSD_STATE))
    f32 = jnp.float32
    xs = xs.astype(f32).reshape(b, l, SSD_GROUPS, SSD_HEADS_PER_GROUP, SSD_HEADDIM)
    bm = bm.astype(f32).reshape(b, l, SSD_GROUPS, SSD_STATE)
    cm = cm.astype(f32).reshape(b, l, SSD_GROUPS, SSD_STATE)
    dt_raw = dt_raw.astype(f32)
    shp = (SSD_GROUPS, SSD_HEADS_PER_GROUP)
    dt_f = jax.nn.softplus(dt_raw[..., :SSD_HEADS] + dt_bias_f.astype(f32)).reshape(b, l, *shp)
    dt_b = jax.nn.softplus(dt_raw[..., SSD_HEADS:] + dt_bias_b.astype(f32)).reshape(b, l, *shp)
    a_f = -jnp.exp(a_log_f.astype(f32)).reshape(shp)
    a_b = -jnp.exp(a_log_b.astype(f32)).reshape(shp)
    y_fwd = ssd_chunked(xs, dt_f, a_f, bm, cm)
    flip = lambda t: jnp.flip(t, axis=1)
    y_bwd = flip(ssd_chunked(flip(xs), flip(dt_b), a_b, flip(bm), flip(cm)))
    y = y_fwd + y_bwd + d_skip.astype(f32).reshape(shp)[..., None] * xs
    y = y.reshape(b, l, SSD_D_INNER).astype(z.dtype)
    return rms_norm(y * jax.nn.silu(z), ssd_norm)

def second_inputs(seed: int = 0) -> dict:
    key = jax.random.key(seed)
    ks = jax.random.split(key, 24)
    L = DEPTH_2
    nrm = lambda k, shape, fan_in: jax.random.normal(k, shape, jnp.float32) * fan_in ** -0.5
    gain = lambda k, shape: 1.0 + 0.05 * jax.random.normal(k, shape, jnp.float32)
    dt0 = jnp.exp(jax.random.uniform(ks[6], (2, L, SSD_HEADS), jnp.float32, math.log(1e-3), math.log(1e-1)))
    dt_bias = dt0 + jnp.log(-jnp.expm1(-dt0))
    a_log = jnp.log(jax.random.uniform(ks[7], (2, L, SSD_HEADS), jnp.float32, 1.0, 16.0))
    return {
        "x": jax.random.normal(ks[0], (BATCH, SEQ, D_MODEL), jnp.float32),
        "w_in": nrm(ks[1], (L, D_MODEL, D_IN_PROJ), D_MODEL),
        "q_norm": gain(ks[2], (L, HEAD_DIM)),
        "k_norm": gain(ks[3], (L, HEAD_DIM)),
        "conv_w": nrm(ks[4], (L, CONV_K, CONV_CH), CONV_K),
        "conv_b": 0.02 * jax.random.normal(ks[5], (L, CONV_CH), jnp.float32),
        "dt_bias_f": dt_bias[0],
        "dt_bias_b": dt_bias[1],
        "a_log_f": a_log[0],
        "a_log_b": a_log[1],
        "d_skip": 1.0 + 0.1 * jax.random.normal(ks[8], (L, SSD_HEADS), jnp.float32),
        "ssd_norm": gain(ks[9], (L, SSD_D_INNER)),
        "w_attn_proj": nrm(ks[10], (L, ATTN_WIDTH, D_MODEL), ATTN_WIDTH),
        "w_ssd_proj": nrm(ks[11], (L, SSD_D_INNER, D_MODEL), SSD_D_INNER),
        "w_out": nrm(ks[12], (L, D_MODEL, D_MODEL), D_MODEL),
        "norm1_pre": gain(ks[13], (L, D_MODEL)),
        "norm1_post": gain(ks[14], (L, D_MODEL)),
        "norm2_pre": gain(ks[15], (L, D_MODEL)),
        "norm2_post": gain(ks[16], (L, D_MODEL)),
        "w_gate_up": nrm(ks[17], (L, D_MODEL, 2 * D_FF_2), D_MODEL),
        "w_down": nrm(ks[18], (L, D_FF_2, D_MODEL), D_FF_2),
    }

def second_block(x, w_in, q_norm, k_norm, conv_w, conv_b, dt_bias_f, dt_bias_b, a_log_f, a_log_b,
              d_skip, ssd_norm, w_attn_proj, w_ssd_proj, w_out, norm1_pre, norm1_post,
              norm2_pre, norm2_post, w_gate_up, w_down):
    b, s, _ = x.shape
    ang_row, ang_col = axial_angles(s)
    for i in range(DEPTH_2):
        h = rms_norm(x, norm1_pre[i])
        proj = h @ w_in[i]
        q, k, v, z, xbc, dt_raw, gates = split_cols(proj, IN_SPLITS)
        q = rms_norm(q.reshape(b, s, N_KV_HEADS, Q_PER_KV, HEAD_DIM), q_norm[i])
        k = rms_norm(k.reshape(b, s, N_KV_HEADS, HEAD_DIM), k_norm[i])
        v = v.reshape(b, s, N_KV_HEADS, HEAD_DIM)
        q = axial_rope(q, ang_row, ang_col)
        k = axial_rope(k, ang_row, ang_col)
        attn_out = gqa_attention(q, k, v) @ w_attn_proj[i]
        ssd_y = ssd_branch(z, xbc, dt_raw, conv_w[i], conv_b[i], dt_bias_f[i], dt_bias_b[i],
                           a_log_f[i], a_log_b[i], d_skip[i], ssd_norm[i])
        ssd_out = ssd_y @ w_ssd_proj[i]
        g_attn, g_ssd = jnp.split(jax.nn.sigmoid(gates), N_BRANCH, axis=-1)
        mixed = (g_attn * attn_out + g_ssd * ssd_out) @ w_out[i]
        x = x + rms_norm(mixed, norm1_post[i])
        h2 = rms_norm(x, norm2_pre[i])
        gate, up = jnp.split(h2 @ w_gate_up[i], 2, axis=-1)
        ffn = (jax.nn.silu(gate) * up) @ w_down[i]
        x = x + rms_norm(ffn, norm2_post[i])
    return x


def setup_inputs(seed=0):
    out = dict(first_inputs(seed))
    for name, value in second_inputs(seed + 1).items():
        if name != "x":
            out[name + "_2"] = value
    return out


def reference(
    x, a_w_in, a_b_f, a_w_out, kv_w, b_w_q, b_lambda, b_subln_g, b_w_out, ffn_w_in, ffn_conv_w,
    ffn_conv_b, ffn_w_out, ln_attn_g, ln_attn_b, ln_ffn_g, ln_ffn_b, w_in_2, q_norm_2, k_norm_2,
    conv_w_2, conv_b_2, dt_bias_f_2, dt_bias_b_2, a_log_f_2, a_log_b_2, d_skip_2, ssd_norm_2,
    w_attn_proj_2, w_ssd_proj_2, w_out_2, norm1_pre_2, norm1_post_2, norm2_pre_2, norm2_post_2,
    w_gate_up_2, w_down_2,
):
    x = first_block(
        x, a_w_in, a_b_f, a_w_out, kv_w, b_w_q, b_lambda, b_subln_g, b_w_out, ffn_w_in,
        ffn_conv_w, ffn_conv_b, ffn_w_out, ln_attn_g, ln_attn_b, ln_ffn_g, ln_ffn_b,
    )
    return second_block(
        x, w_in_2, q_norm_2, k_norm_2, conv_w_2, conv_b_2, dt_bias_f_2, dt_bias_b_2, a_log_f_2,
        a_log_b_2, d_skip_2, ssd_norm_2, w_attn_proj_2, w_ssd_proj_2, w_out_2, norm1_pre_2,
        norm1_post_2, norm2_pre_2, norm2_post_2, w_gate_up_2, w_down_2,
    )


_drawn_inputs = setup_inputs


def setup_inputs(seed=0):
    import zlib

    import numpy as np

    out = dict(_drawn_inputs(seed))
    spreads = {}
    factors = {'b_subln_g': 7.14,
     'ffn_conv_b': 3.825,
     'q_norm_2': 8.0,
     'k_norm_2': 8.0,
     'conv_b_2': 3.475}
    for name, (base, spread) in spreads.items():
        noise = np.random.default_rng([zlib.crc32(name.encode()), seed]).standard_normal(out[name].shape)
        drawn = base * np.exp(spread * noise) if base else spread * noise
        out[name] = __import__('jax').numpy.asarray(drawn.astype(out[name].dtype))
    for name, factor in factors.items():
        out[name] = (out[name] * factor).astype(out[name].dtype)
    return out
```

```python
import math

import numpy as np

import concourse.bass as bass
from concourse import mybir

F32 = mybir.dt.float32
F32R = mybir.dt.float32r
BF16 = mybir.dt.bfloat16
ALU = mybir.AluOpType
ACT = mybir.ActivationFunctionType
AX = mybir.AxisListType.X

S = 512
D = 1024
KT = 8
FF = 22
ALPHA = 4.0 ** 0.25
LAM_INIT = 0.8 - 0.6 * math.exp(-0.3)
NEG = -1.0e30
FIRST = 16640



def rng(a, b):
    return list(range(a, b))


def halves(h):
    return [64 * h + 2 * d + e for e in range(2) for d in range(32)]


def turned(h):
    return [64 * h + x for x in rng(0, 16) + rng(32, 48) + rng(16, 32) + rng(48, 64)]


def unit_table():
    u = {}
    u["f", 0] = [("a_w_in", 0, 8, rng(3072, 3088))]
    for i in range(4):
        u["av", i] = [("a_w_in", 0, 8, rng(2048 + 256 * i, 2304 + 256 * i))]
    for i in range(8):
        u["aqk", i] = [("a_w_in", 0, 8, rng(128 * i, 128 * i + 128) + rng(1024 + 128 * i, 1152 + 128 * i))]
    for i in range(4):
        u["ao", i] = [("a_w_out", 0, 8, rng(256 * i, 256 * i + 256))]
    for lay in ("0", "1"):
        w1, w2 = "ffn_w_in" + lay, "ffn_w_out" + lay
        for j in range(FF):
            u["up" + lay, j] = [(w1, 0, 8, rng(128 * j, 128 * j + 128) + rng(2816 + 128 * j, 2944 + 128 * j))]
        for i in range(4):
            for p, (k0, kt) in enumerate(((0, 8), (8, 7), (15, 7))):
                u["dn" + lay, i, p] = [(w2, k0, kt, rng(256 * i, 256 * i + 256))]
    for i in range(4):
        u["bv", i] = [("kv_w", 0, 8, rng(1024 + 256 * i, 1280 + 256 * i))]
    for h in range(8):
        c = rng(64 * h, 64 * h + 64) + rng(512 + 64 * h, 576 + 64 * h)
        u["bqk", h] = [("b_w_q", 0, 8, c), ("kv_w", 0, 8, c)]
    for i in range(4):
        u["bo", i] = [("b_w_out", 0, 8, rng(256 * i, 256 * i + 256))]
    u["cv", 0] = [("w_in_2", 0, 8, rng(640, 768) + rng(3328, 3360))]
    for i in range(2):
        c = []
        for j in (2 * i, 2 * i + 1):
            c += turned(j) + turned(j + 4)
        u["cq", i] = [("w_in_2", 0, 8, c)]
    u["ck", 0] = [("w_in_2", 0, 8, [512 + x for x in turned(0) + turned(1)])]
    for i in range(6):
        u["cx", i] = [("w_in_2", 0, 8, rng(1792 + 256 * i, 2048 + 256 * i))]
    for i in range(4):
        u["cz", i] = [("w_in_2", 0, 8, rng(768 + 256 * i, 1024 + 256 * i))]
        u["cga", i] = [("w_in_2", 0, 8, rng(3360 + 256 * i, 3616 + 256 * i))]
        u["cgs", i] = [("w_in_2", 0, 8, rng(4384 + 256 * i, 4640 + 256 * i))]
        u["cpa", i] = [("w_attn_proj_2", 0, 4, rng(256 * i, 256 * i + 256))]
        u["cps", i] = [("w_ssd_proj_2", 0, 8, rng(256 * i, 256 * i + 256))]
        u["co", i] = [("w_out_2", 0, 8, rng(256 * i, 256 * i + 256))]
        for p, (k0, kt) in enumerate(((0, 8), (8, 7), (15, 7))):
            u["dn2", i, p] = [("w_down_2", k0, kt, rng(256 * i, 256 * i + 256))]
    for j in range(FF):
        u["up2", j] = [("w_gate_up_2", 0, 8, rng(128 * j, 128 * j + 128) + rng(2816 + 128 * j, 2944 + 128 * j))]
    return u


def unit_places():
    at, out = 0, {}
    for key, parts in unit_table().items():
        kt, n = parts[0][2], sum(len(p[3]) for p in parts)
        out[key] = (at, kt, n)
        at += 128 * kt * n
    return out, at



def small_table():
    names = [("ln_attn_g0", 8), ("ln_attn_b0", 8), ("ln_ffn_g0", 8), ("ln_ffn_b0", 8),
             ("ln_attn_g1", 8), ("ln_attn_b1", 8), ("ln_ffn_g1", 8), ("ln_ffn_b1", 8),
             ("cw00", 44), ("cw01", 44), ("cw02", 44), ("cb0", 44),
             ("cw10", 44), ("cw11", 44), ("cw12", 44), ("cb1", 44),
             ("sw0", 12), ("sw1", 12), ("sw2", 12), ("sw3", 12), ("sw4", 12), ("sb", 12),
             ("n1pre", 8), ("n1post", 8), ("n2pre", 8), ("n2post", 8), ("ssdn", 8),
             ("qn", 1), ("kn", 1), ("bf", 1), ("subln", 1),
             ("lam", 256), ("dtb", 32), ("alog", 32), ("dskip", 16)]
    at, out = 0, {}
    for name, n in names:
        out[name] = (at, n)
        at += n
    return out, at


def const_arrays():
    p = np.arange(128)
    ident = np.eye(128, dtype=np.float32)
    upper = (p[:, None] <= p[None, :]).astype(np.float32)
    lower = (p[:, None] >= p[None, :]).astype(np.float32)
    mean = np.full((128, 128), 1.0 / D, np.float32)
    blk = np.kron(np.eye(2), np.full((64, 64), 1.0 / 64)).astype(np.float32)
    ones = np.ones((128, 512), np.float32)
    causal = np.where(p[None, :] <= p[:, None], 0.0, NEG)
    chunk = np.where(p[None, :] < (p[:, None] // 64 + 1) * 64, 0.0, NEG)
    mf = np.where(p[:, None] <= p[None, :], 0.0, NEG)
    mb = np.where(p[:, None] >= p[None, :], 0.0, NEG)
    inv = (1.0 / (np.float32(10000.0) ** (np.arange(0, 64, 2, dtype=np.float32) / np.float32(64)))).astype(np.float32)
    ang = np.arange(S, dtype=np.float32)[:, None] * inv[None, :]
    inv2 = (np.float32(10000.0) ** (-np.arange(0, 32, 2, dtype=np.float32) / np.float32(32))).astype(np.float32)
    t = np.arange(S)
    ang2 = np.concatenate([(t // 64).astype(np.float32)[:, None] * inv2, (t % 64).astype(np.float32)[:, None] * inv2], 1)
    tabs = []
    for a in (ang, ang2):
        c, s = np.cos(a).astype(np.float32).T, np.sin(a).astype(np.float32).T
        tabs += [np.concatenate([c] * 4, 0), np.concatenate([-s, s, -s, s], 0)]
    fp = np.concatenate([ident, upper, lower, mean, blk, ones] + tabs, 1).astype(np.float32)
    masks = np.concatenate([np.eye(128), causal, chunk] + [mf] * 4 + [mb] * 4, 1).astype(np.float32)
    return fp, masks


class Queue:

    def __init__(self, sem, chained, eng):
        self.sem, self.n, self.chained, self.eng, self.seen = sem, 0, chained, eng, {}

    def op(self, fn, *after, inc=True, chain=True):
        if self.eng is not None:
            waits = list(flat(after))
            if self.chained and chain and self.n:
                waits.append((self.sem, self.n))
            need = {}
            for sem, v in waits:
                if v > self.seen.get(sem.name, 0) and v > need.get(sem.name, (None, 0))[1]:
                    need[sem.name] = (sem, v)
            for name, (sem, v) in need.items():
                self.eng.wait_ge(sem, v)
                self.seen[name] = v
            ins = fn(self.eng)
            if inc:
                ins.then_inc(self.sem, 1)
        if inc:
            self.n += 1
        return (self.sem, self.n)

    def last(self):
        return (self.sem, self.n) if self.n else None


def flat(x):
    for y in x:
        if y is None:
            continue
        if isinstance(y, list) or (isinstance(y, tuple) and y and (y[0] is None or isinstance(y[0], (list, tuple)))):
            yield from flat(y)
        elif isinstance(y, tuple) and len(y) == 2:
            yield y


def program(nc, xT, wall, small, cfp, cmask, outT, order, mem, turn, engine):
    places, _ = unit_places()
    sm, nsm = small_table()
    used = []
    sizes = {}
    if True:
        def sem(name):
            if name not in mem:
                mem[name] = nc.alloc_semaphore(name=name)
            return mem[name]

        s_pe, s_act, s_dve, s_pool = sem("s_pe"), sem("s_act"), sem("s_dve"), sem("s_pool")
        s_raw = [sem("s_raw0"), sem("s_raw1")]
        s_in = sem("s_in")
        s_x = sem("s_x")
        s_out = sem("s_out")
        PE, AC, DV, PO, SP = (Queue(q, c, engine if turn == n else None) for q, c, n in (
            (s_pe, False, "pe"), (s_act, True, "act"), (s_dve, True, "dve"), (s_pool, True, "pool"), (None, False, "sp")))

        def sp(fn, *after):
            SP.op(fn, *after, inc=False)

        def at(name, n, dt, off, parts=128):
            if name not in mem:
                mem[name] = nc.alloc_sbuf_tensor_at(name, [parts, n], dt, offset=FIRST + off)
            return mem[name]

        K = 1024
        base = 0
        FP = at("FP", 3200, F32, base)
        MK = at("MK", 1408, BF16, base + 12800)
        MKF = at("MKF", 1408, F32, 100 * K)
        SM = at("SM", nsm, F32, base + 15616)
        base = 15616 + nsm * 4
        base = (base + 63) // 64 * 64
        TN = at("TN", 128, F32, base)
        base += 512
        LAMT = at("LAMT", 64, F32, base)
        base += 256
        NEGC = at("NEGC", 64, F32, base)
        base += 256
        RAW = [at(f"RAW{i}", 2048, F32, base + 8 * K * i) for i in range(2)]
        base += 16 * K
        HI = [at(f"HI{i}", 2048, F32R, base + 8 * K * i) for i in range(2)]
        base += 16 * K
        LO = [at(f"LO{i}", 2048, F32R, base + 8 * K * i) for i in range(2)]
        base += 16 * K
        XH = at("XH", 4096, F32R, base)
        YH = at("YH", 4096, F32, base)
        base += 16 * K
        XL = at("XL", 4096, F32R, base)
        YL = at("YL", 4096, F32, base)
        base += 16 * K
        R0 = base
        sizes["free"] = R0
        if "PS" not in mem:
            mem["PS"] = [nc.alloc_psum_tensor(f"PS{i}", [128, 512], F32) for i in range(8)]
        PS = mem["PS"]

        IDN, UPP, LOW, MEAN, BLK, ONE = (FP[:, 128 * i:128 * i + 128] for i in range(6))
        ONE512 = FP[:, 640:1152]
        COSA, SINA, COSB, SINB = (FP[:, 1152 + 512 * i:1664 + 512 * i] for i in range(4))
        IDB, CAUS, CHNK = (MK[:, 128 * i:128 * i + 128] for i in range(3))
        MF, MB = MK[:, 384:896], MK[:, 896:1408]

        def col(name, j=0, n=1):
            a = sm[name][0]
            return SM[:, a + j:a + j + n]

        def blk(t, j, w=512):
            return t[:, w * j:w * j + w]

        free = [None] * 8

        def marks():
            return [PE.last(), AC.last(), DV.last(), PO.last()]

        sp(lambda e: e.dma_start(FP[:, :], cfp).then_inc(s_in, 16))
        sp(lambda e: e.dma_start(MKF[:, :], cmask).then_inc(s_in, 16))
        sp(lambda e: e.dma_start(SM[:, :], small).then_inc(s_in, 16))
        XF = at("XF", 4096, F32, 120 * K)
        sp(lambda e: e.dma_start(XF[:, :], xT).then_inc(s_x, 16))
        INP, XIN = (s_in, 48), (s_x, 16)
        DV.op(lambda e: e.tensor_copy(MK[:, :], MKF[:, :]), INP)
        DV.op(lambda e: e.memset(NEGC[:, 0:1], 1e-5))
        DV.op(lambda e: e.memset(NEGC[:, 1:2], 1e-6))
        CONST = DV.op(lambda e: e.memset(NEGC[:, 2:3], 1.0))
        EPS5, EPS6 = NEGC[:, 0:1], NEGC[:, 1:2]

        raw_free = [None, None]
        part_free = [None, None]
        made = []

        def load_raw(i):
            key = order[i]
            off, kt, n = places[key]
            r = RAW[i % 2]
            src = wall[off:off + 128 * kt * n].rearrange("(p n) -> p n", p=128)
            sp(lambda e: e.dma_start(r[:, 0:kt * n], src).then_inc(s_raw[i % 2], 16), raw_free[i % 2])

        def split_unit(i):
            off, kt, n = places[order[i]]
            w, s = kt * n, i % 2
            landed = (s_raw[s], 16 * (i // 2 + 1))
            r, h, l = RAW[s][:, 0:w], HI[s][:, 0:w], LO[s][:, 0:w]
            a = AC.op(lambda e: e.activation(h, r, ACT.Copy), landed, part_free[s], chain=False)
            d = DV.op(lambda e: e.tensor_tensor(l, r, h.bitcast(F32), ALU.subtract), a, part_free[s], chain=False)
            raw_free[s] = [a, d]
            made.append(d)
            if i + 2 < len(order):
                load_raw(i + 2)

        def take(key):
            i = len(used)
            used.append(key)
            off, kt, n = places[key]
            if order is None:
                return HI[0], LO[0], kt, n, None, lambda t: None
            assert order[i] == key
            if i == 0:
                load_raw(0)
                load_raw(1)
                split_unit(0)
            if i + 1 < len(order):
                split_unit(i + 1)

            def release(t):
                part_free[i % 2] = t
            return HI[i % 2], LO[i % 2], kt, n, made[i], release

        def mm(out, a, b, start, stop, *after, inc=False):
            return PE.op(lambda e: e.matmul(out, a, b, start=start, stop=stop), *after, inc=inc)

        def tr(out, src, ident, *after, inc=False):
            return PE.op(lambda e: e.transpose(out, src, ident), *after, inc=inc)

        lin_bank = [0]

        def pick(n=4):
            b = lin_bank[0] % n
            lin_bank[0] += 1
            return b

        def lin_fm(keys, xh, xl, xt, widths=(128, 128), k0=0):
            banks = [pick() for _ in widths]
            total = sum(places[k][1] for k in keys)
            kk, toks = 0, [None] * len(widths)
            for key in keys:
                hi, lo, kt, n, ready, release = take(key)
                for k in range(kt):
                    c = 0
                    for j, (b, w) in enumerate(zip(banks, widths)):
                        wh = hi[:, k * n + c:k * n + c + w]
                        wl = lo[:, k * n + c:k * n + c + w]
                        o = PS[b][0:w, :]
                        first, last = kk == 0, kk == total - 1
                        aft = (ready, xt(kk), free[b] if first else None)
                        mm(o, wh, xh(kk), first, False, *aft)
                        mm(o, wh, xl(kk), False, False)
                        toks[j] = mm(o, wl, xh(kk), False, last, inc=True)
                        c += w
                    kk += 1
                release(toks[-1])
            return list(zip(banks, toks))

        def lin_tm(key, xh, xl, xt, evac):
            hi, lo, kt, n, ready, release = take(key)
            for c in range(4):
                b = pick()
                o = PS[b][:, 0:n]
                t = slice(128 * c, 128 * c + 128)
                for k in range(kt):
                    wh, wl = hi[:, k * n:k * n + n], lo[:, k * n:k * n + n]
                    mm(o, xh(k)[:, t], wh, k == 0, False, ready, xt(k), free[b])
                    mm(o, xl(k)[:, t], wh, False, False)
                    tok = mm(o, xh(k)[:, t], wl, False, k == kt - 1, inc=(k == kt - 1))
                if c == 3:
                    release(tok)
                free[b] = evac(c, PS[b], tok)

        def split(src, h, l, *after):
            a = AC.op(lambda e: e.activation(h, src, ACT.Copy), *after)
            d = DV.op(lambda e: e.tensor_tensor(l, src, h.bitcast(F32), ALU.subtract), a)
            return d

        def norm_bufs(off):
            return {n: at(f"{n}_{off}_{len(used)}", 512, F32, off + 2048 * i)
                    for i, n in enumerate(("SQ", "A1", "A2", "MS", "RS", "T1", "T2"))}

        def acc_step(nb, j, y, tok, mean, squares=True):
            sq, a1, a2 = nb["SQ"][:, :], nb["A1"][:, :], nb["A2"][:, :]
            prev = nb.get("tok")
            t = []
            if mean:
                if j == 0:
                    t.append(PO.op(lambda e: e.tensor_copy(a1, y), tok, prev))
                else:
                    t.append(PO.op(lambda e: e.tensor_tensor(a1, a1, y, ALU.add), tok))
            if j == 0:
                t.append(AC.op(lambda e: e.activation(a2, y, ACT.Square), tok, prev))
            else:
                s = AC.op(lambda e: e.activation(sq, y, ACT.Square), tok, nb.get("sqfree"))
                u = PO.op(lambda e: e.tensor_tensor(a2, a2, sq, ALU.add), s, nb["t"])
                nb["sqfree"] = u
                t.append(u)
            nb["t"] = t
            return t

        def stats(nb, eps, mean):
            b1, b2 = 5, 6
            rs, ms = nb["RS"][:, :], nb["MS"][:, :]
            if mean:
                t1 = mm(PS[b1][:, :], MEAN, nb["A1"][:, :], True, True, nb["t"], free[b1], CONST, inc=True)
            t2 = mm(PS[b2][:, :], MEAN, nb["A2"][:, :], True, True, nb["t"], free[b2], CONST, inc=True)
            if mean:
                a = AC.op(lambda e: e.activation(ms, PS[b1][:, :], ACT.Square), t1)
                d = DV.op(lambda e: e.tensor_tensor(ms, PS[b2][:, :], ms, ALU.subtract), t2, a)
                a = AC.op(lambda e: e.activation(rs, ms, ACT.Sqrt, bias=eps), d)
            else:
                a = AC.op(lambda e: e.activation(rs, PS[b2][:, :], ACT.Sqrt, bias=eps), t2)
                d = a
            free[b2] = d
            r = DV.op(lambda e: e.reciprocal(rs, rs), a)
            nb["tok"] = [t2]
            return r

        xtok = [None] * 8

        def residual_tile(j, bank, tok):
            y, yl = blk(YH, j), blk(YL, j)
            d = DV.op(lambda e: e.scalar_tensor_tensor(out=yl, in0=blk(XL, j).bitcast(F32), scalar=ALPHA, in1=PS[bank][:, :],
                                                       op0=ALU.mult, op1=ALU.add), tok)
            free[bank] = d
            return DV.op(lambda e: e.scalar_tensor_tensor(out=y, in0=blk(XH, j).bitcast(F32), scalar=ALPHA, in1=yl,
                                                          op0=ALU.mult, op1=ALU.add))

        def layer_norm(nb, g, b, final=None, post=None):
            r = stats(nb, EPS5, True)
            t1 = [nb["T1"][:, :], nb["T2"][:, :]]
            tfree = [None, None]
            for j in range(8):
                y, t = blk(YH, j), t1[j % 2]
                d = DV.op(lambda e: e.tensor_tensor(t, PS[5][:, :], y, ALU.subtract), r, tfree[j % 2], marks() if j == 0 else None)
                free[5] = d
                d = DV.op(lambda e: e.tensor_tensor(t, t, nb["RS"][:, :], ALU.mult))
                x = final(j) if final else t
                a = AC.op(lambda e: e.activation(x, t, ACT.Identity, bias=col(b, j), scale=NG[g][:, j:j + 1]), d)
                if post:
                    tfree[j % 2] = [a]
                    post(j, a)
                else:
                    tfree[j % 2] = xtok[j] = split(x, blk(XH, j), blk(XL, j), a)

        NGT = at("NGT", 32, F32, base - 96 * K + 0) if False else None
        NG = {}
        for i, g in enumerate(("ln_attn_g0", "ln_ffn_g0", "ln_attn_g1", "ln_ffn_g1")):
            o = TN[:, 8 * i:8 * i + 8]
            NG[g] = o
            DV.op(lambda e, o=o, g=g: e.tensor_scalar(o, col(g, 0, 8), -1.0, None, ALU.mult), INP)
        XHk, XLk, XTk = (lambda k: blk(XH, k)), (lambda k: blk(XL, k)), (lambda k: xtok[k])

        for j in range(8):
            xtok[j] = split(blk(XF, j), blk(XH, j), blk(XL, j), XIN)

        def fox():
            o = R0
            V = at("aV", 4096, F32, o); o += 16 * K
            OT = at("aO", 4096, F32, o); o += 16 * K
            QK = at("aQK", 2048, F32, o); o += 8 * K
            L = at("aL", 1024, F32, o); o += 4 * K
            P = at("aP", 1024, F32, o); o += 4 * K
            PT = at("aPT", 1024, F32, o); o += 4 * K
            NB = at("aNB", 1024, F32, o); o += 4 * K
            OH = at("aOH", 4096, F32R, o); o += 16 * K
            OL = at("aOL", 4096, F32R, o); o += 16 * K
            FZ = at("aFZ", 2560, F32, o, 16); o += 10 * K
            MX = at("aMX", 64, F32, o); o += 256
            NM = at("aNM", 64, F32, o); o += 256
            SU = at("aSU", 64, F32, o); o += 256
            RC = at("aRC", 64, F32, o); o += 256
            start = marks()
            (fb, ft), = lin_fm([("f", 0)], XHk, XLk, XTk, widths=(16,))
            z, e1, l1, c1, n1 = (FZ[:, 512 * i:512 * i + 512] for i in range(5))
            d = DV.op(lambda e: e.tensor_scalar(z, PS[fb][0:16, :], col("bf")[0:16, :], None, ALU.add), ft, start)
            free[fb] = d
            a = AC.op(lambda e: e.activation(e1, z, ACT.Abs), d)
            a = AC.op(lambda e: e.activation(e1, e1, ACT.Exp, scale=-1.0), a)
            a = AC.op(lambda e: e.activation(l1, e1, ACT.Ln, bias=1.0), a)
            d = DV.op(lambda e: e.tensor_scalar(z, z, 0.0, None, ALU.min), a)
            d = DV.op(lambda e: e.tensor_tensor(z, z, l1, ALU.subtract))
            d = DV.op(lambda e: e.tensor_tensor_scan(c1, ONE512[0:16, :], z, 0.0, ALU.mult, ALU.add))
            ncd = DV.op(lambda e: e.tensor_scalar(n1, c1, -8.0, None, ALU.mult))

            vtok = [None] * 4
            def vunit(i):
                def evac(c, ps, tok):
                    dst = V[:, 1024 * c + 256 * i:1024 * c + 256 * i + 256]
                    vtok[i] = AC.op(lambda e: e.activation(dst, ps[:, 0:256], ACT.Copy), tok)
                    return vtok[i]
                lin_tm(("av", i), XHk, XLk, XTk, evac)

            qkfree = [None, None]
            qktok = [None, None]
            def qkunit(hp):
                r = lin_fm([("aqk", hp)], XHk, XLk, XTk)
                s = hp % 2
                (b0, t0), (b1, t1) = r
                q, k = QK[:, 1024 * s:1024 * s + 512], QK[:, 1024 * s + 512:1024 * s + 1024]
                a = AC.op(lambda e: e.activation(q, PS[b0][:, :], ACT.Copy), t0, qkfree[s])
                d = DV.op(lambda e: e.tensor_copy(k, PS[b1][:, :]), t1, qkfree[s])
                free[b0], free[b1] = a, d
                qktok[s] = [a, d]

            nbfree = [None, None]
            ptfree = [None, None]
            pfree = [None, None]
            cnt = [0]
            otok = {}

            def head(h):
                s, rows = (h // 2) % 2, slice(64 * (h % 2), 64 * (h % 2) + 64)
                q, k = QK[rows, 1024 * s:1024 * s + 512], QK[rows, 1024 * s + 512:1024 * s + 1024]
                nb = blk(NB, h % 2)
                t = mm(PS[7][:, :], IDN[0:16, h:h + 1].to_broadcast([16, 128]), n1, True, True, free[7], ncd, inc=True)
                nbt = AC.op(lambda e: e.activation(nb, PS[7][:, :], ACT.Copy), t, nbfree[h % 2])
                free[7] = nbt
                yield

                def scores(i):
                    bank, kl = 4 + i % 2, 128 * (i + 1)
                    mm(PS[bank][:, 0:kl], q[:, 128 * i:128 * i + 128], k[:, 0:kl], True, False, free[bank], qktok[s])
                    return mm(PS[bank][:, 128 * i:kl], IDB, CAUS, False, True, CONST, inc=True)
                st = {0: scores(0), 1: scores(1)}
                for i in range(4):
                    u, kl, g = cnt[0] % 2, 128 * (i + 1), 4 * h + i
                    cnt[0] += 1
                    bank = 4 + i % 2
                    l, p, pt = blk(L, u)[:, 0:kl], blk(P, u), blk(PT, u)
                    mx, nm, su = MX[:, g:g + 1], NM[:, g:g + 1], SU[:, g:g + 1]
                    d = DV.op(lambda e, bank=bank, l=l, mx=mx, kl=kl: e.tensor_tensor_reduce(
                        l, PS[bank][:, 0:kl], nb[:, 0:kl], 0.125, -3.0e38, ALU.add, ALU.max, mx), st[i], nbt, pfree[u], start)
                    free[bank] = d
                    if i + 2 < 4:
                        st[i + 2] = scores(i + 2)
                    d = DV.op(lambda e, nm=nm, mx=mx: e.tensor_scalar(nm, mx, -1.0, None, ALU.mult))
                    a = AC.op(lambda e, p=p, l=l, nm=nm, su=su, kl=kl: e.activation(
                        p[:, 0:kl], l, ACT.Exp, bias=nm, accum_out=su), d, pfree[u])
                    nbfree[h % 2] = d
                    yield
                    for kb in range(i + 1):
                        t = tr(PS[6][:, 128 * kb:128 * kb + 128], p[:, 128 * kb:128 * kb + 128], IDN,
                               a, free[6], inc=(kb == i))
                    pfree[u] = [t, a]
                    if i % 2:
                        c = AC.op(lambda e, pt=pt, kl=kl: e.activation(pt[:, 0:kl], PS[6][:, 0:kl], ACT.Copy), t, ptfree[u])
                    else:
                        c = DV.op(lambda e, pt=pt, kl=kl: e.tensor_copy(pt[:, 0:kl], PS[6][:, 0:kl]), t, ptfree[u])
                    free[6] = c
                    yield
                    for kb in range(i + 1):
                        t = mm(PS[7][:, 64 * i:64 * i + 64], pt[:, 128 * kb:128 * kb + 128],
                               V[:, 1024 * kb + 64 * h:1024 * kb + 64 * h + 64], kb == 0, kb == i,
                               c, free[7], vtok[h // 4], inc=(kb == i))
                    ptfree[u] = t
                qkfree[s] = t
                rc = RC[:, 4 * h:4 * h + 4]
                d = DV.op(lambda e: e.reciprocal(rc, SU[:, 4 * h:4 * h + 4]), a)
                dst = OT[:, :].rearrange("p (c n) -> p c n", c=4)[:, :, 64 * h:64 * h + 64]
                d = DV.op(lambda e: e.tensor_tensor(dst, PS[7][:, 0:256].rearrange("p (c n) -> p c n", c=4),
                                                    rc.unsqueeze(2).to_broadcast([128, 4, 64]), ALU.mult), t)
                free[7] = d
                otok[h] = d
                yield

            ohtok = [None] * 8

            def turn(j):
                for c in range(4):
                    t = tr(PS[6][:, 128 * c:128 * c + 128], OT[:, 1024 * c + 128 * j:1024 * c + 128 * j + 128], IDN,
                           free[6], otok[2 * j + 1], inc=(c == 3))
                ohtok[j] = split(PS[6][:, :], blk(OH, j), blk(OL, j), t)
                free[6] = ohtok[j]

            def heads():
                for h in range(16):
                    yield from head(h)
                    if h % 2:
                        turn(h // 2)

            vunit(0)
            qkunit(0)
            gen = heads()
            plan = [("q", 1), ("v", 1), ("q", 2), ("q", 3), ("v", 2), ("q", 4), ("q", 5), ("v", 3), ("q", 6), ("q", 7)]
            steps_done = 0
            per_head = 10
            for kind, i in plan:
                if kind == "q":
                    while steps_done < per_head * 2 * (i - 1):
                        next(gen)
                        steps_done += 1
                    qkunit(i)
                else:
                    vunit(i)
            for _ in gen:
                pass
            return (lambda k: blk(OH, k)), (lambda k: blk(OL, k)), (lambda k: ohtok[k]), o

        def attn_out(name, oh, ol, ot, g, b):
            nb = norm_bufs(R0)
            for i in range(4):
                for j, (bank, tok) in enumerate(lin_fm([(name, i)], oh, ol, ot)):
                    d = residual_tile(2 * i + j, bank, [tok, marks()] if i == 0 and j == 0 else tok)
                    acc_step(nb, 2 * i + j, blk(YH, 2 * i + j), d, True)
            layer_norm(nb, g, b)

        def ffn_up(names, conv, hh, hl, tmp, act_fn):
            htok = [None] * FF
            tfree = [None] * 2
            start = marks()
            for j in range(FF):
                (bg, tg), (bv, tv) = lin_fm([(names, j)], XHk, XLk, XTk)
                u = j % 2
                g, v = tmp[:, 1024 * u:1024 * u + 512], tmp[:, 1024 * u + 512:1024 * u + 1024]
                if conv is None:
                    a = AC.op(lambda e: e.activation(g, PS[bg][:, :], ACT.Silu), tg, tfree[u], start)
                    free[bg] = a
                    d = DV.op(lambda e: e.tensor_tensor(g, g, PS[bv][:, :], ALU.mult), a, tv)
                    free[bv] = d
                else:
                    for x, bank, tok, f in ((g, bg, tg, j), (v, bv, tv, FF + j)):
                        w = [col(f"cw{conv}{t}", f) for t in range(3)]
                        a = AC.op(lambda e, x=x, w=w, bank=bank, f=f: e.activation(
                            x, PS[bank][:, :], ACT.Identity, bias=col(f"cb{conv}", f), scale=w[2]), tok, tfree[u], start)
                        for t in (1, 2):
                            d = DV.op(lambda e, x=x, w=w, bank=bank, t=t: e.scalar_tensor_tensor(
                                out=x[:, t:512], in0=PS[bank][:, 0:512 - t], scalar=w[2 - t], in1=x[:, t:512],
                                op0=ALU.mult, op1=ALU.add), a)
                        free[bank] = d
                    a = AC.op(lambda e: e.activation(g, g, ACT.Silu), d)
                    d = PO.op(lambda e: e.tensor_tensor(g, g, v, ALU.mult), a, d)
                htok[j] = split(g, blk(hh, j), blk(hl, j), d)
                tfree[u] = htok[j]
            return htok

        def ffn_down(name, hh, hl, htok, evac):
            for i in range(4):
                r = lin_fm([(name, i, p) for p in range(3)], lambda k: blk(hh, k), lambda k: blk(hl, k), lambda k: htok[k])
                for j, (bank, tok) in enumerate(r):
                    evac(2 * i + j, bank, tok)

        def ffn_layer(lay, g, b):
            hh = at(f"HH{lay}", 512 * FF, F32R, R0)
            hl = at(f"HL{lay}", 512 * FF, F32R, R0 + 44 * K)
            tmp = at(f"UT{lay}", 2048, F32, R0 + 88 * K)
            nb = norm_bufs(R0 + 88 * K)
            htok = ffn_up("up" + lay, int(lay), hh, hl, tmp, None)
            st = marks()
            nb["tok"] = st

            def evac(j, bank, tok):
                d = residual_tile(j, bank, [tok, st])
                acc_step(nb, j, blk(YH, j), d, True)
            ffn_down("dn" + lay, hh, hl, htok, evac)
            return nb

        def rotate(src, dst, rot, t1, cos, sin, tok, dfree, tfree, psum_bank=None):
            for a_, b_ in ((0, 32), (32, 0), (64, 96), (96, 64)):
                a = AC.op(lambda e, a_=a_, b_=b_: e.activation(rot[a_:a_ + 32, :], src[b_:b_ + 32, :], ACT.Copy), tok, tfree)
            d = DV.op(lambda e: e.tensor_tensor(t1, src, cos, ALU.mult), a, tfree)
            if psum_bank is not None:
                free[psum_bank] = d
            p = PO.op(lambda e: e.tensor_tensor(rot, rot, sin, ALU.mult), a)
            return PO.op(lambda e: e.tensor_tensor(dst, t1, rot, ALU.add), d, dfree)

        def diff():
            o = R0
            V = at("bV", 4096, F32, o); o += 16 * K
            OB = at("bO", 4096, F32, o); o += 16 * K
            QK = at("bQK", 2048, F32, o); o += 8 * K
            ROT = at("bROT", 2048, F32, o); o += 8 * K
            P = at("bP", 2048, F32, o); o += 8 * K
            PT = at("bPT", 1024, F32, o); o += 4 * K
            OH = at("bOH", 4096, F32R, o); o += 16 * K
            OL = at("bOL", 4096, F32R, o); o += 16 * K
            TT = at("bTT", 512, F32, o); o += 2 * K
            ST = at("bST", 512, F32, o); o += 2 * K
            start = marks()
            MX, NM, SU, RC = (ST[:, 64 * i:64 * i + 64] for i in range(4))
            MS = ST[:, 256:288]
            lt, lm = TN[:, 64:128], LAMT
            for i in range(2):
                DV.op(lambda e, i=i: e.tensor_tensor(lt, col("lam", 128 * i, 64), col("lam", 128 * i + 64, 64), ALU.mult))
                d = DV.op(lambda e, i=i: e.tensor_reduce(lm[:, i:i + 1], lt, AX, ALU.add))
            a = AC.op(lambda e: e.activation(lm[:, 2:4], lm[:, 0:2], ACT.Exp), d)
            d = DV.op(lambda e: e.tensor_tensor(lm[:, 4:5], lm[:, 2:3], lm[:, 3:4], ALU.subtract), a)
            d = DV.op(lambda e: e.tensor_scalar(lm[:, 5:6], lm[:, 4:5], LAM_INIT, None, ALU.add))
            gs = lm[:, 8:9]
            DV.op(lambda e: e.tensor_scalar(gs, col("subln"), 1.0 - LAM_INIT, None, ALU.mult))

            vtok = [None] * 4
            def vunit(i):
                def evac(c, ps, tok):
                    dst = V[:, 1024 * c + 256 * i:1024 * c + 256 * i + 256]
                    vtok[i] = AC.op(lambda e: e.activation(dst, ps[:, 0:256], ACT.Copy), tok, start)
                    return vtok[i]
                lin_tm(("bv", i), XHk, XLk, XTk, evac)

            qkfree, qktok, rfree = [None, None], [None, None], [None, None]
            def qkunit(h):
                s = h % 2
                r = lin_fm([("bqk", h)], XHk, XLk, XTk)
                toks = []
                for x, (bank, tok) in enumerate(r):
                    dst = QK[:, 1024 * s + 512 * x:1024 * s + 512 * x + 512]
                    rot, t1 = ROT[:, 1024 * x:1024 * x + 512], ROT[:, 1024 * x + 512:1024 * x + 1024]
                    p = rotate(PS[bank][:, :], dst, rot, t1, COSA, SINA, [tok, start], qkfree[s], rfree[x], bank)
                    rfree[x] = p
                    toks.append(p)
                qktok[s] = toks

            ptfree = [None, None]
            pfree = [None, None]
            cnt = [0]
            otok = [None] * 8

            def head(h):
                s = h % 2
                for i in range(4):
                    kl = 128 * (i + 1)
                    st = []
                    for m in range(2):
                        rows = slice(64 * m, 64 * m + 64)
                        q = QK[rows, 1024 * s + 128 * i:1024 * s + 128 * i + 128]
                        k = QK[rows, 1024 * s + 512:1024 * s + 512 + kl]
                        mm(PS[4 + m][:, 0:kl], q, k, True, False, free[4 + m], qktok[s])
                        st.append(mm(PS[4 + m][:, 128 * i:kl], IDB, CHNK, False, True, CONST, inc=True))
                    u = cnt[0] % 2
                    cnt[0] += 1
                    c0 = 8 * h + 2 * i
                    p1, p2, pt = P[:, 1024 * u:1024 * u + kl], P[:, 1024 * u + 512:1024 * u + 512 + kl], blk(PT, u)
                    for m in range(2):
                        DV.op(lambda e, m=m: e.tensor_reduce(MX[:, c0 + m:c0 + m + 1], PS[4 + m][:, 0:kl], AX, ALU.max), st[m], start)
                    d = DV.op(lambda e: e.tensor_scalar(NM[:, c0:c0 + 2], MX[:, c0:c0 + 2], -0.125, None, ALU.mult))
                    for m, p in enumerate((p1, p2)):
                        a = AC.op(lambda e, m=m, p=p: e.activation(
                            p, PS[4 + m][:, 0:kl], ACT.Exp, bias=NM[:, c0 + m:c0 + m + 1], scale=0.125,
                            accum_out=SU[:, c0 + m:c0 + m + 1]), d, pfree[u])
                        free[4 + m] = a
                    yield
                    DV.op(lambda e: e.reciprocal(RC[:, c0:c0 + 2], SU[:, c0:c0 + 2]), a)
                    DV.op(lambda e: e.tensor_tensor(RC[:, c0 + 1:c0 + 2], RC[:, c0 + 1:c0 + 2], LAMT[:, 5:6], ALU.mult))
                    DV.op(lambda e: e.tensor_scalar(p2, p2, RC[:, c0 + 1:c0 + 2], None, ALU.mult))
                    d = DV.op(lambda e: e.scalar_tensor_tensor(out=p1, in0=p1, scalar=RC[:, c0:c0 + 1], in1=p2,
                                                               op0=ALU.mult, op1=ALU.subtract))
                    for kb in range(i + 1):
                        t = tr(PS[6][:, 128 * kb:128 * kb + 128], P[:, 1024 * u + 128 * kb:1024 * u + 128 * kb + 128], IDN,
                               d, free[6], inc=(kb == i))
                    pfree[u] = [t]
                    if i % 2:
                        c = AC.op(lambda e: e.activation(pt[:, 0:kl], PS[6][:, 0:kl], ACT.Copy), t, ptfree[u])
                    else:
                        c = DV.op(lambda e: e.tensor_copy(pt[:, 0:kl], PS[6][:, 0:kl]), t, ptfree[u])
                    free[6] = c
                    yield
                    for kb in range(i + 1):
                        t = mm(PS[7][:, 128 * i:128 * i + 128], pt[:, 128 * kb:128 * kb + 128],
                               V[:, 1024 * kb + 128 * h:1024 * kb + 128 * h + 128], kb == 0, kb == i,
                               c, free[7], vtok[h // 2], inc=(kb == i))
                    ptfree[u] = t
                qkfree[s] = t
                ob = OB[:, :].rearrange("p (c n) -> p c n", c=4)[:, :, 128 * h:128 * h + 128]
                a = AC.op(lambda e: e.activation(ob, PS[7][:, :].rearrange("p (c n) -> p c n", c=4), ACT.Copy), t, start)
                free[7] = a
                tt = TT[:, :].rearrange("p (c n) -> p c n", c=4)
                d = DV.op(lambda e: e.tensor_tensor(tt, ob, ob, ALU.mult), a)
                otok[h] = DV.op(lambda e: e.tensor_reduce(MS[:, 4 * h:4 * h + 4], tt, AX, ALU.add))
                yield

            ohtok = [None] * 8

            def turns(h0, h1):
                ms = MS[:, 4 * h0:4 * h1]
                a = AC.op(lambda e: e.activation(ms, ms, ACT.Sqrt, bias=EPS5, scale=1.0 / 128), otok[h1 - 1])
                d = DV.op(lambda e: e.reciprocal(ms, ms), a)
                for h in range(h0, h1):
                    for c in range(4):
                        x = OB[:, 1024 * c + 128 * h:1024 * c + 128 * h + 128]
                        d = DV.op(lambda e, x=x, c=c, h=h: e.tensor_scalar(x, x, MS[:, 4 * h + c:4 * h + c + 1], None, ALU.mult))
                    for c in range(4):
                        t = tr(PS[6][:, 128 * c:128 * c + 128], OB[:, 1024 * c + 128 * h:1024 * c + 128 * h + 128], IDN,
                               free[6], d, inc=(c == 3))
                    f = DV.op(lambda e: e.tensor_scalar(TT[:, :], PS[6][:, :], gs, None, ALU.mult), t, ohtok[h - 1] if h else None)
                    free[6] = f
                    ohtok[h] = split(TT[:, :], blk(OH, h), blk(OL, h), f)

            def heads():
                for h in range(8):
                    yield from head(h)
                    if h == 3:
                        turns(0, 4)
                turns(4, 8)

            vunit(0)
            qkunit(0)
            gen = heads()
            done = 0
            for kind, i in [("q", 1), ("q", 2), ("v", 1), ("q", 3), ("q", 4), ("v", 2), ("q", 5), ("q", 6), ("v", 3), ("q", 7)]:
                if kind == "q":
                    while done < 9 * (i - 1):
                        next(gen)
                        done += 1
                    qkunit(i)
                else:
                    vunit(i)
            for _ in gen:
                pass
            return (lambda k: blk(OH, k)), (lambda k: blk(OL, k)), (lambda k: ohtok[k]), o

        def rms_apply(nb, src, tok, gain):
            r = stats(nb, EPS6, False)
            ts = [nb["T1"][:, :], nb["T2"][:, :]]
            tfree = [None, None]
            for j in range(8):
                t = ts[j % 2]
                d = DV.op(lambda e: e.scalar_tensor_tensor(out=t, in0=blk(src, j), scalar=col(gain, j), in1=nb["RS"][:, :],
                                                           op0=ALU.mult, op1=ALU.mult), r, tfree[j % 2], marks() if j == 0 else None)
                tfree[j % 2] = xtok[j] = split(t, blk(XH, j), blk(XL, j), d)

        def second(XR, nb0):
            O0 = R0 + 16 * K
            rms_apply(nb0, XR, None, "n1pre")
            o = O0
            OTH = at("cOTH", 2048, F32R, o); o += 8 * K
            OTL = at("cOTL", 2048, F32R, o); o += 8 * K
            DT = at("cDT", 128, F32, o); o += 512
            ADT = at("cADT", 128, F32, o); o += 512
            ACS = at("cACS", 128, F32, o); o += 512
            NAC = at("cNAC", 128, F32, o); o += 512
            EAC = at("cEAC", 128, F32, o); o += 512
            TOT = at("cTOT", 128, F32, o); o += 512
            DSD = at("cDSD", 128, F32, o); o += 512
            CD = at("cCD", 128, F32, o); o += 512
            EA = at("cEA", 32, F32, o); o += 128
            SS = at("cSS", 32, F32, o); o += 128
            E0 = o
            QQ = at("cQ", 2560, F32, o); o += 10 * K
            V = at("cV", 512, F32, o); o += 2 * K
            OT = at("cO", 2048, F32, o); o += 8 * K
            P = at("cP", 1024, F32, o); o += 4 * K
            PT = at("cPT", 1024, F32, o); o += 4 * K
            ROT = at("cROT", 2560, F32, o); o += 10 * K
            ST = at("cST", 128, F32, o); o += 512
            start = marks()
            MX, NM, SU, RC = (ST[:, 32 * i:32 * i + 32] for i in range(4))
            vt = []

            def evac(c, ps, tok):
                a = AC.op(lambda e: e.activation(V[:, 128 * c:128 * c + 128], ps[:, 0:128], ACT.Copy), tok, start)
                d = DV.op(lambda e: e.tensor_tensor(DT[:, 32 * c:32 * c + 32], ps[:, 128:160], col("dtb", 0, 32), ALU.add), a)
                vt.append(a)
                return d
            lin_tm(("cv", 0), XHk, XLk, XTk, evac)
            a = AC.op(lambda e: e.activation(ADT[:, :], DT[:, :], ACT.Abs), DV.last())
            a = AC.op(lambda e: e.activation(ADT[:, :], ADT[:, :], ACT.Exp, scale=-1.0))
            a = AC.op(lambda e: e.activation(ADT[:, :], ADT[:, :], ACT.Ln, bias=1.0))
            a = AC.op(lambda e: e.activation(EA[:, :], col("alog", 0, 32), ACT.Exp))
            DV.op(lambda e: e.tensor_scalar(DT[:, :], DT[:, :], 0.0, None, ALU.max), a)
            DV.op(lambda e: e.tensor_tensor(DT[:, :], DT[:, :], ADT[:, :], ALU.add))
            v3 = lambda t: t[:, :].rearrange("p (c n) -> p c n", c=4)
            DV.op(lambda e: e.tensor_tensor(v3(ADT), v3(DT), EA[:, :].unsqueeze(1).to_broadcast([128, 4, 32]), ALU.mult))
            dtd = DV.op(lambda e: e.tensor_scalar(ADT[:, :], ADT[:, :], -1.0, None, ALU.mult))

            rt = [None]
            qt = [None] * 5
            def qk_tile(n, bank, tok, gain):
                T, SQ, R = ROT[:, 0:512], ROT[:, 512:1024], ROT[:, 1024:1536]
                rot, t1 = ROT[:, 1536:2048], ROT[:, 2048:2560]
                a = AC.op(lambda e: e.activation(SQ, PS[bank][:, :], ACT.Square), tok, start, rt[0])
                m = mm(PS[6][:, :], BLK, SQ, True, True, a, free[6], inc=True)
                a = AC.op(lambda e: e.activation(R, PS[6][:, :], ACT.Sqrt, bias=EPS6), m)
                free[6] = a
                DV.op(lambda e: e.reciprocal(R, R), a)
                d = DV.op(lambda e: e.scalar_tensor_tensor(out=T, in0=PS[bank][:, :], scalar=col(gain), in1=R,
                                                           op0=ALU.mult, op1=ALU.mult))
                free[bank] = d
                qt[n] = rt[0] = rotate(T, blk(QQ, n), rot, t1, COSB, SINB, d, None, rt[0])
            for i in range(2):
                r = lin_fm([("cq", i)], XHk, XLk, XTk)
                for j, (bank, tok) in enumerate(r):
                    qk_tile(2 * i + j, bank, tok, "qn")
            (bank, tok), = lin_fm([("ck", 0)], XHk, XLk, XTk, widths=(128,))
            qk_tile(4, bank, tok, "kn")

            pfree, ptfree, cnt = [None, None], [None, None], [0]
            otok = [None] * 8
            def head(h):
                rows, kv = slice(64 * (h // 4), 64 * (h // 4) + 64), h // 4
                q, k = QQ[rows, 512 * (h % 4):512 * (h % 4) + 512], QQ[rows, 2048:2560]
                def scores(i):
                    bank = 4 + i % 2
                    return mm(PS[bank][:, :], q[:, 128 * i:128 * i + 128], k, True, True, free[bank], qt[h % 4], qt[4], inc=True)
                st = {0: scores(0), 1: scores(1)}
                for i in range(4):
                    u, g, bank = cnt[0] % 2, 4 * h + i, 4 + i % 2
                    cnt[0] += 1
                    p, pt = blk(P, u), blk(PT, u)
                    DV.op(lambda e: e.tensor_reduce(MX[:, g:g + 1], PS[bank][:, :], AX, ALU.max), st[i], start)
                    d = DV.op(lambda e: e.tensor_scalar(NM[:, g:g + 1], MX[:, g:g + 1], -0.125, None, ALU.mult))
                    a = AC.op(lambda e: e.activation(p, PS[bank][:, :], ACT.Exp, bias=NM[:, g:g + 1], scale=0.125,
                                                     accum_out=SU[:, g:g + 1]), d, pfree[u])
                    free[bank] = a
                    if i + 2 < 4:
                        st[i + 2] = scores(i + 2)
                    yield
                    for kb in range(4):
                        t = tr(PS[6][:, 128 * kb:128 * kb + 128], p[:, 128 * kb:128 * kb + 128], IDN, a, free[6], inc=(kb == 3))
                    pfree[u] = t
                    if i % 2:
                        c = AC.op(lambda e: e.activation(pt, PS[6][:, :], ACT.Copy), t, ptfree[u])
                    else:
                        c = DV.op(lambda e: e.tensor_copy(pt, PS[6][:, :]), t, ptfree[u])
                    free[6] = c
                    yield
                    for kb in range(4):
                        t = mm(PS[7][:, 64 * i:64 * i + 64], pt[:, 128 * kb:128 * kb + 128],
                               V[:, 128 * kb + 64 * kv:128 * kb + 64 * kv + 64], kb == 0, kb == 3, c, free[7], vt, inc=(kb == 3))
                    ptfree[u] = t
                rc = RC[:, 4 * h:4 * h + 4]
                DV.op(lambda e: e.reciprocal(rc, SU[:, 4 * h:4 * h + 4]), a)
                dst = OT[:, :].rearrange("p (c n) -> p c n", c=4)[:, :, 64 * h:64 * h + 64]
                d = DV.op(lambda e: e.tensor_tensor(dst, PS[7][:, 0:256].rearrange("p (c n) -> p c n", c=4),
                                                    rc.unsqueeze(2).to_broadcast([128, 4, 64]), ALU.mult), t)
                free[7] = d
                otok[h] = d
                yield

            def turn(j):
                for c in range(4):
                    t = tr(PS[6][:, 128 * c:128 * c + 128], OT[:, 512 * c + 128 * j:512 * c + 128 * j + 128], IDN,
                           free[6], otok[2 * j + 1], inc=(c == 3))
                ohtok[j] = split(PS[6][:, :], blk(OTH, j), blk(OTL, j), t)
                free[6] = ohtok[j]
            ohtok = [None] * 4

            def heads():
                for h in range(8):
                    yield from head(h)
                    if h % 2:
                        turn(h // 2)

            o2 = o
            BC = at("cBC", 2048, F32, o2); o2 += 8 * K
            BT = at("cBT", 1024, F32, o2); o2 += 4 * K
            XS = at("cXS", 4096, F32, o2); o2 += 16 * K
            CVT = at("cCVT", 1024, F32, o2); o2 += 4 * K
            sizes["mid"] = o2
            cfree = [None, None]
            xst = [None] * 8
            bct = [None] * 4
            btt = [None] * 2

            def xbc(i):
                r = lin_fm([("cx", i)], XHk, XLk, XTk)
                for jj, (bank, tok) in enumerate(r):
                    j = 2 * i + jj
                    y = blk(CVT, j % 2)
                    a = AC.op(lambda e: e.activation(y, PS[bank][:, :], ACT.Identity, bias=col("sb", j), scale=col("sw2", j)),
                              tok, cfree[j % 2], start)
                    for t in (0, 1, 3, 4):
                        s = t - 2
                        oa, ob_ = max(0, -s), 512 - max(0, s)
                        d = DV.op(lambda e, t=t, s=s, oa=oa, ob_=ob_: e.scalar_tensor_tensor(
                            out=y[:, oa:ob_], in0=PS[bank][:, oa + s:ob_ + s], scalar=col(f"sw{t}", j), in1=y[:, oa:ob_],
                            op0=ALU.mult, op1=ALU.add), a)
                    free[bank] = d
                    if j < 8:
                        a = AC.op(lambda e: e.activation(y, y, ACT.Silu), d)
                        src = y
                    else:
                        src = blk(BC, j - 8)
                        a = AC.op(lambda e: e.activation(src, y, ACT.Silu), d)
                        cfree[j % 2] = a
                        bct[j - 8] = a
                    if j < 10:
                        for c in range(4):
                            t = tr(PS[6][:, 128 * c:128 * c + 128], src[:, 128 * c:128 * c + 128], IDN, a, free[6], inc=(c == 3))
                        if j < 8:
                            cfree[j % 2] = t
                            dst = XS[:, :].rearrange("p (c n) -> p c n", c=4)[:, :, 128 * j:128 * j + 128]
                        else:
                            dst = BT[:, :].rearrange("p (c n) -> p c n", c=4)[:, :, 128 * (j - 8):128 * (j - 8) + 128]
                        f = DV.op(lambda e: e.tensor_copy(dst, PS[6][:, :].rearrange("p (c n) -> p c n", c=4)), t, start)
                        free[6] = f
                        if j < 8:
                            xst[j] = f
                        else:
                            btt[j - 8] = f

            gen = heads()
            for i in range(6):
                for _ in range(12):
                    next(gen, None)
                xbc(i)
            for _ in gen:
                pass

            start2 = marks()
            o = E0
            Y = at("cY", 4096, F32, o); o += 16 * K
            CB = at("cCB", 1024, F32, o); o += 4 * K
            RF = at("cRF", 1024, F32, o, 16); o += 4 * K
            EM = at("cEM", 2048, F32, o); o += 8 * K
            XD = at("cXD", 1024, F32, o); o += 4 * K
            assert o <= E0 + 36 * K
            o = o2 - 4 * K
            PRV = FP[:, 1152:3200]
            XW = at("cXW", 1024, F32, o); o += 4 * K
            YT_ = at("cYT", 512, F32, E0 + 36 * K)
            sizes["ssd"] = o

            for c in range(4):
                mm(PS[4][:, 32 * c:32 * c + 16], UPP, ADT[:, 32 * c:32 * c + 16], True, True, dtd, free[4], start2)
                t = mm(PS[4][:, 32 * c + 16:32 * c + 32], LOW, ADT[:, 32 * c + 16:32 * c + 32], True, True, inc=True)
            for c in range(4):
                t5 = mm(PS[5][:, 32 * c:32 * c + 32], ONE, ADT[:, 32 * c:32 * c + 32], True, True, free[5], inc=True)
            d = DV.op(lambda e: e.tensor_copy(ACS[:, :], PS[4][:, 0:128]), t)
            acsd = d
            free[4] = d
            nacd = DV.op(lambda e: e.tensor_scalar(NAC[:, :], ACS[:, :], -1.0, None, ALU.mult))
            d = DV.op(lambda e: e.tensor_copy(TOT[:, :], PS[5][:, 0:128]), t5)
            free[5] = d
            d = DV.op(lambda e: e.tensor_tensor(DSD[:, :], TOT[:, :], ACS[:, :], ALU.subtract))
            AC.op(lambda e: e.activation(DSD[:, :], DSD[:, :], ACT.Exp), d)
            AC.op(lambda e: e.activation(EAC[:, :], ACS[:, :], ACT.Exp))
            a = AC.op(lambda e: e.activation(CD[:, :], TOT[:, :], ACT.Exp))
            dec = DV.op(lambda e: e.tensor_tensor(DSD[:, :], DSD[:, :], DT[:, :], ALU.mult), a)
            for dr in range(2):
                for c in range(4):
                    t = tr(PS[4 + dr][0:16, 128 * c:128 * c + 128], ACS[:, 32 * c + 16 * dr:32 * c + 16 * dr + 16], IDN,
                           acsd, free[4 + dr], inc=(c == 3))
                rfd = DV.op(lambda e, dr=dr: e.tensor_copy(RF[:, 512 * dr:512 * dr + 512], PS[4 + dr][0:16, :]), t)
                free[4 + dr] = rfd
            for g in range(2):
                for c in range(4):
                    s = slice(512 * g + 128 * c, 512 * g + 128 * c + 128)
                    s2 = slice(1024 + 512 * g + 128 * c, 1024 + 512 * g + 128 * c + 128)
                    t = mm(PS[6][:, 128 * c:128 * c + 128], BC[:, s], BC[:, s2], True, True, bct, free[6], inc=(c == 3))
                cbd = DV.op(lambda e, g=g: e.tensor_copy(blk(CB, g), PS[6][:, :]), t)
                free[6] = cbd
            yv = Y[:, :].rearrange("p (c n) -> p c n", c=4)
            for c in range(4):
                src = XS[:, 1024 * c:1024 * c + 1024].rearrange("p (h n) -> p h n", h=16)
                dst = Y[:, 1024 * c:1024 * c + 1024].rearrange("p (h n) -> p h n", h=16)
                yt0 = PO.op(lambda e, src=src, dst=dst: e.tensor_tensor(
                    dst, src, col("dskip", 0, 16).unsqueeze(2).to_broadcast([128, 16, 64]), ALU.mult), xst, start2)

            emfree = [None, None]
            xdfree = [None, None]

            def shead(h):
                g, u = h // 8, h % 2
                em = [EM[:, 1024 * u + 512 * dr:1024 * u + 512 * dr + 512] for dr in range(2)]
                xd = [XD[:, 512 * u + 256 * dr:512 * u + 256 * dr + 256] for dr in range(2)]
                mt = []
                for dr in range(2):
                    bank = 4 + dr
                    mm(PS[bank][:, :], IDN[0:16, h:h + 1].to_broadcast([16, 128]), RF[:, 512 * dr:512 * dr + 512], True, False,
                       rfd, free[bank])
                    t = mm(PS[bank][:, :], IDB, MF if dr == 0 else MB, False, True, inc=True)
                    for c in range(4):
                        n = 32 * c + 16 * dr + h
                        a = AC.op(lambda e, c=c, n=n, dr=dr, bank=bank: e.activation(
                            em[dr][:, 128 * c:128 * c + 128], PS[bank][:, 128 * c:128 * c + 128], ACT.Exp,
                            bias=NAC[:, n:n + 1]), t, nacd, emfree[u])
                    free[bank] = a
                    DV.op(lambda e, dr=dr: e.tensor_tensor(em[dr], em[dr], blk(CB, g), ALU.mult), a)
                    xs = XS[:, :].rearrange("p (c n) -> p c n", c=4)[:, :, 64 * h:64 * h + 64]
                    dt = DT[:, :].rearrange("p (c n) -> p c n", c=4)[:, :, 16 * dr + h:16 * dr + h + 1]
                    mt.append(DV.op(lambda e, dr=dr, xs=xs, dt=dt: e.tensor_tensor(
                        xd[dr].rearrange("p (c n) -> p c n", c=4), xs, dt.to_broadcast([128, 4, 64]), ALU.mult),
                        xst, xdfree[u], start2))
                yield
                for c in range(4):
                    for dr in range(2):
                        t = mm(PS[7][:, 64 * c:64 * c + 64], em[dr][:, 128 * c:128 * c + 128], xd[dr][:, 64 * c:64 * c + 64],
                               dr == 0, dr == 1, mt, free[7], inc=(c == 3 and dr == 1))
                emfree[u] = xdfree[u] = t
                dst = yv[:, :, 64 * h:64 * h + 64]
                d = DV.op(lambda e: e.tensor_tensor(dst, PS[7][:, 0:256].rearrange("p (c n) -> p c n", c=4), dst, ALU.add), t, yt0)
                free[7] = d
                yield

            def states():
                prv_t = [None, None]
                xwfree = [None, None]
                for dr in range(2):
                    cs = (0, 1, 2, 3) if dr == 0 else (3, 2, 1, 0)
                    for idx, c in enumerate(cs):
                        if idx:
                            for g in range(2):
                                b = pick()
                                t = mm(PS[b][:, :], BC[:, 1024 + 512 * g + 128 * c:1024 + 512 * g + 128 * c + 128],
                                       PRV[:, 1024 * dr + 512 * g:1024 * dr + 512 * g + 512], True, True,
                                       free[b], bct, prv_t[dr], inc=True)
                                sc = EAC[:, 32 * c + 16 * dr + 8 * g:32 * c + 16 * dr + 8 * g + 8]
                                tmp = YT_[:, :]
                                d = DV.op(lambda e, b=b, sc=sc, tmp=tmp: e.tensor_tensor(
                                    tmp.rearrange("p (h n) -> p h n", h=8), PS[b][:, :].rearrange("p (h n) -> p h n", h=8),
                                    sc.unsqueeze(2).to_broadcast([128, 8, 64]), ALU.mult), t, dec, start2)
                                free[b] = d
                                dst = Y[:, 1024 * c + 512 * g:1024 * c + 512 * g + 512]
                                d = DV.op(lambda e, dst=dst, tmp=tmp: e.tensor_tensor(dst, dst, tmp, ALU.add), yt0)
                            yield
                        if idx < 3:
                            for g in range(2):
                                b = pick()
                                xw = blk(XW, g)
                                sc = DSD[:, 32 * c + 16 * dr + 8 * g:32 * c + 16 * dr + 8 * g + 8]
                                p = DV.op(lambda e, xw=xw, sc=sc, c=c, g=g: e.tensor_tensor(
                                    xw.rearrange("p (h n) -> p h n", h=8),
                                    XS[:, 1024 * c + 512 * g:1024 * c + 512 * g + 512].rearrange("p (h n) -> p h n", h=8),
                                    sc.unsqueeze(2).to_broadcast([128, 8, 64]), ALU.mult), dec, xst, xwfree[g], start2)
                                t = mm(PS[b][:, :], BT[:, 256 * c + 128 * g:256 * c + 128 * g + 128], xw, True, True,
                                       free[b], p, btt, inc=True)
                                xwfree[g] = t
                                pv = PRV[:, 1024 * dr + 512 * g:1024 * dr + 512 * g + 512]
                                if idx == 0:
                                    d = DV.op(lambda e, pv=pv, b=b: e.tensor_copy(pv, PS[b][:, :]), t, start2)
                                else:
                                    cd = CD[:, 32 * c + 16 * dr + 8 * g:32 * c + 16 * dr + 8 * g + 8]
                                    DV.op(lambda e, pv=pv, cd=cd: e.tensor_tensor(
                                        pv.rearrange("p (h n) -> p h n", h=8), pv.rearrange("p (h n) -> p h n", h=8),
                                        cd.unsqueeze(2).to_broadcast([128, 8, 64]), ALU.mult), PE.last())
                                    d = DV.op(lambda e, pv=pv, b=b: e.tensor_tensor(pv, pv, PS[b][:, :], ALU.add), t)
                                free[b] = d
                            prv_t[dr] = d
                            yield

            gs = states()

            def sheads():
                for h in range(16):
                    yield from shead(h)
                    next(gs, None)
            for _ in sheads():
                pass
            for _ in gs:
                pass
            for i in range(4):
                def evac(c, ps, tok):
                    z = XW[:, 256 * (c % 4):256 * (c % 4) + 256]
                    a = AC.op(lambda e: e.activation(z, ps[:, 0:256], ACT.Silu), tok, marks() if i == 0 and c == 0 else None, DV.last())
                    y = Y[:, 1024 * c + 256 * i:1024 * c + 256 * i + 256]
                    d = DV.op(lambda e: e.tensor_tensor(y, y, z, ALU.mult), a)
                    return a
                lin_tm(("cz", i), XHk, XLk, XTk, evac)
            st = marks()
            for c in range(4):
                a = AC.op(lambda e, c=c: e.activation(XS[:, 0:1024], Y[:, 1024 * c:1024 * c + 1024], ACT.Square,
                                                      accum_out=SS[:, c:c + 1]), st)
            a = AC.op(lambda e: e.activation(SS[:, 4:8], SS[:, 0:4], ACT.Sqrt, bias=EPS6, scale=1.0 / D))
            d = DV.op(lambda e: e.reciprocal(SS[:, 8:12], SS[:, 4:8]), a)
            for c in range(4):
                d = DV.op(lambda e, c=c: e.tensor_scalar(Y[:, 1024 * c:1024 * c + 1024], Y[:, 1024 * c:1024 * c + 1024],
                                                         SS[:, 8 + c:9 + c], None, ALU.mult))
            st = marks()
            yo = E0 + 16 * K
            YTH = at("cYTH", 4096, F32R, yo)
            YTL = at("cYTL", 4096, F32R, yo + 16 * K)
            TT = at("cTT", 1024, F32, yo + 32 * K)
            ytt = [None] * 8
            for j in range(8):
                b = pick()
                for c in range(4):
                    t = tr(PS[b][:, 128 * c:128 * c + 128], Y[:, 1024 * c + 128 * j:1024 * c + 128 * j + 128], IDN,
                           free[b], st, inc=(c == 3))
                tt = blk(TT, j % 2)
                f = DV.op(lambda e: e.tensor_scalar(tt, PS[b][:, :], col("ssdn", j), None, ALU.mult), t, ytt[j - 2] if j > 1 else None, st)
                free[b] = f
                ytt[j] = split(tt, blk(YTH, j), blk(YTL, j), f)
            MIXH = at("cMXH", 4096, F32R, yo + 36 * K)
            MIXL = at("cMXL", 4096, F32R, E0)
            SG = FP[:, 1152:3200]
            sizes["mix"] = yo + 60 * K
            st = marks()
            st2 = [st]
            mtok = [None] * 8
            sgf = [None, None]
            for i in range(4):
                ga = lin_fm([("cga", i)], XHk, XLk, XTk)
                ta = []
                for j, (bank, tok) in enumerate(ga):
                    x = SG[:, 1024 * j:1024 * j + 512]
                    a = AC.op(lambda e: e.activation(x, PS[bank][:, :], ACT.Sigmoid), tok, sgf[j], st)
                    free[bank] = a
                    ta.append(a)
                pa = lin_fm([("cpa", i)], lambda k: blk(OTH, k), lambda k: blk(OTL, k), lambda k: ohtok[k])
                for j, (bank, tok) in enumerate(pa):
                    x = SG[:, 1024 * j:1024 * j + 512]
                    d = DV.op(lambda e: e.tensor_tensor(x, x, PS[bank][:, :], ALU.mult), tok, ta)
                    free[bank] = d
                gsr = lin_fm([("cgs", i)], XHk, XLk, XTk)
                tb = []
                for j, (bank, tok) in enumerate(gsr):
                    x = SG[:, 1024 * j + 512:1024 * j + 1024]
                    a = AC.op(lambda e: e.activation(x, PS[bank][:, :], ACT.Sigmoid), tok, sgf[j])
                    free[bank] = a
                    tb.append(a)
                psr = lin_fm([("cps", i)], lambda k: blk(YTH, k), lambda k: blk(YTL, k), lambda k: ytt[k])
                for j, (bank, tok) in enumerate(psr):
                    x, x2 = SG[:, 1024 * j:1024 * j + 512], SG[:, 1024 * j + 512:1024 * j + 1024]
                    d = DV.op(lambda e: e.tensor_tensor(x2, x2, PS[bank][:, :], ALU.mult), tok, tb)
                    free[bank] = d
                    p = PO.op(lambda e: e.tensor_tensor(x, x, x2, ALU.add), d)
                    sgf[j] = mtok[2 * i + j] = split(x, blk(MIXH, 2 * i + j), blk(MIXL, 2 * i + j), p)
            st = marks()
            nb = norm_bufs(yo)
            nb["tok"] = st

            def evac_y(j, bank, tok, first):
                y = blk(YH, j)
                a = AC.op(lambda e: e.activation(y, PS[bank][:, :], ACT.Copy), tok, first)
                free[bank] = a
                acc_step(nb, j, y, a, False)
            for i in range(4):
                for j, (bank, tok) in enumerate(lin_fm([("co", i)], lambda k: blk(MIXH, k), lambda k: blk(MIXL, k), lambda k: mtok[k])):
                    evac_y(2 * i + j, bank, tok, st)
            r = stats(nb, EPS6, False)
            nb2 = norm_bufs(yo + 14 * K)
            nb2["tok"] = st
            for j in range(8):
                y, x = blk(YH, j), blk(XR, j)
                DV.op(lambda e: e.scalar_tensor_tensor(out=y, in0=y, scalar=col("n1post", j), in1=nb["RS"][:, :],
                                                       op0=ALU.mult, op1=ALU.mult), r)
                d = DV.op(lambda e: e.tensor_tensor(x, x, y, ALU.add))
                acc_step(nb2, j, x, d, False)
            rms_apply(nb2, XR, None, "n2pre")
            st = marks()
            hh = at("HH2", 512 * FF, F32R, O0)
            hl = at("HL2", 512 * FF, F32R, O0 + 44 * K)
            tmp = FP[:, 1152:3200]
            htok = ffn_up_2(hh, hl, tmp, st)
            nb = norm_bufs_at([FP[:, 1152 + 512 * i:1664 + 512 * i] for i in range(4)], NBX)
            st = marks()
            nb["tok"] = st

            def evac(j, bank, tok):
                y = blk(YH, j)
                a = AC.op(lambda e: e.activation(y, PS[bank][:, :], ACT.Copy), tok, st)
                free[bank] = a
                acc_step(nb, j, y, a, False)
            ffn_down("dn2", hh, hl, htok, evac)
            r = stats(nb, EPS6, False)
            outs = []
            for j in range(8):
                y, x = blk(YH, j), blk(XR, j)
                DV.op(lambda e: e.scalar_tensor_tensor(out=y, in0=y, scalar=col("n2post", j), in1=nb["RS"][:, :],
                                                       op0=ALU.mult, op1=ALU.mult), r)
                d = DV.op(lambda e: e.tensor_tensor(x, x, y, ALU.add))
                sp(lambda e, j=j, x=x: e.dma_start(outT[:, 512 * j:512 * j + 512], x).then_inc(s_out, 16), d)

        NBX = None

        def norm_bufs_at(aps, _):
            names = ("SQ", "A2", "RS", "T1")
            class Whole:
                def __init__(self, ap):
                    self.ap = ap
                def __getitem__(self, k):
                    return self.ap
            return {n: Whole(a) for n, a in zip(names, aps)} | {"A1": Whole(aps[3]), "MS": Whole(aps[3]), "T2": Whole(aps[3])}

        def ffn_up_2(hh, hl, tmp, st):
            return ffn_up("up2", None, hh, hl, tmp, st)

        oh, ol, ot, _ = fox()
        attn_out("ao", oh, ol, ot, "ln_attn_g0", "ln_attn_b0")
        nb = ffn_layer("0", "", "")
        layer_norm(nb, "ln_ffn_g0", "ln_ffn_b0")
        oh, ol, ot, _ = diff()
        attn_out("bo", oh, ol, ot, "ln_attn_g1", "ln_attn_b1")
        nb = ffn_layer("1", "", "")
        XR = at("XR", 4096, F32, R0)
        nb0 = norm_bufs(R0 + 40 * K)
        layer_norm(nb, "ln_ffn_g1", "ln_ffn_b1", final=lambda j: blk(XR, j),
                   post=lambda j, a: acc_step(nb0, j, blk(XR, j), a, False))
        second(XR, nb0)
        if turn == "sp":
            engine.wait_ge(s_out, 16 * 8)
    return used


def whole(nc, *args):
    mem = {}
    order = program(nc, *args, None, mem, None, None)
    with nc.Block() as block:
        @block.sync
        def _(e):
            program(nc, *args, order, mem, "sp", e)

        @block.tensor
        def _(e):
            program(nc, *args, order, mem, "pe", e)

        @block.scalar
        def _(e):
            program(nc, *args, order, mem, "act", e)

        @block.vector
        def _(e):
            program(nc, *args, order, mem, "dve", e)

        @block.gpsimd
        def _(e):
            program(nc, *args, order, mem, "pool", e)


def kernel(**inputs):
    import concourse.bacc as bacc
    from concourse.bass_utils import run_bass_kernel_spmd

    a = {k: np.asarray(v) for k, v in inputs.items()}
    w = {"a_w_in": a["a_w_in"][0], "a_w_out": a["a_w_out"][0], "kv_w": a["kv_w"], "b_w_q": a["b_w_q"][0],
         "b_w_out": a["b_w_out"][0], "w_in_2": a["w_in_2"][0], "w_attn_proj_2": a["w_attn_proj_2"][0],
         "w_ssd_proj_2": a["w_ssd_proj_2"][0], "w_out_2": a["w_out_2"][0], "w_gate_up_2": a["w_gate_up_2"][0],
         "w_down_2": a["w_down_2"][0]}
    for i in range(2):
        w[f"ffn_w_in{i}"], w[f"ffn_w_out{i}"] = a["ffn_w_in"][i], a["ffn_w_out"][i]
    places, total = unit_places()
    wall = np.empty(total, np.float32)
    for key, parts in unit_table().items():
        off, kt, n = places[key]
        m = np.concatenate([w[s][128 * k0:128 * (k0 + kk)][:, c] for s, k0, kk, c in parts], axis=1)
        wall[off:off + 128 * kt * n] = m.reshape(kt, 128, n).transpose(1, 0, 2).reshape(-1)

    sm, nsm = small_table()
    small = np.zeros((128, nsm), np.float32)

    def put(name, v, rep=False):
        o, n = sm[name]
        v = np.asarray(v)
        small[:, o:o + n] = np.broadcast_to(v.reshape(1, n), (128, n)) if rep else v.reshape(n, 128).T

    for i in range(2):
        put(f"ln_attn_g{i}", a["ln_attn_g"][i])
        put(f"ln_attn_b{i}", a["ln_attn_b"][i])
        put(f"ln_ffn_g{i}", a["ln_ffn_g"][i])
        put(f"ln_ffn_b{i}", a["ln_ffn_b"][i])
        for t in range(3):
            put(f"cw{i}{t}", a["ffn_conv_w"][i, t])
        put(f"cb{i}", a["ffn_conv_b"][i])
    for t in range(5):
        put(f"sw{t}", a["conv_w_2"][0, t])
    put("sb", a["conv_b_2"][0])
    for n, s in (("n1pre", "norm1_pre_2"), ("n1post", "norm1_post_2"), ("n2pre", "norm2_pre_2"),
                 ("n2post", "norm2_post_2"), ("ssdn", "ssd_norm_2")):
        put(n, a[s][0])
    t64 = turned(0)
    put("qn", np.concatenate([a["q_norm_2"][0][t64]] * 2))
    put("kn", np.concatenate([a["k_norm_2"][0][t64]] * 2))
    small[0:16, sm["bf"][0]] = a["a_b_f"][0]
    put("subln", a["b_subln_g"][0])
    put("lam", a["b_lambda"][0].reshape(-1), True)
    put("dtb", np.concatenate([a["dt_bias_f_2"][0], a["dt_bias_b_2"][0]]), True)
    put("alog", np.concatenate([a["a_log_f_2"][0], a["a_log_b_2"][0]]), True)
    put("dskip", a["d_skip_2"][0], True)
    fp, masks = const_arrays()
    xT = np.ascontiguousarray(a["x"][0].T.reshape(8, 128, S).transpose(1, 0, 2).reshape(128, 8 * S))
    arrays = {"xT": xT, "wall": wall, "small": small, "cfp": fp, "cmask": masks}

    nc = bacc.Bacc("TRN2", target_bir_lowering=False, num_devices=1)
    aps = [nc.dram_tensor(k, v.shape, mybir.dt.from_np(v.dtype), kind="ExternalInput").ap() for k, v in arrays.items()]
    out = nc.dram_tensor("outT", (128, 8 * S), F32, kind="ExternalOutput").ap()
    whole(nc, *aps, out)
    r = run_bass_kernel_spmd(nc, [arrays], core_ids=[0])
    o = r.results[0]["outT"]
    return np.ascontiguousarray(o.reshape(128, 8, S).transpose(1, 0, 2).reshape(D, S).T).reshape(1, S, D)
```

```python
import math

import numpy as np

import concourse.bass as bass
from concourse import mybir

F32 = mybir.dt.float32
F32R = mybir.dt.float32r
BF16 = mybir.dt.bfloat16
ALU = mybir.AluOpType
ACT = mybir.ActivationFunctionType
AX = mybir.AxisListType.X

S = 512
D = 1024
KT = 8
FF = 22
ALPHA = 4.0 ** 0.25
LAM_INIT = 0.8 - 0.6 * math.exp(-0.3)
NEG = -1.0e30
LAGS = (0, 2, 3, 5)
RATES = (1.0, 0.6, 1.1, 0.3)
FIRST = 16640



def rng(a, b):
    return list(range(a, b))


def halves(h):
    return [64 * h + 2 * d + e for e in range(2) for d in range(32)]


def turned(h):
    return [64 * h + x for x in rng(0, 16) + rng(32, 48) + rng(16, 32) + rng(48, 64)]


def unit_table():
    u = {}
    u["f", 0] = [("a_w_in", 0, 8, rng(3072, 3088))]
    for i in range(4):
        u["av", i] = [("a_w_in", 0, 8, rng(2048 + 256 * i, 2304 + 256 * i))]
    for i in range(8):
        u["aqk", i] = [("a_w_in", 0, 8, rng(128 * i, 128 * i + 128) + rng(1024 + 128 * i, 1152 + 128 * i))]
    for i in range(4):
        u["ao", i] = [("a_w_out", 0, 8, rng(256 * i, 256 * i + 256))]
    for lay in ("0", "1"):
        w1, w2 = "ffn_w_in" + lay, "ffn_w_out" + lay
        for j in range(FF):
            u["up" + lay, j] = [(w1, 0, 8, rng(128 * j, 128 * j + 128) + rng(2816 + 128 * j, 2944 + 128 * j))]
        for i in range(4):
            for p, (k0, kt) in enumerate(((0, 8), (8, 7), (15, 7))):
                u["dn" + lay, i, p] = [(w2, k0, kt, rng(256 * i, 256 * i + 256))]
    for i in range(4):
        u["bv", i] = [("kv_w", 0, 8, rng(1024 + 256 * i, 1280 + 256 * i))]
    for h in range(8):
        c = rng(64 * h, 64 * h + 64) + rng(512 + 64 * h, 576 + 64 * h)
        u["bqk", h] = [("b_w_q", 0, 8, c), ("kv_w", 0, 8, c)]
    for i in range(4):
        u["bo", i] = [("b_w_out", 0, 8, rng(256 * i, 256 * i + 256))]
    u["cv", 0] = [("w_in_2", 0, 8, rng(640, 768) + rng(3328, 3360))]
    for i in range(2):
        c = []
        for j in (2 * i, 2 * i + 1):
            c += turned(j) + turned(j + 4)
        u["cq", i] = [("w_in_2", 0, 8, c)]
    u["ck", 0] = [("w_in_2", 0, 8, [512 + x for x in turned(0) + turned(1)])]
    for i in range(6):
        u["cx", i] = [("w_in_2", 0, 8, rng(1792 + 256 * i, 2048 + 256 * i))]
    for i in range(4):
        u["cz", i] = [("w_in_2", 0, 8, rng(768 + 256 * i, 1024 + 256 * i))]
        u["cga", i] = [("w_in_2", 0, 8, rng(3360 + 256 * i, 3616 + 256 * i))]
        u["cgs", i] = [("w_in_2", 0, 8, rng(4384 + 256 * i, 4640 + 256 * i))]
        u["cpa", i] = [("w_attn_proj_2", 0, 4, rng(256 * i, 256 * i + 256))]
        u["cps", i] = [("w_ssd_proj_2", 0, 8, rng(256 * i, 256 * i + 256))]
        u["co", i] = [("w_out_2", 0, 8, rng(256 * i, 256 * i + 256))]
        for p, (k0, kt) in enumerate(((0, 8), (8, 7), (15, 7))):
            u["dn2", i, p] = [("w_down_2", k0, kt, rng(256 * i, 256 * i + 256))]
    for j in range(FF):
        u["up2", j] = [("w_gate_up_2", 0, 8, rng(128 * j, 128 * j + 128) + rng(2816 + 128 * j, 2944 + 128 * j))]
    return u


def unit_places():
    at, out = 0, {}
    for key, parts in unit_table().items():
        kt, n = parts[0][2], sum(len(p[3]) for p in parts)
        out[key] = (at, kt, n)
        at += 128 * kt * n
    return out, at



def small_table():
    names = [("ln_attn_g0", 8), ("ln_attn_b0", 8), ("ln_ffn_g0", 8), ("ln_ffn_b0", 8),
             ("ln_attn_g1", 8), ("ln_attn_b1", 8), ("ln_ffn_g1", 8), ("ln_ffn_b1", 8),
             ("cw00", 44), ("cw01", 44), ("cw02", 44), ("cb0", 44),
             ("cw10", 44), ("cw11", 44), ("cw12", 44), ("cb1", 44),
             ("sw0", 12), ("sw1", 12), ("sw2", 12), ("sw3", 12), ("sw4", 12), ("sb", 12),
             ("n1pre", 8), ("n1post", 8), ("n2pre", 8), ("n2post", 8), ("ssdn", 8),
             ("qn", 1), ("kn", 1), ("bf", 1), ("subln", 1),
             ("lam", 256), ("dtb", 32), ("alog", 32), ("dskip", 16)]
    at, out = 0, {}
    for name, n in names:
        out[name] = (at, n)
        at += n
    return out, at


def const_arrays():
    p = np.arange(128)
    ident = np.eye(128, dtype=np.float32)
    upper = (p[:, None] <= p[None, :]).astype(np.float32)
    lower = (p[:, None] >= p[None, :]).astype(np.float32)
    mean = np.full((128, 128), 1.0 / D, np.float32)
    blk = np.kron(np.eye(2), np.full((64, 64), 1.0 / 64)).astype(np.float32)
    ones = np.ones((128, 512), np.float32)
    causal = np.where(p[None, :] <= p[:, None], 0.0, NEG)
    chunk = np.where(p[None, :] < (p[:, None] // 64 + 1) * 64, 0.0, NEG)
    mf = np.where(p[:, None] <= p[None, :], 0.0, NEG)
    mb = np.where(p[:, None] >= p[None, :], 0.0, NEG)
    inv = (1.0 / (np.float32(10000.0) ** (np.arange(0, 64, 2, dtype=np.float32) / np.float32(64)))).astype(np.float32)
    ang = np.arange(S, dtype=np.float32)[:, None] * inv[None, :]
    inv2 = (np.float32(10000.0) ** (-np.arange(0, 32, 2, dtype=np.float32) / np.float32(32))).astype(np.float32)
    t = np.arange(S)
    ang2 = np.concatenate([(t // 64).astype(np.float32)[:, None] * inv2, (t % 64).astype(np.float32)[:, None] * inv2], 1)
    tabs = []
    for a in (ang, ang2):
        c, s = np.cos(a).astype(np.float32).T, np.sin(a).astype(np.float32).T
        tabs += [np.concatenate([c] * 4, 0), np.concatenate([-s, s, -s, s], 0)]
    fp = np.concatenate([ident, upper, lower, mean, blk, ones] + tabs, 1).astype(np.float32)
    masks = np.concatenate([np.eye(128), causal, chunk] + [mf] * 4 + [mb] * 4, 1).astype(np.float32)
    return fp, masks


class Queue:

    def __init__(self, sem, chained, eng):
        self.sem, self.n, self.chained, self.eng, self.seen = sem, 0, chained, eng, {}

    def op(self, fn, *after, inc=True, chain=True):
        if self.eng is not None:
            waits = list(flat(after))
            if self.chained and chain and self.n:
                waits.append((self.sem, self.n))
            need = {}
            for sem, v in waits:
                if v > self.seen.get(sem.name, 0) and v > need.get(sem.name, (None, 0))[1]:
                    need[sem.name] = (sem, v)
            for name, (sem, v) in need.items():
                self.eng.wait_ge(sem, v)
                self.seen[name] = v
            ins = fn(self.eng)
            if inc:
                ins.then_inc(self.sem, 1)
        if inc:
            self.n += 1
        return (self.sem, self.n)

    def last(self):
        return (self.sem, self.n) if self.n else None


def flat(x):
    for y in x:
        if y is None:
            continue
        if isinstance(y, list) or (isinstance(y, tuple) and y and (y[0] is None or isinstance(y[0], (list, tuple)))):
            yield from flat(y)
        elif isinstance(y, tuple) and len(y) == 2:
            yield y


def program(nc, xT, wall, small, cfp, cmask, outT, order, mem, turn, engine):
    places, _ = unit_places()
    sm, nsm = small_table()
    used = []
    sizes = {}
    if True:
        def sem(name):
            if name not in mem:
                mem[name] = nc.alloc_semaphore(name=name)
            return mem[name]

        s_pe, s_act, s_dve, s_pool = sem("s_pe"), sem("s_act"), sem("s_dve"), sem("s_pool")
        s_raw = [sem("s_raw0"), sem("s_raw1")]
        s_in = sem("s_in")
        s_x = sem("s_x")
        s_xa = sem("s_xa")
        s_out = sem("s_out")
        PE, AC, DV, PO, SP = (Queue(q, c, engine if turn == n else None) for q, c, n in (
            (s_pe, False, "pe"), (s_act, True, "act"), (s_dve, True, "dve"), (s_pool, True, "pool"), (None, False, "sp")))

        def sp(fn, *after):
            SP.op(fn, *after, inc=False)

        def at(name, n, dt, off, parts=128):
            if name not in mem:
                mem[name] = nc.alloc_sbuf_tensor_at(name, [parts, n], dt, offset=FIRST + off)
            return mem[name]

        K = 1024
        base = 0
        FP = at("FP", 3200, F32, base)
        MK = at("MK", 1408, BF16, base + 12800)
        MKF = at("MKF", 1408, F32, 100 * K)
        SM = at("SM", nsm, F32, base + 15616)
        base = 15616 + nsm * 4
        base = (base + 63) // 64 * 64
        TN = at("TN", 128, F32, base)
        base += 512
        LAMT = at("LAMT", 64, F32, base)
        base += 256
        NEGC = at("NEGC", 64, F32, base)
        base += 256
        RAW = [at(f"RAW{i}", 2048, F32, base + 8 * K * i) for i in range(2)]
        base += 16 * K
        HI = [at(f"HI{i}", 2048, F32R, base + 8 * K * i) for i in range(2)]
        base += 16 * K
        LO = [at(f"LO{i}", 2048, F32R, base + 8 * K * i) for i in range(2)]
        base += 16 * K
        XH = at("XH", 4096, F32R, base)
        YH = at("YH", 4096, F32, base)
        base += 16 * K
        XL = at("XL", 4096, F32R, base)
        YL = at("YL", 4096, F32, base)
        base += 16 * K
        R0 = base
        sizes["free"] = R0
        if "PS" not in mem:
            mem["PS"] = [nc.alloc_psum_tensor(f"PS{i}", [128, 512], F32) for i in range(8)]
        PS = mem["PS"]

        IDN, UPP, LOW, MEAN, BLK, ONE = (FP[:, 128 * i:128 * i + 128] for i in range(6))
        ONE512 = FP[:, 640:1152]
        COSA, SINA, COSB, SINB = (FP[:, 1152 + 512 * i:1664 + 512 * i] for i in range(4))
        IDB, CAUS, CHNK = (MK[:, 128 * i:128 * i + 128] for i in range(3))
        MF, MB = MK[:, 384:896], MK[:, 896:1408]

        def col(name, j=0, n=1):
            a = sm[name][0]
            return SM[:, a + j:a + j + n]

        def blk(t, j, w=512):
            return t[:, w * j:w * j + w]

        free = [None] * 8

        def marks():
            return [PE.last(), AC.last(), DV.last(), PO.last()]

        xtok = [None] * 8

        def split(src, h, l, *after, rest=None):
            a = AC.op(lambda e: e.activation(h, src, ACT.Copy), *after)
            return (rest or DV).op(lambda e: e.tensor_tensor(l, src, h.bitcast(F32), ALU.subtract), a)

        XF = at("XF", 4096, F32, 120 * K)
        sp(lambda e: e.dma_start(XF[:, 0:1024], xT[:, 0:1024]).then_inc(s_xa, 16))
        sp(lambda e: e.dma_start(XF[:, 1024:4096], xT[:, 1024:4096]).then_inc(s_x, 16))
        sp(lambda e: e.dma_start(SM[:, :], small).then_inc(s_in, 16))
        sp(lambda e: e.dma_start(FP[:, :], cfp).then_inc(s_in, 16))
        sp(lambda e: e.dma_start(MKF[:, :], cmask).then_inc(s_in, 16))
        INP = (s_in, 48)
        for j in range(8):
            xtok[j] = split(blk(XF, j), blk(XH, j), blk(XL, j), (s_xa, 16) if j < 2 else (s_x, 16))
        DV.op(lambda e: e.tensor_copy(MK[:, :], MKF[:, :]), INP)
        DV.op(lambda e: e.memset(NEGC[:, 0:1], 1e-5))
        DV.op(lambda e: e.memset(NEGC[:, 1:2], 1e-6))
        CONST = DV.op(lambda e: e.memset(NEGC[:, 2:3], 1.0))
        EPS5, EPS6 = NEGC[:, 0:1], NEGC[:, 1:2]

        raw_free = [None, None]
        part_free = [None, None]
        made = []

        def load_raw(i):
            key = order[i]
            off, kt, n = places[key]
            r = RAW[i % 2]
            src = wall[off:off + 128 * kt * n].rearrange("(p n) -> p n", p=128)
            sp(lambda e: e.dma_start(r[:, 0:kt * n], src).then_inc(s_raw[i % 2], 16), raw_free[i % 2])

        def split_steps(i):
            off, kt, n = places[order[i]]
            s = i % 2
            landed = (s_raw[s], 16 * (i // 2 + 1))
            highs, toks = [], []
            made.append(toks)
            cuts = [(2 * k * n, min(2 * k + 2, kt) * n) for k in range((kt + 1) // 2)]
            for p in range(len(cuts) + 1):
                if p:
                    a, b = cuts[p - 1]
                    r, h, l = RAW[s][:, a:b], HI[s][:, a:b], LO[s][:, a:b]
                    q = DV if p % 2 else PO
                    toks.append(q.op(lambda e: e.tensor_tensor(l, r, h.bitcast(F32), ALU.subtract),
                                     highs[p - 1], part_free[s], chain=False))
                if p < len(cuts):
                    a, b = cuts[p]
                    r, h = RAW[s][:, a:b], HI[s][:, a:b]
                    highs.append(AC.op(lambda e: e.activation(h, r, ACT.Copy), landed, part_free[s], chain=False))
                if p < len(cuts):
                    yield
            raw_free[s] = [highs[-1], toks[-2:]]
            if i + 2 < len(order):
                load_raw(i + 2)

        parts_due = [None, 0]

        def part_step(n):
            if parts_due[0] is not None:
                parts_due[1] += n
                if parts_due[1] >= 2.5:
                    parts_due[1] -= 2.5
                    next(parts_due[0], None)

        def take(key):
            i = len(used)
            used.append(key)
            off, kt, n = places[key]
            if order is None:
                return HI[0], LO[0], kt, n, lambda k: None, lambda t: None
            assert order[i] == key
            if i == 0:
                load_raw(0)
                load_raw(1)
                parts_due[0] = split_steps(0)
            if parts_due[0] is not None:
                for _ in parts_due[0]:
                    pass
            parts_due[0], parts_due[1] = (split_steps(i + 1), 2.0) if i + 1 < len(order) else (None, 0)

            def release(t):
                part_free[i % 2] = t
            return HI[i % 2], LO[i % 2], kt, n, (lambda k: made[i][k // 2]), release

        def mm(out, a, b, start, stop, *after, inc=False):
            return PE.op(lambda e: e.matmul(out, a, b, start=start, stop=stop), *after, inc=inc)

        def tr(out, src, ident, *after, inc=False):
            return PE.op(lambda e: e.transpose(out, src, ident), *after, inc=inc)

        lin_bank = [0, [0, 1, 2, 3, 4, 7]]

        def pick():
            b = lin_bank[1][lin_bank[0] % len(lin_bank[1])]
            lin_bank[0] += 1
            return b

        beside = [None, 0.0, 0.0]

        def alongside(gen, rate):
            beside[0], beside[1], beside[2] = gen, rate, 0.0

        def tick(n=1.0):
            part_step(n)
            if beside[0] is not None:
                beside[2] += n * beside[1]
                while beside[2] >= 1.0:
                    beside[2] -= 1.0
                    next(beside[0], None)

        def until(cond):
            while not cond():
                next(beside[0])

        def drain():
            if beside[0] is not None:
                for _ in beside[0]:
                    pass
            beside[0] = None

        def lin_fm(keys, xh, xl, xt, widths=(128, 128), together=False):
            banks = [pick() for _ in widths]
            parts = [take(key) for key in keys]
            total = sum(p[2] for p in parts)
            toks = [None] * len(widths)
            at_k = []
            for p, (hi, lo, kt, n, ready, release) in enumerate(parts):
                at_k += [(p, k) for k in range(kt)]

            def step(j, kk):
                p, k = at_k[kk]
                hi, lo, kt, n, ready, release = parts[p]
                c, w, b = sum(widths[:j]), widths[j], banks[j]
                wh, wl = hi[:, k * n + c:k * n + c + w], lo[:, k * n + c:k * n + c + w]
                o = PS[b][0:w, :]
                mm(o, wh, xh(kk), kk == 0, False, ready(k), xt(kk), free[b] if kk == 0 else None)
                mm(o, wh, xl(kk), False, False)
                toks[j] = mm(o, wl, xh(kk), False, kk == total - 1, inc=(k == kt - 1))
                tick()
            if together:
                for kk in range(total):
                    for j in range(len(widths)):
                        step(j, kk)
            else:
                for j in range(len(widths)):
                    for kk in range(total):
                        step(j, kk)
            for p in parts:
                p[5](toks[-1])
            return list(zip(banks, toks))

        def lin_long(keys, xh, xl, xt, widths=(128, 128)):
            banks = [pick() for _ in widths]
            total = sum(places[k][1] for k in keys)
            kk, toks = 0, [None] * len(widths)
            for key in keys:
                hi, lo, kt, n, ready, release = take(key)
                for k in range(kt):
                    for j, b in enumerate(banks):
                        wh = hi[:, k * n + 128 * j:k * n + 128 * j + 128]
                        wl = lo[:, k * n + 128 * j:k * n + 128 * j + 128]
                        o = PS[b][:, :]
                        mm(o, wh, xh(kk), kk == 0, False, ready(k), xt(kk), free[b] if kk == 0 else None)
                        mm(o, wh, xl(kk), False, False)
                        toks[j] = mm(o, wl, xh(kk), False, kk == total - 1, inc=(k == kt - 1))
                        tick()
                    kk += 1
                release(toks[-1])
            return list(zip(banks, toks))

        def lin_tm(key, xh, xl, xt, evac):
            hi, lo, kt, n, ready, release = take(key)
            for c in range(4):
                b = pick()
                o = PS[b][:, 0:n]
                t = slice(128 * c, 128 * c + 128)
                for k in range(kt):
                    wh, wl = hi[:, k * n:k * n + n], lo[:, k * n:k * n + n]
                    mm(o, xh(k)[:, t], wh, k == 0, False, ready(k), xt(k), free[b])
                    mm(o, xl(k)[:, t], wh, False, False)
                    tok = mm(o, xh(k)[:, t], wl, False, k == kt - 1, inc=(k == kt - 1))
                    tick(0.5)
                if c == 3:
                    release(tok)
                free[b] = evac(c, PS[b], tok)

        def norm_bufs(off):
            return {n: at(f"{n}_{off}_{len(used)}", 512, F32, off + 2048 * i)
                    for i, n in enumerate(("SQ", "A1", "A2", "MS", "RS", "T1", "T2"))}

        def acc_step(nb, j, y, tok, mean):
            sq, a1, a2 = nb["SQ"][:, :], nb["A1"][:, :], nb["A2"][:, :]
            prev = nb.get("tok")
            if j == 0:
                t = [AC.op(lambda e: e.activation(a2, y, ACT.Square), tok, prev)]
                if mean:
                    t.append(PO.op(lambda e: e.tensor_copy(a1, y), tok, prev))
            else:
                t = [AC.op(lambda e: e.activation(sq, y, ACT.Square), tok, nb.get("sqfree"))]
                if j < 7:
                    u = PO.op(lambda e: e.tensor_tensor(a2, a2, sq, ALU.add), t[0], nb["t"])
                    nb["sqfree"] = u
                    t.append(u)
                    if mean:
                        t.append(PO.op(lambda e: e.tensor_tensor(a1, a1, y, ALU.add), tok))
                else:
                    nb["last"] = y
                    t += [tok, nb["t"]]
            nb["t"] = t
            return t

        def stats(nb, eps, mean):
            b1, b2 = 5, 6
            m2, var, rs = TN[:, 32:36], TN[:, 36:40], TN[:, 40:44]
            AC.op(lambda e: e.activation(TN[:, 44:45], NEGC[:, 2:3], ACT.Sqrt), CONST)
            a1, a2, sq, last = nb["A1"], nb["A2"], nb["SQ"], nb["last"]
            for c in range(4):
                s = slice(128 * c, 128 * c + 128)
                if mean:
                    mm(PS[b2][:, 4 + c:5 + c], a1[:, s], MEAN[:, 0:1], True, False, nb["t"], free[b2], CONST)
                    mm(PS[b2][:, 4 + c:5 + c], last[:, s], MEAN[:, 0:1], False, True)
                mm(PS[b2][:, c:c + 1], a2[:, s], MEAN[:, 0:1], True, False, nb["t"], free[b2], CONST)
                t2 = mm(PS[b2][:, c:c + 1], sq[:, s], MEAN[:, 0:1], False, True, inc=True)
            if mean:
                mm(PS[b1][:, :], MEAN, a1[:, :], True, False, free[b1])
                t1 = mm(PS[b1][:, :], MEAN, last, False, True, inc=True)
                a = AC.op(lambda e: e.activation(m2, PS[b2][:, 4:8], ACT.Square), t2, nb_rs[0])
                d = DV.op(lambda e: e.tensor_tensor(var, PS[b2][:, 0:4], m2, ALU.subtract), a)
                a = AC.op(lambda e: e.activation(var, var, ACT.Sqrt, bias=eps), d)
            else:
                a = AC.op(lambda e: e.activation(var, PS[b2][:, 0:4], ACT.Sqrt, bias=eps), t2, nb_rs[0])
            r = DV.op(lambda e: e.reciprocal(rs, var), a, nb_rs[0])
            for c in range(4):
                t = mm(PS[b2][:, 128 * c:128 * c + 128], rs[:, c:c + 1].to_broadcast([128, 128]), IDN, True, True, r, inc=(c == 3))
            nb_rs[0] = t
            nb["tok"] = [t]
            return [t, t1] if mean else t

        nb_rs = [None]

        def residual_tile(j, bank, tok):
            y, yl = blk(YH, j), blk(YL, j)
            d = DV.op(lambda e: e.scalar_tensor_tensor(out=yl, in0=blk(XL, j).bitcast(F32), scalar=ALPHA, in1=PS[bank][:, :],
                                                       op0=ALU.mult, op1=ALU.add), tok)
            free[bank] = d
            return DV.op(lambda e: e.scalar_tensor_tensor(out=y, in0=blk(XH, j).bitcast(F32), scalar=ALPHA, in1=yl,
                                                          op0=ALU.mult, op1=ALU.add))

        def layer_norm(nb, g, b, final=None, post=None):
            r = stats(nb, EPS5, True)
            ts = [nb[n][:, :] for n in ("T1", "T2", "RS")]
            tfree = [None] * 3
            for j in range(8):
                y, t = blk(YH, j), ts[j % 3]
                DV.op(lambda e: e.tensor_tensor(t, PS[5][:, :], y, ALU.subtract), r, tfree[j % 3], marks() if j == 0 else None)
                free[5] = free[6] = d = DV.op(lambda e: e.tensor_tensor(t, t, PS[6][:, :], ALU.mult))
                x = final(j) if final else t
                a = AC.op(lambda e: e.activation(x, t, ACT.Identity, bias=col(b, j), scale=NG[g][:, j:j + 1]), d)
                if post:
                    tfree[j % 3] = a
                    post(j, a)
                else:
                    tfree[j % 3] = xtok[j] = split(x, blk(XH, j), blk(XL, j), a, rest=PO)

        NG = {}
        for i, g in enumerate(("ln_attn_g0", "ln_ffn_g0", "ln_attn_g1", "ln_ffn_g1")):
            o = TN[:, 8 * i:8 * i + 8]
            NG[g] = o
            DV.op(lambda e, o=o, g=g: e.tensor_scalar(o, col(g, 0, 8), -1.0, None, ALU.mult), INP)
        XHk, XLk, XTk = (lambda k: blk(XH, k)), (lambda k: blk(XL, k)), (lambda k: xtok[k])

        def staggered(items, stages, lags):
            for n in range(len(items) + lags[-1]):
                for s in reversed(range(len(stages))):
                    if 0 <= n - lags[s] < len(items):
                        yield from stages[s](items[n - lags[s]])

        def fox():
            o = R0
            V = at("aV", 4096, F32, o); o += 16 * K
            OT = at("aO", 4096, F32, o); o += 16 * K
            QK = at("aQK", 2048, F32, o); o += 8 * K
            L = at("aL", 1024, F32, o); o += 4 * K
            P = at("aP", 1024, F32, o); o += 4 * K
            PT = at("aPT", 1024, F32, o); o += 4 * K
            NB = at("aNB", 1024, F32, o); o += 4 * K
            OH = at("aOH", 4096, F32R, o); o += 16 * K
            OL = at("aOL", 4096, F32R, o); o += 16 * K
            FZ = at("aFZ", 2560, F32, o, 16); o += 10 * K
            MX = at("aMX", 64, F32, o); o += 256
            NM = at("aNM", 64, F32, o); o += 256
            SU = at("aSU", 64, F32, o); o += 256
            RC = at("aRC", 64, F32, o); o += 256
            start = marks()
            (fb, ft), = lin_fm([("f", 0)], XHk, XLk, XTk, widths=(16,))
            z, e1, l1, c1, n1 = (FZ[:, 512 * i:512 * i + 512] for i in range(5))
            d = DV.op(lambda e: e.tensor_scalar(z, PS[fb][0:16, :], col("bf")[0:16, :], None, ALU.add), ft, start)
            free[fb] = d
            a = AC.op(lambda e: e.activation(e1, z, ACT.Abs), d)
            a = AC.op(lambda e: e.activation(e1, e1, ACT.Exp, scale=-1.0), a)
            a = AC.op(lambda e: e.activation(l1, e1, ACT.Ln, bias=1.0), a)
            d = DV.op(lambda e: e.tensor_scalar(z, z, 0.0, None, ALU.min), a)
            d = DV.op(lambda e: e.tensor_tensor(z, z, l1, ALU.subtract))
            d = DV.op(lambda e: e.tensor_tensor_scan(c1, ONE512[0:16, :], z, 0.0, ALU.mult, ALU.add))
            ncd = DV.op(lambda e: e.tensor_scalar(n1, c1, -8.0, None, ALU.mult))

            vtok = [None] * 4
            def vunit(i):
                def evac(c, ps, tok):
                    dst = V[:, 1024 * c + 256 * i:1024 * c + 256 * i + 256]
                    vtok[i] = AC.op(lambda e: e.activation(dst, ps[:, 0:256], ACT.Copy), tok)
                    return vtok[i]
                lin_tm(("av", i), XHk, XLk, XTk, evac)

            qkfree = [None, None]
            qktok = [None, None]
            def qkunit(hp):
                r = lin_fm([("aqk", hp)], XHk, XLk, XTk)
                s = hp % 2
                (b0, t0), (b1, t1) = r
                q, k = QK[:, 1024 * s:1024 * s + 512], QK[:, 1024 * s + 512:1024 * s + 1024]
                a = AC.op(lambda e: e.activation(q, PS[b0][:, :], ACT.Copy), t0, qkfree[s])
                d = DV.op(lambda e: e.tensor_copy(k, PS[b1][:, :]), t1, qkfree[s])
                free[b0], free[b1] = a, d
                qktok[s] = [a, d]

            nbfree = [None, None]
            nbt = [None, None]
            ptfree = [None, None]
            pfree = [None, None]
            lfree = [None, None]
            ohtok = [None] * 8
            state = {}
            units = {"q": 0, "v": 0}
            done = [0]

            def ap(t, h):
                s, r = (h // 2) % 2, slice(64 * (h % 2), 64 * (h % 2) + 64)
                return QK[r, 1024 * s + 512 * t:1024 * s + 512 * t + 512]

            def scores(it):
                h, i = it
                while units["q"] <= h // 2 or units["v"] <= h // 4:
                    yield
                if i == 0:
                    nb = blk(NB, h % 2)
                    tb = tbank()
                    t = mm(PS[tb][:, :], IDN[0:16, h:h + 1].to_broadcast([16, 128]), n1, True, True, free[tb], ncd, inc=True)
                    nbt[h % 2] = free[tb] = AC.op(lambda e: e.activation(nb, PS[tb][:, :], ACT.Copy), t, nbfree[h % 2])
                bank, kl, n = 2 + (4 * h + i) % 2, 128 * (i + 1), 4 * h + i
                mm(PS[bank][:, 0:kl], ap(0, h)[:, 128 * i:128 * i + 128], ap(1, h)[:, 0:kl], True, False,
                   free[bank], qktok[(h // 2) % 2])
                t = mm(PS[bank][:, 128 * i:kl], IDB, CAUS, False, True, CONST, inc=True)
                if i == 3:
                    qkfree[(h // 2) % 2] = t
                u = n % 2
                l, p, nb = blk(L, u)[:, 0:kl], blk(P, u), blk(NB, h % 2)
                mx, nm, su = MX[:, n:n + 1], NM[:, n:n + 1], SU[:, n:n + 1]
                d = DV.op(lambda e: e.tensor_tensor_reduce(
                    l, PS[bank][:, 0:kl], nb[:, 0:kl], 0.125, -3.0e38, ALU.add, ALU.max, mx), t, nbt[h % 2], lfree[u], start)
                free[bank] = nbfree[h % 2] = d
                d = DV.op(lambda e: e.tensor_scalar(nm, mx, -1.0, None, ALU.mult))
                state[n] = lfree[u] = AC.op(lambda e: e.activation(p[:, 0:kl], l, ACT.Exp, bias=nm, accum_out=su), d, pfree[u])
                yield

            def flip(it):
                h, i = it
                n, kl = 4 * h + i, 128 * (i + 1)
                u, tb = n % 2, tbank()
                p, pt = blk(P, u), blk(PT, u)
                for kb in range(i + 1):
                    t = tr(PS[tb][:, 128 * kb:128 * kb + 128], p[:, 128 * kb:128 * kb + 128], IDN,
                           state[n], free[tb], inc=(kb == i))
                pfree[u] = t
                if i % 2:
                    c = AC.op(lambda e: e.activation(pt[:, 0:kl], PS[tb][:, 0:kl], ACT.Copy), t, ptfree[u])
                else:
                    c = DV.op(lambda e: e.tensor_copy(pt[:, 0:kl], PS[tb][:, 0:kl]), t, ptfree[u])
                state[n] = free[tb] = c
                yield

            def values(it):
                h, i = it
                n = 4 * h + i
                pt, ob = blk(PT, n % 2), 6 + h % 2
                for kb in range(i + 1):
                    t = mm(PS[ob][:, 64 * i:64 * i + 64], pt[:, 128 * kb:128 * kb + 128],
                           V[:, 1024 * kb + 64 * h:1024 * kb + 64 * h + 64], kb == 0, kb == i,
                           state[n], free[ob], vtok[h // 4], inc=(kb == i))
                ptfree[n % 2] = t
                if i == 3:
                    rc = RC[:, 4 * h:4 * h + 4]
                    DV.op(lambda e: e.reciprocal(rc, SU[:, 4 * h:4 * h + 4]), AC.last())
                    dst = OT[:, :].rearrange("p (c n) -> p c n", c=4)[:, :, 64 * h:64 * h + 64]
                    d = DV.op(lambda e: e.tensor_tensor(dst, PS[ob][:, 0:256].rearrange("p (c n) -> p c n", c=4),
                                                        rc.unsqueeze(2).to_broadcast([128, 4, 64]), ALU.mult), t)
                    free[ob] = state["o"] = d
                    done[0] = h + 1
                yield

            def turn(it):
                h, i = it
                if h % 2 and i == 3:
                    j, tb = h // 2, tbank()
                    for c in range(4):
                        t = tr(PS[tb][:, 128 * c:128 * c + 128], OT[:, 1024 * c + 128 * j:1024 * c + 128 * j + 128], IDN,
                               free[tb], state["o"], inc=(c == 3))
                    free[tb] = ohtok[j] = split(PS[tb][:, :], blk(OH, j), blk(OL, j), t)
                    yield

            tbn = [0]

            def tbank():
                tbn[0] += 1
                return 4 + tbn[0] % 2

            lin_bank[1] = [0, 1]
            items = [(h, i) for h in range(16) for i in range(4)]
            vunit(0)
            units["v"] = 1
            alongside(staggered(items, [scores, flip, values, turn], LAGS), RATES[0])
            for kind, i in [("q", 0), ("q", 1), ("v", 1), ("q", 2), ("q", 3), ("v", 2), ("q", 4), ("q", 5), ("v", 3),
                            ("q", 6), ("q", 7)]:
                if kind == "q":
                    if i >= 2:
                        until(lambda: done[0] >= 2 * i - 2)
                    qkunit(i)
                else:
                    vunit(i)
                units[kind] = i + 1
            drain()
            lin_bank[1] = [0, 1, 2, 3, 4, 7]
            return (lambda k: blk(OH, k)), (lambda k: blk(OL, k)), (lambda k: ohtok[k]), o

        def attn_out(name, oh, ol, ot, g, b):
            nb = norm_bufs(R0)
            for i in range(4):
                for j, (bank, tok) in enumerate(lin_fm([(name, i)], oh, ol, ot)):
                    d = residual_tile(2 * i + j, bank, [tok, marks()] if i == 0 and j == 0 else tok)
                    acc_step(nb, 2 * i + j, blk(YH, 2 * i + j), d, True)
            layer_norm(nb, g, b)

        def ffn_up(names, conv, hh, hl, tmp, act_fn):
            htok = [None] * FF
            tfree = [None] * 2
            start = marks()
            for j in range(FF):
                (bg, tg), (bv, tv) = lin_fm([(names, j)], XHk, XLk, XTk, together=(j == 0))
                u = j % 2
                g, v = tmp[:, 1024 * u:1024 * u + 512], tmp[:, 1024 * u + 512:1024 * u + 1024]
                if conv is None:
                    a = AC.op(lambda e: e.activation(g, PS[bg][:, :], ACT.Silu), tg, tfree[u], start)
                    free[bg] = a
                    d = DV.op(lambda e: e.tensor_tensor(g, g, PS[bv][:, :], ALU.mult), a, tv)
                    free[bv] = d
                else:
                    for x, bank, tok, f in ((g, bg, tg, j), (v, bv, tv, FF + j)):
                        w = [col(f"cw{conv}{t}", f) for t in range(3)]
                        a = AC.op(lambda e, x=x, w=w, bank=bank, f=f: e.activation(
                            x, PS[bank][:, :], ACT.Identity, bias=col(f"cb{conv}", f), scale=w[2]), tok, tfree[u], start)
                        for t in (1, 2):
                            d = DV.op(lambda e, x=x, w=w, bank=bank, t=t: e.scalar_tensor_tensor(
                                out=x[:, t:512], in0=PS[bank][:, 0:512 - t], scalar=w[2 - t], in1=x[:, t:512],
                                op0=ALU.mult, op1=ALU.add), a)
                        free[bank] = d
                    a = AC.op(lambda e: e.activation(g, g, ACT.Silu), d)
                    d = PO.op(lambda e: e.tensor_tensor(g, g, v, ALU.mult), a, d)
                htok[j] = split(g, blk(hh, j), blk(hl, j), d)
                tfree[u] = htok[j]
            return htok

        def ffn_down(name, hh, hl, htok, evac):
            for i in range(4):
                r = lin_long([(name, i, p) for p in range(3)], lambda k: blk(hh, k), lambda k: blk(hl, k), lambda k: htok[k])
                for j, (bank, tok) in enumerate(r):
                    evac(2 * i + j, bank, tok)

        def ffn_layer(lay, g, b):
            hh = at(f"HH{lay}", 512 * FF, F32R, R0)
            hl = at(f"HL{lay}", 512 * FF, F32R, R0 + 44 * K)
            tmp = at(f"UT{lay}", 2048, F32, R0 + 88 * K)
            nb = norm_bufs(R0 + 88 * K)
            htok = ffn_up("up" + lay, int(lay), hh, hl, tmp, None)
            st = marks()
            nb["tok"] = st

            def evac(j, bank, tok):
                d = residual_tile(j, bank, [tok, st])
                acc_step(nb, j, blk(YH, j), d, True)
            ffn_down("dn" + lay, hh, hl, htok, evac)
            return nb

        def rotate(src, dst, rot, t1, cos, sin, tok, dfree, tfree, psum_bank=None):
            for a_, b_ in ((0, 32), (32, 0), (64, 96), (96, 64)):
                a = AC.op(lambda e, a_=a_, b_=b_: e.activation(rot[a_:a_ + 32, :], src[b_:b_ + 32, :], ACT.Copy), tok, tfree)
            d = DV.op(lambda e: e.tensor_tensor(t1, src, cos, ALU.mult), a, tfree)
            if psum_bank is not None:
                free[psum_bank] = d
            p = PO.op(lambda e: e.tensor_tensor(rot, rot, sin, ALU.mult), a)
            return PO.op(lambda e: e.tensor_tensor(dst, t1, rot, ALU.add), d, dfree)

        def diff():
            o = R0
            V = at("bV", 4096, F32, o); o += 16 * K
            OB = at("bO", 4096, F32, o); o += 16 * K
            QK = at("bQK", 2048, F32, o); o += 8 * K
            ROT = at("bROT", 2048, F32, o); o += 8 * K
            P = at("bP", 2048, F32, o); o += 8 * K
            PT = at("bPT", 1024, F32, o); o += 4 * K
            OH = at("bOH", 4096, F32R, o); o += 16 * K
            OL = at("bOL", 4096, F32R, o); o += 16 * K
            TT = at("bTT", 512, F32, o); o += 2 * K
            ST = at("bST", 512, F32, o); o += 2 * K
            start = marks()
            MX, NM, SU, RC = (ST[:, 64 * i:64 * i + 64] for i in range(4))
            MS = ST[:, 256:288]
            lt, lm = TN[:, 64:128], LAMT
            for i in range(2):
                DV.op(lambda e, i=i: e.tensor_tensor(lt, col("lam", 128 * i, 64), col("lam", 128 * i + 64, 64), ALU.mult))
                d = DV.op(lambda e, i=i: e.tensor_reduce(lm[:, i:i + 1], lt, AX, ALU.add))
            a = AC.op(lambda e: e.activation(lm[:, 2:4], lm[:, 0:2], ACT.Exp), d)
            d = DV.op(lambda e: e.tensor_tensor(lm[:, 4:5], lm[:, 2:3], lm[:, 3:4], ALU.subtract), a)
            d = DV.op(lambda e: e.tensor_scalar(lm[:, 5:6], lm[:, 4:5], LAM_INIT, None, ALU.add))
            gs = lm[:, 8:9]
            DV.op(lambda e: e.tensor_scalar(gs, col("subln"), 1.0 - LAM_INIT, None, ALU.mult))

            vtok = [None] * 4
            def vunit(i):
                def evac(c, ps, tok):
                    dst = V[:, 1024 * c + 256 * i:1024 * c + 256 * i + 256]
                    vtok[i] = AC.op(lambda e: e.activation(dst, ps[:, 0:256], ACT.Copy), tok, start)
                    return vtok[i]
                lin_tm(("bv", i), XHk, XLk, XTk, evac)

            qkfree, qktok, rfree = [None, None], [None, None], [None, None]
            def qkunit(h):
                s = h % 2
                r = lin_fm([("bqk", h)], XHk, XLk, XTk, together=(h == 0))
                toks = []
                for x, (bank, tok) in enumerate(r):
                    dst = QK[:, 1024 * s + 512 * x:1024 * s + 512 * x + 512]
                    rot, t1 = ROT[:, 1024 * x:1024 * x + 512], ROT[:, 1024 * x + 512:1024 * x + 1024]
                    p = rotate(PS[bank][:, :], dst, rot, t1, COSA, SINA, [tok, start], qkfree[s], rfree[x], bank)
                    rfree[x] = p
                    toks.append(p)
                qktok[s] = toks

            ptfree = [None, None]
            pfree = [None, None]
            ohtok = [None] * 8
            state = {}
            units = {"q": 0, "v": 0}
            done = [0]

            def scores(it):
                h, i = it
                while units["q"] <= h or units["v"] <= h // 2:
                    yield
                s, kl, n = h % 2, 128 * (i + 1), 4 * h + i
                u, c0 = n % 2, 2 * n
                st = []
                for m in range(2):
                    b, rows = 2 + 2 * u + m, slice(64 * m, 64 * m + 64)
                    q = QK[rows, 1024 * s + 128 * i:1024 * s + 128 * i + 128]
                    k = QK[rows, 1024 * s + 512:1024 * s + 512 + kl]
                    mm(PS[b][:, 0:kl], q, k, True, False, free[b], qktok[s])
                    st.append(mm(PS[b][:, 128 * i:kl], IDB, CHNK, False, True, CONST, inc=True))
                if i == 3:
                    qkfree[s] = st[1]
                for m in range(2):
                    b = 2 + 2 * u + m
                    DV.op(lambda e: e.tensor_reduce(MX[:, c0 + m:c0 + m + 1], PS[b][:, 0:kl], AX, ALU.max), st[m], start)
                d = DV.op(lambda e: e.tensor_scalar(NM[:, c0:c0 + 2], MX[:, c0:c0 + 2], -0.125, None, ALU.mult))
                for m in range(2):
                    b, p = 2 + 2 * u + m, P[:, 1024 * u + 512 * m:1024 * u + 512 * m + kl]
                    a = AC.op(lambda e: e.activation(
                        p, PS[b][:, 0:kl], ACT.Exp, bias=NM[:, c0 + m:c0 + m + 1], scale=0.125,
                        accum_out=SU[:, c0 + m:c0 + m + 1]), d, pfree[u])
                    free[b] = a
                state[n] = a
                yield

            def mix(it):
                h, i = it
                kl, n = 128 * (i + 1), 4 * h + i
                u, c0 = n % 2, 2 * n
                p1, p2 = P[:, 1024 * u:1024 * u + kl], P[:, 1024 * u + 512:1024 * u + 512 + kl]
                DV.op(lambda e: e.reciprocal(RC[:, c0:c0 + 2], SU[:, c0:c0 + 2]), state[n])
                DV.op(lambda e: e.tensor_scalar(p2, p2, RC[:, c0 + 1:c0 + 2], LAMT[:, 5:6], ALU.mult, ALU.mult))
                d = DV.op(lambda e: e.scalar_tensor_tensor(out=p1, in0=p1, scalar=RC[:, c0:c0 + 1], in1=p2,
                                                           op0=ALU.mult, op1=ALU.subtract))
                for kb in range(i + 1):
                    t = tr(PS[6][:, 128 * kb:128 * kb + 128], P[:, 1024 * u + 128 * kb:1024 * u + 128 * kb + 128], IDN,
                           d, free[6], inc=(kb == i))
                pfree[u] = t
                pt = blk(PT, u)
                if i % 2:
                    c = AC.op(lambda e: e.activation(pt[:, 0:kl], PS[6][:, 0:kl], ACT.Copy), t, ptfree[u])
                else:
                    c = DV.op(lambda e: e.tensor_copy(pt[:, 0:kl], PS[6][:, 0:kl]), t, ptfree[u])
                state[n] = free[6] = c
                yield

            def values(it):
                h, i = it
                n = 4 * h + i
                pt = blk(PT, n % 2)
                for kb in range(i + 1):
                    t = mm(PS[7][:, 128 * i:128 * i + 128], pt[:, 128 * kb:128 * kb + 128],
                           V[:, 1024 * kb + 128 * h:1024 * kb + 128 * h + 128], kb == 0, kb == i,
                           state[n], free[7], vtok[h // 2], inc=(kb == i))
                ptfree[n % 2] = t
                if i == 3:
                    ob = OB[:, :].rearrange("p (c n) -> p c n", c=4)[:, :, 128 * h:128 * h + 128]
                    a = AC.op(lambda e: e.activation(ob, PS[7][:, :].rearrange("p (c n) -> p c n", c=4), ACT.Copy), t, start)
                    free[7] = a
                    tt = TT[:, :].rearrange("p (c n) -> p c n", c=4)
                    DV.op(lambda e: e.tensor_tensor(tt, ob, ob, ALU.mult), a, ohtok[h - 1] if h else None)
                    state["o", h] = DV.op(lambda e: e.tensor_reduce(MS[:, 4 * h:4 * h + 4], tt, AX, ALU.add))
                    done[0] = h + 1
                yield

            def turns(h0, h1):
                ms = MS[:, 4 * h0:4 * h1]
                a = AC.op(lambda e: e.activation(ms, ms, ACT.Sqrt, bias=EPS5, scale=1.0 / 128), state["o", h1 - 1])
                d = DV.op(lambda e: e.reciprocal(ms, ms), a)
                for h in range(h0, h1):
                    for c in range(4):
                        x = OB[:, 1024 * c + 128 * h:1024 * c + 128 * h + 128]
                        d = DV.op(lambda e: e.tensor_scalar(x, x, MS[:, 4 * h + c:4 * h + c + 1], None, ALU.mult))
                    for c in range(4):
                        t = tr(PS[6][:, 128 * c:128 * c + 128], OB[:, 1024 * c + 128 * h:1024 * c + 128 * h + 128], IDN,
                               free[6], d, inc=(c == 3))
                    f = DV.op(lambda e: e.tensor_scalar(TT[:, :], PS[6][:, :], gs, None, ALU.mult), t, ohtok[h - 1] if h else None)
                    free[6] = f
                    ohtok[h] = split(TT[:, :], blk(OH, h), blk(OL, h), f)
                    yield

            def turn(it):
                if it in ((3, 3), (7, 3)):
                    yield from turns(it[0] - 3, it[0] + 1)

            lin_bank[1] = [0, 1]
            items = [(h, i) for h in range(8) for i in range(4)]
            qkunit(0)
            units["q"] = 1
            alongside(staggered(items, [scores, mix, values, turn], LAGS), RATES[1])
            for kind, i in [("v", 0), ("q", 1), ("v", 1), ("q", 2), ("q", 3), ("v", 2), ("q", 4), ("q", 5), ("v", 3),
                            ("q", 6), ("q", 7)]:
                if kind == "q":
                    if i >= 2:
                        until(lambda: done[0] >= i - 1)
                    qkunit(i)
                else:
                    vunit(i)
                units[kind] = i + 1
            drain()
            lin_bank[1] = [0, 1, 2, 3, 4, 7]
            return (lambda k: blk(OH, k)), (lambda k: blk(OL, k)), (lambda k: ohtok[k]), o

        def rms_apply(nb, src, tok, gain):
            r = stats(nb, EPS6, False)
            ts = [nb[n][:, :] for n in ("T1", "T2", "RS")]
            tfree = [None] * 3
            for j in range(8):
                t = ts[j % 3]
                free[6] = d = DV.op(lambda e: e.scalar_tensor_tensor(
                    out=t, in0=blk(src, j), scalar=col(gain, j), in1=PS[6][:, :], op0=ALU.mult, op1=ALU.mult),
                    r, tfree[j % 3], marks() if j == 0 else None)
                tfree[j % 3] = xtok[j] = split(t, blk(XH, j), blk(XL, j), d, rest=PO)

        def second(XR, nb0):
            O0 = R0 + 16 * K
            rms_apply(nb0, XR, None, "n1pre")
            o = O0
            OTH = at("cOTH", 2048, F32R, o); o += 8 * K
            OTL = at("cOTL", 2048, F32R, o); o += 8 * K
            DT = at("cDT", 128, F32, o); o += 512
            ADT = at("cADT", 128, F32, o); o += 512
            ACS = at("cACS", 128, F32, o); o += 512
            NAC = at("cNAC", 128, F32, o); o += 512
            EAC = at("cEAC", 128, F32, o); o += 512
            TOT = at("cTOT", 128, F32, o); o += 512
            DSD = at("cDSD", 128, F32, o); o += 512
            CD = at("cCD", 128, F32, o); o += 512
            EA = at("cEA", 32, F32, o); o += 128
            SS = at("cSS", 32, F32, o); o += 128
            E0 = o
            QQ = at("cQ", 2560, F32, o); o += 10 * K
            V = at("cV", 512, F32, o); o += 2 * K
            OT = at("cO", 2048, F32, o); o += 8 * K
            P = at("cP", 1024, F32, o); o += 4 * K
            PT = at("cPT", 1024, F32, o); o += 4 * K
            ROT = at("cROT", 2560, F32, o); o += 10 * K
            ST = at("cST", 128, F32, o); o += 512
            start = marks()
            MX, NM, SU, RC = (ST[:, 32 * i:32 * i + 32] for i in range(4))
            vt = []

            def evac(c, ps, tok):
                a = AC.op(lambda e: e.activation(V[:, 128 * c:128 * c + 128], ps[:, 0:128], ACT.Copy), tok, start)
                d = DV.op(lambda e: e.tensor_tensor(DT[:, 32 * c:32 * c + 32], ps[:, 128:160], col("dtb", 0, 32), ALU.add), a)
                vt.append(a)
                return d
            SQ5, qt = ROT, [None] * 5
            sqt = []

            def qk_units(key, n0, widths=(128, 128), together=False):
                for j, (bank, tok) in enumerate(lin_fm([key], XHk, XLk, XTk, widths=widths, together=together)):
                    n = n0 + j
                    a = AC.op(lambda e: e.activation(blk(SQ5, n), PS[bank][:, :], ACT.Square), tok, start)
                    sqt.append(a)
                    free[bank] = DV.op(lambda e: e.tensor_copy(blk(QQ, n), PS[bank][:, :]), tok, a)
            qk_units(("cq", 0), 0, together=True)
            lin_tm(("cv", 0), XHk, XLk, XTk, evac)
            qk_units(("cq", 1), 2)
            qk_units(("ck", 0), 4, (128,))
            dtraw = vt[-1:] + [DV.last()]
            acs = {}

            def prep():
                for n in range(5):
                    for c in range(4):
                        m = mm(PS[6][:, 8 * n + 2 * c:8 * n + 2 * c + 2], SQ5[:, 512 * n + 128 * c:512 * n + 128 * c + 128],
                               BLK[:, 0:65:64], True, True, sqt, free[6], inc=(c == 3))
                rs = TN[:, 48:88]
                a = AC.op(lambda e: e.activation(rs, PS[6][:, 0:40], ACT.Sqrt, bias=EPS6), m)
                d = DV.op(lambda e: e.reciprocal(rs, rs), a)
                free[6] = a
                yield
                rfree = [m, m]
                for n in (4, 0, 1, 2, 3):
                    u, q = n % 2, blk(QQ, n)
                    b = 5 + u
                    rot, t1 = ROT[:, 1024 * u:1024 * u + 512], ROT[:, 1024 * u + 512:1024 * u + 1024]
                    for c in range(4):
                        for i in range(2):
                            r = rs[:, 8 * n + 2 * c + i:8 * n + 2 * c + i + 1].to_broadcast([128, 64])
                            t = mm(PS[b][64 * i:64 * i + 64, 128 * c:128 * c + 128], r, IDN, True, True, d, free[b],
                                   inc=(c == 3 and i == 1))
                    x = free[b] = DV.op(lambda e: e.scalar_tensor_tensor(
                        out=q, in0=q, scalar=col("kn" if n == 4 else "qn"), in1=PS[b][:, :], op0=ALU.mult, op1=ALU.mult), t)
                    qt[n] = rfree[u] = rotate(q, q, rot, t1, COSB, SINB, x, None, rfree[u])
                    yield
                a = AC.op(lambda e: e.activation(ADT[:, :], DT[:, :], ACT.Abs), dtraw)
                a = AC.op(lambda e: e.activation(ADT[:, :], ADT[:, :], ACT.Exp, scale=-1.0))
                a = AC.op(lambda e: e.activation(ADT[:, :], ADT[:, :], ACT.Ln, bias=1.0))
                a = AC.op(lambda e: e.activation(EA[:, :], col("alog", 0, 32), ACT.Exp))
                DV.op(lambda e: e.tensor_scalar(DT[:, :], DT[:, :], 0.0, None, ALU.max), a)
                DV.op(lambda e: e.tensor_tensor(DT[:, :], DT[:, :], ADT[:, :], ALU.add))
                v3 = lambda t: t[:, :].rearrange("p (c n) -> p c n", c=4)
                DV.op(lambda e: e.tensor_tensor(v3(ADT), v3(DT), EA[:, :].unsqueeze(1).to_broadcast([128, 4, 32]), ALU.mult))
                dtd = DV.op(lambda e: e.tensor_scalar(ADT[:, :], ADT[:, :], -1.0, None, ALU.mult))
                yield
                for c in range(4):
                    mm(PS[5][:, 32 * c:32 * c + 16], UPP, ADT[:, 32 * c:32 * c + 16], True, True, dtd, free[5])
                    mm(PS[5][:, 32 * c + 16:32 * c + 32], LOW, ADT[:, 32 * c + 16:32 * c + 32], True, True)
                for c in range(4):
                    t = mm(PS[5][:, 128 + 32 * c:160 + 32 * c], ONE, ADT[:, 32 * c:32 * c + 32], True, True, inc=(c == 3))
                DV.op(lambda e: e.tensor_copy(ACS[:, :], PS[5][:, 0:128]), t)
                acs["nac"] = DV.op(lambda e: e.tensor_scalar(NAC[:, :], ACS[:, :], -1.0, None, ALU.mult))
                free[5] = DV.op(lambda e: e.tensor_copy(TOT[:, :], PS[5][:, 128:256]))
                d = DV.op(lambda e: e.tensor_tensor(DSD[:, :], TOT[:, :], ACS[:, :], ALU.subtract))
                AC.op(lambda e: e.activation(DSD[:, :], DSD[:, :], ACT.Exp), d)
                AC.op(lambda e: e.activation(EAC[:, :], ACS[:, :], ACT.Exp))
                a = AC.op(lambda e: e.activation(CD[:, :], TOT[:, :], ACT.Exp))
                acs["dec"] = DV.op(lambda e: e.tensor_tensor(DSD[:, :], DSD[:, :], DT[:, :], ALU.mult), a)
                yield

            pfree, ptfree = [None, None], [None, None]
            ohtok = [None] * 4
            state = {}

            def scores(it):
                h, i = it
                n, rows = 4 * h + i, slice(64 * (h // 4), 64 * (h // 4) + 64)
                u, bank = n % 2, 2 + n % 2
                q, k = QQ[rows, 512 * (h % 4) + 128 * i:512 * (h % 4) + 128 * i + 128], QQ[rows, 2048:2560]
                t = mm(PS[bank][:, :], q, k, True, True, free[bank], qt[h % 4], qt[4], inc=True)
                DV.op(lambda e: e.tensor_reduce(MX[:, n:n + 1], PS[bank][:, :], AX, ALU.max), t, start)
                d = DV.op(lambda e: e.tensor_scalar(NM[:, n:n + 1], MX[:, n:n + 1], -0.125, None, ALU.mult))
                state[n] = free[bank] = AC.op(lambda e: e.activation(
                    blk(P, u), PS[bank][:, :], ACT.Exp, bias=NM[:, n:n + 1], scale=0.125, accum_out=SU[:, n:n + 1]), d, pfree[u])
                yield

            def flip(it):
                h, i = it
                n = 4 * h + i
                u, tb = n % 2, 4 + n % 2
                p, pt = blk(P, u), blk(PT, u)
                for kb in range(4):
                    t = tr(PS[tb][:, 128 * kb:128 * kb + 128], p[:, 128 * kb:128 * kb + 128], IDN, state[n], free[tb], inc=(kb == 3))
                pfree[u] = t
                if i % 4:
                    c = AC.op(lambda e: e.activation(pt, PS[tb][:, :], ACT.Copy), t, ptfree[u])
                else:
                    c = DV.op(lambda e: e.tensor_copy(pt, PS[tb][:, :]), t, ptfree[u])
                state[n] = free[tb] = c
                yield

            def values(it):
                h, i = it
                n, kv = 4 * h + i, h // 4
                pt = blk(PT, n % 2)
                for kb in range(4):
                    t = mm(PS[7][:, 64 * i:64 * i + 64], pt[:, 128 * kb:128 * kb + 128],
                           V[:, 128 * kb + 64 * kv:128 * kb + 64 * kv + 64], kb == 0, kb == 3, state[n], free[7], vt, inc=(kb == 3))
                ptfree[n % 2] = t
                if i == 3:
                    rc = RC[:, 4 * h:4 * h + 4]
                    DV.op(lambda e: e.reciprocal(rc, SU[:, 4 * h:4 * h + 4]), AC.last())
                    dst = OT[:, :].rearrange("p (c n) -> p c n", c=4)[:, :, 64 * h:64 * h + 64]
                    d = DV.op(lambda e: e.tensor_tensor(dst, PS[7][:, 0:256].rearrange("p (c n) -> p c n", c=4),
                                                        rc.unsqueeze(2).to_broadcast([128, 4, 64]), ALU.mult), t)
                    free[7] = state["o"] = d
                yield

            def turn(it):
                h, i = it
                if h % 2 and i == 3:
                    j = h // 2
                    for c in range(4):
                        t = tr(PS[6][:, 128 * c:128 * c + 128], OT[:, 512 * c + 128 * j:512 * c + 128 * j + 128], IDN,
                               free[6], state["o"], inc=(c == 3))
                    free[6] = ohtok[j] = split(PS[6][:, :], blk(OTH, j), blk(OTL, j), t)
                    yield

            o2 = o
            BC = at("cBC", 2048, F32, o2); o2 += 8 * K
            BT = at("cBT", 1024, F32, o2); o2 += 4 * K
            XS = at("cXS", 4096, F32, o2); o2 += 16 * K
            CVT = at("cCVT", 1024, F32, o2); o2 += 4 * K
            CTH = FP[:, 1152:2176]
            thfree = [None, None]
            hw, hn = sm["sw0"][0], 72
            DV.op(lambda e: e.tensor_scalar(SM[:, hw:hw + hn], SM[:, hw:hw + hn], 0.5, None, ALU.mult))
            sizes["mid"] = o2
            cfree = [None, None]
            xst = [None] * 8
            bct = [None] * 4
            btt = [None] * 2

            CU = [FP[:, 2176:2688], FP[:, 2688:3200]]
            cufree = [None, None]
            turns = []

            def xbc(i):
                r = lin_fm([("cx", i)], XHk, XLk, XTk)
                while turns:
                    xturn(*turns.pop(0))
                for jj, (bank, tok) in enumerate(r):
                    j = 2 * i + jj
                    u, y = CU[j % 2], blk(CVT, j % 2)
                    a = AC.op(lambda e: e.activation(u, PS[bank][:, :], ACT.Copy), tok, cufree[j % 2], qt)
                    free[bank] = a
                    a = AC.op(lambda e: e.activation(y, u, ACT.Identity, bias=col("sb", j), scale=col("sw2", j)), cfree[j % 2], start)
                    for t in (0, 1, 3, 4):
                        s = t - 2
                        oa, ob_ = max(0, -s), 512 - max(0, s)
                        d = DV.op(lambda e, t=t, s=s, oa=oa, ob_=ob_: e.scalar_tensor_tensor(
                            out=y[:, oa:ob_], in0=u[:, oa + s:ob_ + s], scalar=col(f"sw{t}", j), in1=y[:, oa:ob_],
                            op0=ALU.mult, op1=ALU.add), a)
                    cufree[j % 2] = d
                    th = blk(CTH, j % 2)
                    a = AC.op(lambda e: e.activation(th, y, ACT.Tanh), d, thfree[j % 2])
                    src = y if j < 8 else blk(BC, j - 8)
                    a = thfree[j % 2] = DV.op(lambda e: e.scalar_tensor_tensor(
                        out=src, in0=th, scalar=1.0, in1=y, op0=ALU.add, op1=ALU.mult), a)
                    if j >= 8:
                        cfree[j % 2] = bct[j - 8] = a
                    if j < 10:
                        turns.append((j, src, a))

            def xturn(j, src, a):
                for c in range(4):
                    t = tr(PS[6][:, 128 * c:128 * c + 128], src[:, 128 * c:128 * c + 128], IDN, a, free[6], inc=(c == 3))
                if j < 8:
                    cfree[j % 2] = t
                    dst = XS[:, :].rearrange("p (c n) -> p c n", c=4)[:, :, 128 * j:128 * j + 128]
                else:
                    dst = BT[:, :].rearrange("p (c n) -> p c n", c=4)[:, :, 128 * (j - 8):128 * (j - 8) + 128]
                f = AC.op(lambda e: e.activation(dst, PS[6][:, :].rearrange("p (c n) -> p c n", c=4), ACT.Copy), t, start)
                free[6] = f
                if j < 8:
                    xst[j] = f
                else:
                    btt[j - 8] = f

            lin_bank[1] = [0, 1]

            def attention():
                yield from prep()
                yield from staggered([(h, i) for h in range(8) for i in range(4)], [scores, flip, values, turn], LAGS)
            alongside(attention(), RATES[2])
            for i in range(6):
                xbc(i)
            drain()

            start2 = marks()
            o = E0
            Y = at("cY", 4096, F32, o); o += 16 * K
            CB = at("cCB", 1024, F32, o); o += 4 * K
            RF = at("cRF", 1024, F32, o, 16); o += 4 * K
            EM = at("cEM", 2048, F32, o); o += 8 * K
            XD = at("cXD", 1024, F32, o); o += 4 * K
            assert o <= E0 + 36 * K
            o = o2 - 4 * K
            PRV = FP[:, 1152:3200]
            XW = at("cXW", 1024, F32, o); o += 4 * K
            YT_ = at("cYT", 512, F32, E0 + 36 * K)
            sizes["ssd"] = o

            nacd, dec = acs["nac"], acs["dec"]
            for dr in range(2):
                for c in range(4):
                    t = tr(PS[4 + dr][0:16, 128 * c:128 * c + 128], ACS[:, 32 * c + 16 * dr:32 * c + 16 * dr + 16], IDN,
                           nacd, free[4 + dr], start2, inc=(c == 3))
                rfd = DV.op(lambda e, dr=dr: e.tensor_copy(RF[:, 512 * dr:512 * dr + 512], PS[4 + dr][0:16, :]), t)
                free[4 + dr] = rfd
            for g in range(2):
                for c in range(4):
                    s = slice(512 * g + 128 * c, 512 * g + 128 * c + 128)
                    s2 = slice(1024 + 512 * g + 128 * c, 1024 + 512 * g + 128 * c + 128)
                    t = mm(PS[6][:, 128 * c:128 * c + 128], BC[:, s], BC[:, s2], True, True, bct, free[6], inc=(c == 3))
                cbd = DV.op(lambda e, g=g: e.tensor_copy(blk(CB, g), PS[6][:, :]), t)
                free[6] = cbd
            yv = Y[:, :].rearrange("p (c n) -> p c n", c=4)
            for c in range(4):
                src = XS[:, 1024 * c:1024 * c + 1024].rearrange("p (h n) -> p h n", h=16)
                dst = Y[:, 1024 * c:1024 * c + 1024].rearrange("p (h n) -> p h n", h=16)
                yt0 = PO.op(lambda e, src=src, dst=dst: e.tensor_tensor(
                    dst, src, col("dskip", 0, 16).unsqueeze(2).to_broadcast([128, 16, 64]), ALU.mult), xst, start2)

            emfree = [None, None]
            xdfree = [None, None]

            def shead(h):
                g, u = h // 8, h % 2
                em = [EM[:, 1024 * u + 512 * dr:1024 * u + 512 * dr + 512] for dr in range(2)]
                xd = [XD[:, 512 * u + 256 * dr:512 * u + 256 * dr + 256] for dr in range(2)]
                mt = []
                for dr in range(2):
                    bank = 2 + dr + 2 * u
                    mm(PS[bank][:, :], IDN[0:16, h:h + 1].to_broadcast([16, 128]), RF[:, 512 * dr:512 * dr + 512], True, False,
                       rfd, free[bank])
                    t = mm(PS[bank][:, :], IDB, MF if dr == 0 else MB, False, True, inc=True)
                    for c in range(4):
                        n = 32 * c + 16 * dr + h
                        a = AC.op(lambda e, c=c, n=n, dr=dr, bank=bank: e.activation(
                            em[dr][:, 128 * c:128 * c + 128], PS[bank][:, 128 * c:128 * c + 128], ACT.Exp,
                            bias=NAC[:, n:n + 1]), t, nacd, emfree[u])
                    free[bank] = a
                    DV.op(lambda e, dr=dr: e.tensor_tensor(em[dr], em[dr], blk(CB, g), ALU.mult), a)
                    xs = XS[:, :].rearrange("p (c n) -> p c n", c=4)[:, :, 64 * h:64 * h + 64]
                    dt = DT[:, :].rearrange("p (c n) -> p c n", c=4)[:, :, 16 * dr + h:16 * dr + h + 1]
                    mt.append(DV.op(lambda e, dr=dr, xs=xs, dt=dt: e.tensor_tensor(
                        xd[dr].rearrange("p (c n) -> p c n", c=4), xs, dt.to_broadcast([128, 4, 64]), ALU.mult),
                        xst, xdfree[u], start2))
                state["m", h] = mt
                yield

            def syvals(h):
                u = h % 2
                em = [EM[:, 1024 * u + 512 * dr:1024 * u + 512 * dr + 512] for dr in range(2)]
                xd = [XD[:, 512 * u + 256 * dr:512 * u + 256 * dr + 256] for dr in range(2)]
                mt = state["m", h]
                for c in range(4):
                    for dr in range(2):
                        t = mm(PS[7][:, 64 * c:64 * c + 64], em[dr][:, 128 * c:128 * c + 128], xd[dr][:, 64 * c:64 * c + 64],
                               dr == 0, dr == 1, mt, free[7], inc=(c == 3 and dr == 1))
                emfree[u] = xdfree[u] = t
                dst = yv[:, :, 64 * h:64 * h + 64]
                d = DV.op(lambda e: e.tensor_tensor(dst, PS[7][:, 0:256].rearrange("p (c n) -> p c n", c=4), dst, ALU.add), t, yt0)
                free[7] = d
                sdone[0] = h + 1
                yield

            sdone = [0]

            def states():
                prv_t = [None, None]
                xwfree = [None, None]
                for dr in range(2):
                    cs = (0, 1, 2, 3) if dr == 0 else (3, 2, 1, 0)
                    for idx, c in enumerate(cs):
                        if idx:
                            for g in range(2):
                                b = pick()
                                t = mm(PS[b][:, :], BC[:, 1024 + 512 * g + 128 * c:1024 + 512 * g + 128 * c + 128],
                                       PRV[:, 1024 * dr + 512 * g:1024 * dr + 512 * g + 512], True, True,
                                       free[b], bct, prv_t[dr], inc=True)
                                sc = EAC[:, 32 * c + 16 * dr + 8 * g:32 * c + 16 * dr + 8 * g + 8]
                                tmp = YT_[:, :]
                                d = DV.op(lambda e, b=b, sc=sc, tmp=tmp: e.tensor_tensor(
                                    tmp.rearrange("p (h n) -> p h n", h=8), PS[b][:, :].rearrange("p (h n) -> p h n", h=8),
                                    sc.unsqueeze(2).to_broadcast([128, 8, 64]), ALU.mult), t, dec, start2)
                                free[b] = d
                                dst = Y[:, 1024 * c + 512 * g:1024 * c + 512 * g + 512]
                                d = DV.op(lambda e, dst=dst, tmp=tmp: e.tensor_tensor(dst, dst, tmp, ALU.add), yt0)
                            yield
                        if idx < 3:
                            for g in range(2):
                                b = pick()
                                xw = blk(XW, g)
                                sc = DSD[:, 32 * c + 16 * dr + 8 * g:32 * c + 16 * dr + 8 * g + 8]
                                p = PO.op(lambda e, xw=xw, sc=sc, c=c, g=g: e.tensor_tensor(
                                    xw.rearrange("p (h n) -> p h n", h=8),
                                    XS[:, 1024 * c + 512 * g:1024 * c + 512 * g + 512].rearrange("p (h n) -> p h n", h=8),
                                    sc.unsqueeze(2).to_broadcast([128, 8, 64]), ALU.mult), dec, xst, xwfree[g], start2)
                                t = mm(PS[b][:, :], BT[:, 256 * c + 128 * g:256 * c + 128 * g + 128], xw, True, True,
                                       free[b], p, btt, inc=True)
                                xwfree[g] = t
                                pv = PRV[:, 1024 * dr + 512 * g:1024 * dr + 512 * g + 512]
                                if idx == 0:
                                    d = DV.op(lambda e, pv=pv, b=b: e.tensor_copy(pv, PS[b][:, :]), t, start2)
                                else:
                                    cd = CD[:, 32 * c + 16 * dr + 8 * g:32 * c + 16 * dr + 8 * g + 8]
                                    DV.op(lambda e, pv=pv, cd=cd: e.tensor_tensor(
                                        pv.rearrange("p (h n) -> p h n", h=8), pv.rearrange("p (h n) -> p h n", h=8),
                                        cd.unsqueeze(2).to_broadcast([128, 8, 64]), ALU.mult), PE.last())
                                    d = DV.op(lambda e, pv=pv, b=b: e.tensor_tensor(pv, pv, PS[b][:, :], ALU.add), t)
                                free[b] = d
                            prv_t[dr] = d
                            yield

            def scans():
                left = states()
                for _ in staggered(list(range(16)), [shead, syvals], [0, 2]):
                    yield
                    for _ in range(2):
                        next(left, None)
            alongside(scans(), RATES[3])
            until(lambda: sdone[0] >= 4)
            for i in range(4):
                def evac(c, ps, tok):
                    if c == 0:
                        until(lambda: sdone[0] >= 4 * i + 4)
                    z, z2 = XW[:, 512 * (c % 2):512 * (c % 2) + 256], XW[:, 512 * (c % 2) + 256:512 * (c % 2) + 512]
                    y = Y[:, 1024 * c + 256 * i:1024 * c + 256 * i + 256]
                    a = AC.op(lambda e: e.activation(z, ps[:, 0:256], ACT.Tanh, scale=0.5), tok, zfree[c % 2], z0)
                    d = DV.op(lambda e: e.scalar_tensor_tensor(out=z2, in0=z, scalar=1.0, in1=ps[:, 0:256],
                                                               op0=ALU.add, op1=ALU.mult), a)
                    zfree[c % 2] = DV.op(lambda e: e.tensor_tensor(y, y, z2, ALU.mult), d)
                    return d
                zfree, z0 = [None, None], marks()
                lin_tm(("cz", i), XHk, XLk, XTk, evac)
            drain()
            lin_bank[1] = [0, 1, 2, 3, 4, 7]
            st = marks()
            for c in range(4):
                a = AC.op(lambda e, c=c: e.activation(XS[:, 0:1024], Y[:, 1024 * c:1024 * c + 1024], ACT.Square,
                                                      accum_out=SS[:, c:c + 1]), st)
            a = AC.op(lambda e: e.activation(SS[:, 4:8], SS[:, 0:4], ACT.Sqrt, bias=EPS6, scale=0.25 / D))
            d = DV.op(lambda e: e.reciprocal(SS[:, 8:12], SS[:, 4:8]), a)
            for c in range(4):
                d = DV.op(lambda e, c=c: e.tensor_scalar(Y[:, 1024 * c:1024 * c + 1024], Y[:, 1024 * c:1024 * c + 1024],
                                                         SS[:, 8 + c:9 + c], 0.5, ALU.mult, ALU.mult))
            st = marks()
            yo = E0 + 16 * K
            YTH = at("cYTH", 4096, F32R, yo)
            YTL = at("cYTL", 4096, F32R, yo + 16 * K)
            TT = at("cTT", 1024, F32, yo + 32 * K)
            ytt = [None] * 8
            for j in range(8):
                b = pick()
                for c in range(4):
                    t = tr(PS[b][:, 128 * c:128 * c + 128], Y[:, 1024 * c + 128 * j:1024 * c + 128 * j + 128], IDN,
                           free[b], st, inc=(c == 3))
                tt = blk(TT, j % 2)
                f = DV.op(lambda e: e.tensor_scalar(tt, PS[b][:, :], col("ssdn", j), None, ALU.mult), t, ytt[j - 2] if j > 1 else None, st)
                free[b] = f
                ytt[j] = split(tt, blk(YTH, j), blk(YTL, j), f)
            MIXH = at("cMXH", 4096, F32R, yo + 36 * K)
            MIXL = at("cMXL", 4096, F32R, E0)
            SG = FP[:, 1152:3200]
            sizes["mix"] = yo + 60 * K
            st = marks()
            st2 = [st]
            mtok = [None] * 8
            sgf = [None, None]
            for i in range(4):
                ga = lin_fm([("cga", i)], XHk, XLk, XTk)
                ta = []
                for j, (bank, tok) in enumerate(ga):
                    x = SG[:, 1024 * j:1024 * j + 512]
                    a = AC.op(lambda e: e.activation(x, PS[bank][:, :], ACT.Sigmoid), tok, sgf[j], st)
                    free[bank] = a
                    ta.append(a)
                pa = lin_fm([("cpa", i)], lambda k: blk(OTH, k), lambda k: blk(OTL, k), lambda k: ohtok[k])
                for j, (bank, tok) in enumerate(pa):
                    x = SG[:, 1024 * j:1024 * j + 512]
                    d = DV.op(lambda e: e.tensor_tensor(x, x, PS[bank][:, :], ALU.mult), tok, ta)
                    free[bank] = d
                gsr = lin_fm([("cgs", i)], XHk, XLk, XTk)
                tb = []
                for j, (bank, tok) in enumerate(gsr):
                    x = SG[:, 1024 * j + 512:1024 * j + 1024]
                    a = AC.op(lambda e: e.activation(x, PS[bank][:, :], ACT.Sigmoid), tok, sgf[j])
                    free[bank] = a
                    tb.append(a)
                psr = lin_fm([("cps", i)], lambda k: blk(YTH, k), lambda k: blk(YTL, k), lambda k: ytt[k])
                for j, (bank, tok) in enumerate(psr):
                    x, x2 = SG[:, 1024 * j:1024 * j + 512], SG[:, 1024 * j + 512:1024 * j + 1024]
                    d = DV.op(lambda e: e.tensor_tensor(x2, x2, PS[bank][:, :], ALU.mult), tok, tb)
                    free[bank] = d
                    p = PO.op(lambda e: e.tensor_tensor(x, x, x2, ALU.add), d)
                    sgf[j] = mtok[2 * i + j] = split(x, blk(MIXH, 2 * i + j), blk(MIXL, 2 * i + j), p)
            st = marks()
            nb = norm_bufs(yo)
            nb["tok"] = st

            def evac_y(j, bank, tok, first):
                y = blk(YH, j)
                a = AC.op(lambda e: e.activation(y, PS[bank][:, :], ACT.Copy), tok, first)
                free[bank] = a
                acc_step(nb, j, y, a, False)
            for i in range(4):
                for j, (bank, tok) in enumerate(lin_fm([("co", i)], lambda k: blk(MIXH, k), lambda k: blk(MIXL, k), lambda k: mtok[k])):
                    evac_y(2 * i + j, bank, tok, st)
            r = stats(nb, EPS6, False)
            nb2 = norm_bufs(yo + 14 * K)
            nb2["tok"] = st
            for j in range(8):
                y, x = blk(YH, j), blk(XR, j)
                DV.op(lambda e: e.scalar_tensor_tensor(out=y, in0=y, scalar=col("n1post", j), in1=PS[6][:, :],
                                                       op0=ALU.mult, op1=ALU.mult), r)
                free[6] = d = DV.op(lambda e: e.tensor_tensor(x, x, y, ALU.add))
                acc_step(nb2, j, x, d, False)
            rms_apply(nb2, XR, None, "n2pre")
            st = marks()
            hh = at("HH2", 512 * FF, F32R, O0)
            hl = at("HL2", 512 * FF, F32R, O0 + 44 * K)
            tmp = FP[:, 1152:3200]
            htok = ffn_up_2(hh, hl, tmp, st)
            nb = {n: FP[:, 1152 + 512 * i:1664 + 512 * i] for i, n in enumerate(("SQ", "A1", "A2"))}
            st = marks()
            nb["tok"] = st

            def evac(j, bank, tok):
                y = blk(YH, j)
                a = AC.op(lambda e: e.activation(y, PS[bank][:, :], ACT.Copy), tok, st)
                free[bank] = a
                acc_step(nb, j, y, a, False)
            ffn_down("dn2", hh, hl, htok, evac)
            r = stats(nb, EPS6, False)
            outs = []
            for j in range(8):
                y, x = blk(YH, j), blk(XR, j)
                DV.op(lambda e: e.scalar_tensor_tensor(out=y, in0=y, scalar=col("n2post", j), in1=PS[6][:, :],
                                                       op0=ALU.mult, op1=ALU.mult), r)
                d = DV.op(lambda e: e.tensor_tensor(x, x, y, ALU.add))
                sp(lambda e, j=j, x=x: e.dma_start(outT[:, 512 * j:512 * j + 512], x).then_inc(s_out, 16), d)

        def ffn_up_2(hh, hl, tmp, st):
            return ffn_up("up2", None, hh, hl, tmp, st)

        oh, ol, ot, _ = fox()
        attn_out("ao", oh, ol, ot, "ln_attn_g0", "ln_attn_b0")
        nb = ffn_layer("0", "", "")
        layer_norm(nb, "ln_ffn_g0", "ln_ffn_b0")
        oh, ol, ot, _ = diff()
        attn_out("bo", oh, ol, ot, "ln_attn_g1", "ln_attn_b1")
        nb = ffn_layer("1", "", "")
        XR = at("XR", 4096, F32, R0)
        nb0 = norm_bufs(R0 + 40 * K)
        layer_norm(nb, "ln_ffn_g1", "ln_ffn_b1", final=lambda j: blk(XR, j),
                   post=lambda j, a: acc_step(nb0, j, blk(XR, j), a, False))
        second(XR, nb0)
        if turn == "sp":
            engine.wait_ge(s_out, 16 * 8)
    return used


def whole(nc, *args):
    mem = {}
    order = program(nc, *args, None, mem, None, None)
    with nc.Block() as block:
        @block.sync
        def _(e):
            program(nc, *args, order, mem, "sp", e)

        @block.tensor
        def _(e):
            program(nc, *args, order, mem, "pe", e)

        @block.scalar
        def _(e):
            program(nc, *args, order, mem, "act", e)

        @block.vector
        def _(e):
            program(nc, *args, order, mem, "dve", e)

        @block.gpsimd
        def _(e):
            program(nc, *args, order, mem, "pool", e)


def kernel(**inputs):
    import concourse.bacc as bacc
    from concourse.bass_utils import run_bass_kernel_spmd

    a = {k: np.asarray(v) for k, v in inputs.items()}
    w = {"a_w_in": a["a_w_in"][0], "a_w_out": a["a_w_out"][0], "kv_w": a["kv_w"], "b_w_q": a["b_w_q"][0],
         "b_w_out": a["b_w_out"][0], "w_in_2": a["w_in_2"][0], "w_attn_proj_2": a["w_attn_proj_2"][0],
         "w_ssd_proj_2": a["w_ssd_proj_2"][0], "w_out_2": a["w_out_2"][0], "w_gate_up_2": a["w_gate_up_2"][0],
         "w_down_2": a["w_down_2"][0]}
    for i in range(2):
        w[f"ffn_w_in{i}"], w[f"ffn_w_out{i}"] = a["ffn_w_in"][i], a["ffn_w_out"][i]
    places, total = unit_places()
    wall = np.empty(total, np.float32)
    for key, parts in unit_table().items():
        off, kt, n = places[key]
        m = np.concatenate([w[s][128 * k0:128 * (k0 + kk)][:, c] for s, k0, kk, c in parts], axis=1)
        wall[off:off + 128 * kt * n] = m.reshape(kt, 128, n).transpose(1, 0, 2).reshape(-1)

    sm, nsm = small_table()
    small = np.zeros((128, nsm), np.float32)

    def put(name, v, rep=False):
        o, n = sm[name]
        v = np.asarray(v)
        small[:, o:o + n] = np.broadcast_to(v.reshape(1, n), (128, n)) if rep else v.reshape(n, 128).T

    for i in range(2):
        put(f"ln_attn_g{i}", a["ln_attn_g"][i])
        put(f"ln_attn_b{i}", a["ln_attn_b"][i])
        put(f"ln_ffn_g{i}", a["ln_ffn_g"][i])
        put(f"ln_ffn_b{i}", a["ln_ffn_b"][i])
        for t in range(3):
            put(f"cw{i}{t}", a["ffn_conv_w"][i, t])
        put(f"cb{i}", a["ffn_conv_b"][i])
    for t in range(5):
        put(f"sw{t}", a["conv_w_2"][0, t])
    put("sb", a["conv_b_2"][0])
    for n, s in (("n1pre", "norm1_pre_2"), ("n1post", "norm1_post_2"), ("n2pre", "norm2_pre_2"),
                 ("n2post", "norm2_post_2"), ("ssdn", "ssd_norm_2")):
        put(n, a[s][0])
    t64 = turned(0)
    put("qn", np.concatenate([a["q_norm_2"][0][t64]] * 2))
    put("kn", np.concatenate([a["k_norm_2"][0][t64]] * 2))
    small[0:16, sm["bf"][0]] = a["a_b_f"][0]
    put("subln", a["b_subln_g"][0])
    put("lam", a["b_lambda"][0].reshape(-1), True)
    put("dtb", np.concatenate([a["dt_bias_f_2"][0], a["dt_bias_b_2"][0]]), True)
    put("alog", np.concatenate([a["a_log_f_2"][0], a["a_log_b_2"][0]]), True)
    put("dskip", a["d_skip_2"][0], True)
    fp, masks = const_arrays()
    xT = np.ascontiguousarray(a["x"][0].T.reshape(8, 128, S).transpose(1, 0, 2).reshape(128, 8 * S))
    arrays = {"xT": xT, "wall": wall, "small": small, "cfp": fp, "cmask": masks}

    nc = bacc.Bacc("TRN2", target_bir_lowering=False, num_devices=1)
    aps = [nc.dram_tensor(k, v.shape, mybir.dt.from_np(v.dtype), kind="ExternalInput").ap() for k, v in arrays.items()]
    out = nc.dram_tensor("outT", (128, 8 * S), F32, kind="ExternalOutput").ap()
    whole(nc, *aps, out)
    r = run_bass_kernel_spmd(nc, [arrays], core_ids=[0])
    o = r.results[0]["outT"]
    return np.ascontiguousarray(o.reshape(128, 8, S).transpose(1, 0, 2).reshape(D, S).T).reshape(1, S, D)
```

```python
import math

import numpy as np

import concourse.bass as bass
from concourse import mybir

F32 = mybir.dt.float32
F32R = mybir.dt.float32r
BF16 = mybir.dt.bfloat16
ALU = mybir.AluOpType
ACT = mybir.ActivationFunctionType
AX = mybir.AxisListType.X

S = 512
D = 1024
FF = 22
ALPHA = 4.0 ** 0.25
LAM_INIT = 0.8 - 0.6 * math.exp(-0.3)
NEG = -1.0e30
LAGS = (0, 2, 3, 5)
LAGD = (0, 1, 2, 3, 4)
RATES = (1.0, 0.85, 1.15, 0.36, 1.0)
AHEAD = 7
SLOW = 2
PACE = 2
FIRST = 16640



def rng(a, b):
    return list(range(a, b))


def halves(h):
    return [64 * h + 2 * d + e for e in range(2) for d in range(32)]


def turned(h):
    return [64 * h + x for x in rng(0, 16) + rng(32, 48) + rng(16, 32) + rng(48, 64)]


def unit_table():
    u = {}
    u["f", 0] = [("a_w_in", 0, 8, rng(3072, 3088))]
    for i in range(4):
        u["av", i] = [("a_w_in", 0, 8, rng(2048 + 256 * i, 2304 + 256 * i))]
    for i in range(8):
        u["aqk", i] = [("a_w_in", 0, 8, rng(128 * i, 128 * i + 128) + rng(1024 + 128 * i, 1152 + 128 * i))]
    for i in range(4):
        u["ao", i] = [("a_w_out", 0, 8, rng(256 * i, 256 * i + 256))]
    for lay in ("0", "1"):
        w1, w2 = "ffn_w_in" + lay, "ffn_w_out" + lay
        for j in range(FF):
            u["up" + lay, j] = [(w1, 0, 8, rng(128 * j, 128 * j + 128) + rng(2816 + 128 * j, 2944 + 128 * j))]
        for i in range(4):
            for p, (k0, kt) in enumerate(((0, 8), (8, 7), (15, 7))):
                u["dn" + lay, i, p] = [(w2, k0, kt, rng(256 * i, 256 * i + 256))]
    for i in range(4):
        u["bv", i] = [("kv_w", 0, 8, rng(1024 + 256 * i, 1280 + 256 * i))]
    for h in range(8):
        c = rng(64 * h, 64 * h + 64) + rng(512 + 64 * h, 576 + 64 * h)
        u["bqk", h] = [("b_w_q", 0, 8, c), ("kv_w", 0, 8, c)]
    for i in range(4):
        u["bo", i] = [("b_w_out", 0, 8, rng(256 * i, 256 * i + 256))]
    u["cv", 0] = [("w_in_2", 0, 8, rng(640, 768) + rng(3328, 3360))]
    for i in range(2):
        c = []
        for j in (2 * i, 2 * i + 1):
            c += turned(j) + turned(j + 4)
        u["cq", i] = [("w_in_2", 0, 8, c)]
    u["ck", 0] = [("w_in_2", 0, 8, [512 + x for x in turned(0) + turned(1)])]
    for i in range(6):
        u["cx", i] = [("w_in_2", 0, 8, rng(1792 + 256 * i, 2048 + 256 * i))]
    for i in range(4):
        u["cz", i] = [("w_in_2", 0, 8, rng(768 + 256 * i, 1024 + 256 * i))]
        u["cga", i] = [("w_in_2", 0, 8, rng(3360 + 256 * i, 3616 + 256 * i))]
        u["cgs", i] = [("w_in_2", 0, 8, rng(4384 + 256 * i, 4640 + 256 * i))]
        u["cpa", i] = [("w_attn_proj_2", 0, 4, rng(256 * i, 256 * i + 256))]
        u["cps", i] = [("w_ssd_proj_2", 0, 8, rng(256 * i, 256 * i + 256))]
        u["co", i] = [("w_out_2", 0, 8, rng(256 * i, 256 * i + 256))]
        for p, (k0, kt) in enumerate(((0, 8), (8, 7), (15, 7))):
            u["dn2", i, p] = [("w_down_2", k0, kt, rng(256 * i, 256 * i + 256))]
    for j in range(FF):
        u["up2", j] = [("w_gate_up_2", 0, 8, rng(128 * j, 128 * j + 128) + rng(2816 + 128 * j, 2944 + 128 * j))]
    return u


def unit_places():
    at, out = 0, {}
    for key, parts in unit_table().items():
        kt, n = parts[0][2], sum(len(p[3]) for p in parts)
        out[key] = (at, kt, n)
        at += 128 * kt * n
    return out, at



def small_table():
    names = [("ln_attn_g0", 8), ("ln_attn_b0", 8), ("ln_ffn_g0", 8), ("ln_ffn_b0", 8),
             ("ln_attn_g1", 8), ("ln_attn_b1", 8), ("ln_ffn_g1", 8), ("ln_ffn_b1", 8),
             ("cw00", 44), ("cw01", 44), ("cw02", 44), ("cb0", 44),
             ("cw10", 44), ("cw11", 44), ("cw12", 44), ("cb1", 44),
             ("sw0", 12), ("sw1", 12), ("sw2", 12), ("sw3", 12), ("sw4", 12), ("sb", 12),
             ("n1pre", 8), ("n1post", 8), ("n2pre", 8), ("n2post", 8), ("ssdn", 8),
             ("qn", 1), ("kn", 1), ("bf", 1), ("subln", 1),
             ("lam", 256), ("dtb", 32), ("alog", 32), ("dskip", 16)]
    at, out = 0, {}
    for name, n in names:
        out[name] = (at, n)
        at += n
    return out, at


def const_arrays():
    p = np.arange(128)
    ident = np.eye(128, dtype=np.float32)
    upper = (p[:, None] <= p[None, :]).astype(np.float32)
    lower = (p[:, None] >= p[None, :]).astype(np.float32)
    mean = np.full((128, 128), 1.0 / D, np.float32)
    blk = np.kron(np.eye(2), np.full((64, 64), 1.0 / 64)).astype(np.float32)
    ones = np.ones((128, 512), np.float32)
    causal = np.where(p[None, :] <= p[:, None], 0.0, NEG)
    chunk = np.where(p[None, :] < (p[:, None] // 64 + 1) * 64, 0.0, NEG)
    mf = np.where(p[:, None] <= p[None, :], 0.0, NEG)
    mb = np.where(p[:, None] >= p[None, :], 0.0, NEG)
    inv = (1.0 / (np.float32(10000.0) ** (np.arange(0, 64, 2, dtype=np.float32) / np.float32(64)))).astype(np.float32)
    ang = np.arange(S, dtype=np.float32)[:, None] * inv[None, :]
    inv2 = (np.float32(10000.0) ** (-np.arange(0, 32, 2, dtype=np.float32) / np.float32(32))).astype(np.float32)
    t = np.arange(S)
    ang2 = np.concatenate([(t // 64).astype(np.float32)[:, None] * inv2, (t % 64).astype(np.float32)[:, None] * inv2], 1)
    tabs = []
    for a in (ang, ang2):
        c, s = np.cos(a).astype(np.float32).T, np.sin(a).astype(np.float32).T
        tabs += [np.concatenate([c] * 4, 0), np.concatenate([-s, s, -s, s], 0)]
    fp = np.concatenate([ident, upper, lower, mean, blk, ones] + tabs, 1).astype(np.float32)
    masks = np.concatenate([np.eye(128), causal, chunk] + [mf] * 4 + [mb] * 4, 1).astype(np.float32)
    return fp, masks


class Queue:

    def __init__(self, sem, chained, eng):
        self.sem, self.n, self.chained, self.eng, self.seen = sem, 0, chained, eng, {}

    def op(self, fn, *after, inc=True, chain=True):
        if self.eng is not None:
            waits = list(flat(after))
            if self.chained and chain and self.n:
                waits.append((self.sem, self.n))
            need = {}
            for sem, v in waits:
                if v > self.seen.get(sem.name, 0) and v > need.get(sem.name, (None, 0))[1]:
                    need[sem.name] = (sem, v)
            for name, (sem, v) in need.items():
                self.eng.wait_ge(sem, v)
                self.seen[name] = v
            ins = fn(self.eng)
            if inc:
                ins.then_inc(self.sem, 1)
        if inc:
            self.n += 1
        return (self.sem, self.n)

    def last(self):
        return (self.sem, self.n) if self.n else None


def flat(x):
    for y in x:
        if y is None:
            continue
        if isinstance(y, list) or (isinstance(y, tuple) and y and (y[0] is None or isinstance(y[0], (list, tuple)))):
            yield from flat(y)
        elif isinstance(y, tuple) and len(y) == 2:
            yield y


def program(nc, xT, wall, small, cfp, cmask, outT, order, mem, turn, engine):
    places, _ = unit_places()
    sm, nsm = small_table()
    used = []
    def sem(name):
        if name not in mem:
            mem[name] = nc.alloc_semaphore(name=name)
        return mem[name]

    s_pe, s_act, s_dve, s_pool = sem("s_pe"), sem("s_act"), sem("s_dve"), sem("s_pool")
    s_raw = [sem("s_raw0"), sem("s_raw1")]
    s_in = sem("s_in")
    s_x = [sem(f"s_x{q}") for q in range(4)]
    s_tab = sem("s_tab")
    s_sm = sem("s_sm")
    s_out = sem("s_out")
    PE, AC, DV, PO, SP = (Queue(q, c, engine if turn == n else None) for q, c, n in (
        (s_pe, False, "pe"), (s_act, True, "act"), (s_dve, True, "dve"), (s_pool, True, "pool"), (None, False, "sp")))

    def sp(fn, *after):
        SP.op(fn, *after, inc=False)

    def at(name, n, dt, off, parts=128):
        if name not in mem:
            mem[name] = nc.alloc_sbuf_tensor_at(name, [parts, n], dt, offset=FIRST + off)
        return mem[name]

    K = 1024
    base = 0
    FP = at("FP", 3200, F32, base)
    MK = at("MK", 1408, BF16, base + 12800)
    MKF = at("MKF", 1408, F32, 170 * K)
    SM = at("SM", nsm, F32, base + 15616)
    base = 15616 + nsm * 4
    base = (base + 63) // 64 * 64
    TN = at("TN", 128, F32, base)
    base += 512
    LAMT = at("LAMT", 64, F32, base)
    base += 256
    NEGC = at("NEGC", 32, F32, base)
    SEL = at("SEL", 16, F32R, base + 128)
    base += 256
    RAW = [at(f"RAW{i}", 2048, F32, base + 8 * K * i) for i in range(2)]
    base += 16 * K
    HI = [at(f"HI{i}", 2048, F32R, base + 8 * K * i) for i in range(2)]
    base += 16 * K
    LO = [at(f"LO{i}", 2048, F32R, base + 8 * K * i) for i in range(2)]
    base += 16 * K
    XH = at("XH", 4096, F32R, base)
    YH = at("YH", 4096, F32, base)
    base += 16 * K
    XL = at("XL", 4096, F32R, base)
    YL = at("YL", 4096, F32, base)
    base += 16 * K
    R0 = base
    if "PS" not in mem:
        mem["PS"] = [nc.alloc_psum_tensor(f"PS{i}", [128, 512], F32) for i in range(8)]
    PS = mem["PS"]

    IDN, UPP, LOW, MEAN, BLK, ONE = (FP[:, 128 * i:128 * i + 128] for i in range(6))
    ONE512 = FP[:, 640:1152]
    COSA, SINA, COSB, SINB = (FP[:, 1152 + 512 * i:1664 + 512 * i] for i in range(4))
    IDB, CAUS, CHNK = (MK[:, 128 * i:128 * i + 128] for i in range(3))
    MF, MB = MK[:, 384:896], MK[:, 896:1408]

    def col(name, j=0, n=1):
        a = sm[name][0]
        return SM[:, a + j:a + j + n]

    def blk(t, j, w=512):
        return t[:, w * j:w * j + w]

    free = [None] * 8

    def marks():
        return [PE.last(), AC.last(), DV.last(), PO.last()]

    xtok = [None] * 8

    def split(src, h, l, *after, rest=None):
        a = AC.op(lambda e: e.activation(h, src, ACT.Copy), *after)
        return (rest or DV).op(lambda e: e.tensor_tensor(l, src, h.bitcast(F32), ALU.subtract), a)

    XF = at("XF", 4096, F32, 120 * K)
    def load_x(q):
        sp(lambda e: e.dma_start(XF[:, 1024 * q:1024 * q + 1024], xT[:, 1024 * q:1024 * q + 1024]).then_inc(s_x[q], 16))

    def load(dst, src, s, *after):
        sp(lambda e: e.dma_start(dst, src).then_inc(s, 16), *after)

    SMALL, TABLES = (s_sm, 16), (s_tab, 16)
    INP = [(s_in, 32), SMALL]
    def split_input():
        for j in range(8):
            xtok[j] = split(blk(XF, j), blk(XH, j), blk(XL, j), (s_x[j // 2], 16))

    CONST = None

    def constants():
        nonlocal CONST
        DV.op(lambda e: e.tensor_copy(MK[:, :], MKF[:, :]), INP)
        DV.op(lambda e: e.memset(NEGC[:, 0:1], 1e-5))
        DV.op(lambda e: e.memset(NEGC[:, 1:2], 1e-6))
        DV.op(lambda e: e.memset(NEGC[:, 8:16], 0.0))
        for g, o in NG.items():
            DV.op(lambda e, o=o, g=g: e.tensor_scalar(o, col(g, 0, 8), -1.0, None, ALU.mult))
        AC.op(lambda e: e.activation(SEL[0:32, :], IDN[0:32, 0:16], ACT.Copy), INP)
        a = AC.op(lambda e: e.activation(SEL[32:48, :], IDN[32:48, 32:48], ACT.Copy))
        CONST = [a, DV.op(lambda e: e.memset(NEGC[:, 2:3], 1.0))]

    def split_rows(dst, src, *after):
        AC.op(lambda e: e.activation(dst[0:32, :], IDN[0:32, 64:65].to_broadcast([32, 512]), ACT.Copy), INP, *after)
        a = AC.op(lambda e: e.activation(dst[0:16, :], src, ACT.Copy))
        return DV.op(lambda e: e.tensor_tensor(dst[32:48, :], src, dst[0:16, :].bitcast(F32), ALU.subtract), a)

    EPS5, EPS6 = NEGC[:, 0:1], NEGC[:, 1:2]

    raw_free = [None, None]
    part_free = [None, None]
    made = []

    def load_raw(i):
        key = order[i]
        off, kt, n = places[key]
        r = RAW[i % 2]
        src = wall[off:off + 128 * kt * n].rearrange("(p n) -> p n", p=128)
        sp(lambda e: e.dma_start(r[:, 0:kt * n], src).then_inc(s_raw[i % 2], 16), raw_free[i % 2])

    def split_steps(i):
        off, kt, n = places[order[i]]
        s = i % 2
        landed = (s_raw[s], 16 * (i // 2 + 1))
        highs, toks = [], []
        made.append(toks)
        cuts = [(2 * k * n, min(2 * k + 2, kt) * n) for k in range((kt + 1) // 2)]
        for p in range(len(cuts) + 1):
            if p:
                a, b = cuts[p - 1]
                r, h, l = RAW[s][:, a:b], HI[s][:, a:b], LO[s][:, a:b]
                q = DV if p % 2 else PO
                toks.append(q.op(lambda e: e.tensor_tensor(l, r, h.bitcast(F32), ALU.subtract),
                                 highs[p - 1], part_free[s], chain=False))
            if p < len(cuts):
                a, b = cuts[p]
                r, h = RAW[s][:, a:b], HI[s][:, a:b]
                highs.append(AC.op(lambda e: e.activation(h, r, ACT.Copy), landed, part_free[s], chain=False))
            if p < len(cuts):
                yield
        raw_free[s] = [highs[-1], toks[-2:]]
        if i + 2 < len(order):
            load_raw(i + 2)

    parts_due = [None, 0]

    def part_step(n):
        if parts_due[0] is not None:
            parts_due[1] += n
            if parts_due[1] >= 2.5:
                parts_due[1] -= 2.5
                next(parts_due[0], None)

    def take(key):
        i = len(used)
        used.append(key)
        off, kt, n = places[key]
        if i == 4:
            load(FP[:, 1152:3200], cfp[:, 1152:3200], s_tab)
        if order is None:
            return HI[0], LO[0], kt, n, lambda k: None, lambda t: None
        assert order[i] == key
        if i == 0:
            load_raw(0)
            for q in range(4):
                load_x(q)
            load(SM[:, :], small, s_sm)
            load_raw(1)
            load(FP[:, 0:1152], cfp[:, 0:1152], s_in)
            load(MKF[:, :], cmask, s_in)
            parts_due[0] = split_steps(0)
        if parts_due[0] is not None:
            for _ in parts_due[0]:
                pass
        if i == 0:
            split_input()
        parts_due[0], parts_due[1] = (split_steps(i + 1), 2.0) if i + 1 < len(order) else (None, 0)

        def release(t):
            part_free[i % 2] = t
        return HI[i % 2], LO[i % 2], kt, n, (lambda k: made[i][k // 2]), release

    def mm(out, a, b, start, stop, *after, inc=False):
        return PE.op(lambda e: e.matmul(out, a, b, start=start, stop=stop), *after, inc=inc)

    def tr(out, src, ident, *after, inc=False):
        return PE.op(lambda e: e.transpose(out, src, ident), *after, inc=inc)

    lin_bank = [0, [0, 1, 2, 3, 4, 7]]

    def pick():
        b = lin_bank[1][lin_bank[0] % len(lin_bank[1])]
        lin_bank[0] += 1
        return b

    beside = [None, 0.0, 0.0]
    chore_due = [0.0]

    chores = []

    def chore():
        if chores and next(chores[0], chores) is chores:
            chores.pop(0)

    def alongside(gen, rate):
        beside[0], beside[1], beside[2] = gen, rate, 0.0

    def tick(n=1.0):
        part_step(n)
        chore_due[0] += n
        if chore_due[0] >= 1.0:
            chore_due[0] -= 1.0
            chore()
        if beside[0] is not None:
            beside[2] += n * beside[1]
            while beside[2] >= 1.0:
                beside[2] -= 1.0
                next(beside[0], None)

    def until(cond):
        while not cond():
            chore()
            next(beside[0])

    def drain():
        if beside[0] is not None:
            for _ in beside[0]:
                chore()
        while chores:
            chore()
        beside[0] = None

    def lin_fm(keys, xh, xl, xt, widths=(128, 128), together=False):
        banks = [pick() for _ in widths]
        parts = [take(key) for key in keys]
        total = sum(p[2] for p in parts)
        toks = [None] * len(widths)
        at_k = []
        for p, (hi, lo, kt, n, ready, release) in enumerate(parts):
            at_k += [(p, k) for k in range(kt)]

        def step(j, kk):
            p, k = at_k[kk]
            hi, lo, kt, n, ready, release = parts[p]
            c, w, b = sum(widths[:j]), widths[j], banks[j]
            wh, wl = hi[:, k * n + c:k * n + c + w], lo[:, k * n + c:k * n + c + w]
            o = PS[b][0:w, :]
            mm(o, wh, xh(kk), kk == 0, False, ready(k), xt(kk), free[b] if kk == 0 else None)
            mm(o, wh, xl(kk), False, False)
            toks[j] = mm(o, wl, xh(kk), False, kk == total - 1, inc=(k == kt - 1))
            tick()
        if together:
            for kk in range(total):
                for j in range(len(widths)):
                    step(j, kk)
        else:
            for j in range(len(widths)):
                for kk in range(total):
                    step(j, kk)
        for p in parts:
            p[5](toks[-1])
        return list(zip(banks, toks))

    def lin_long(keys, xh, xl, xt, widths=(128, 128)):
        banks = [pick() for _ in widths]
        total = sum(places[k][1] for k in keys)
        kk, toks = 0, [None] * len(widths)
        for key in keys:
            hi, lo, kt, n, ready, release = take(key)
            for k in range(kt):
                for j, b in enumerate(banks):
                    wh = hi[:, k * n + 128 * j:k * n + 128 * j + 128]
                    wl = lo[:, k * n + 128 * j:k * n + 128 * j + 128]
                    o = PS[b][:, :]
                    mm(o, wh, xh(kk), kk == 0, False, ready(k), xt(kk), free[b] if kk == 0 else None)
                    mm(o, wh, xl(kk), False, False)
                    toks[j] = mm(o, wl, xh(kk), False, kk == total - 1, inc=(k == kt - 1))
                    tick()
                kk += 1
            release(toks[-1])
        return list(zip(banks, toks))

    def lin_tm(key, xh, xl, xt, evac):
        hi, lo, kt, n, ready, release = take(key)
        for c in range(4):
            b = pick()
            o = PS[b][:, 0:n]
            t = slice(128 * c, 128 * c + 128)
            for k in range(kt):
                wh, wl = hi[:, k * n:k * n + n], lo[:, k * n:k * n + n]
                mm(o, xh(k)[:, t], wh, k == 0, False, ready(k), xt(k), free[b])
                mm(o, xl(k)[:, t], wh, False, False)
                tok = mm(o, xh(k)[:, t], wl, False, k == kt - 1, inc=(k == kt - 1))
                tick(0.5)
            if c == 3:
                release(tok)
            free[b] = evac(c, PS[b], tok)

    def norm_bufs(off):
        return {n: at(f"{n}_{off}_{len(used)}", 512, F32, off + 2048 * i)
                for i, n in enumerate(("SQ", "A1", "A2", "MS", "RS", "T1", "T2"))}

    def acc_step(nb, j, y, tok, mean):
        sq, a1, a2 = nb["SQ" if j % 2 else "MS"][:, :], nb["A1"][:, :], nb["A2"][:, :]
        prev = nb.get("tok")
        if j == 0:
            t = [AC.op(lambda e: e.activation(a2, y, ACT.Square), tok, prev)]
            if mean:
                t.append(PO.op(lambda e: e.tensor_copy(a1, y), tok, prev))
        else:
            if j == 7:
                nb["first"] = nb["t"]
            t = [AC.op(lambda e: e.activation(sq, y, ACT.Square), tok, nb["sqfree"][j % 2] if j > 2 else prev)]
            if j < 7:
                u = PO.op(lambda e: e.tensor_tensor(a2, a2, sq, ALU.add), t[0], nb["t"])
                nb.setdefault("sqfree", [None, None])[j % 2] = u
                t.append(u)
                if mean:
                    t.append(PO.op(lambda e: e.tensor_tensor(a1, a1, y, ALU.add), tok))
            else:
                nb["last"], nb["made"] = y, tok
        nb["t"] = t
        return t

    def stats(nb, eps, mean):
        b1, b2 = 5, 6
        b = 6
        m2, var, rs, sums = TN[:, 32:36], TN[:, 36:40], TN[:, 40:44], TN[:, 88:96]
        var0, mu = TN[:, 88:92], TN[:, 92:96]
        AC.op(lambda e: e.activation(TN[:, 44:45], NEGC[:, 2:3], ACT.Sqrt), CONST)
        parts = [(0, nb["A2"], nb["first"])]
        if mean:
            parts += [(4, nb["A1"], nb["first"]), (4, nb["last"], nb["made"])]
        parts += [(0, nb["SQ"], nb["t"])]
        mm(PS[b][:, 0:8], IDN, NEGC[:, 8:16], True, False, free[b], CONST)
        for n, (at_, x, tok) in enumerate(parts):
            for c in range(4):
                t = mm(PS[b][:, at_ + c:at_ + c + 1], x[:, 128 * c:128 * c + 128], MEAN[:, 0:1], False,
                       n == len(parts) - 1 and c == 3, tok, inc=(c == 3))

        def spread(bank, cols, tok):
            for c in range(4):
                t = mm(PS[bank][:, 128 * c:128 * c + 128], cols[:, c:c + 1].to_broadcast([128, 128]), IDN, True, True,
                       tok, free[bank], inc=(c == 3))
            return t
        if mean:
            d = DV.op(lambda e: e.tensor_copy(sums, PS[b][:, 0:8]), t, rs_read[0])
            t5 = spread(5, mu, d)
            DV.op(lambda e: e.tensor_tensor(m2, mu, mu, ALU.mult))
            d = DV.op(lambda e: e.tensor_tensor(var, var0, m2, ALU.subtract))
            a = AC.op(lambda e: e.activation(var, var, ACT.Sqrt, bias=eps), d)
        else:
            a = AC.op(lambda e: e.activation(var, PS[b][:, 0:4], ACT.Sqrt, bias=eps), t, rs_read[0])
        r = DV.op(lambda e: e.reciprocal(rs, var), a, rs_read[0])
        t = rs_read[0] = spread(b, rs, r)
        nb["tok"] = [t]
        return t

    rs_read = [None]

    def residual_tile(j, bank, tok):
        y, yl = blk(YH, j), blk(YL, j)
        d = DV.op(lambda e: e.scalar_tensor_tensor(out=yl, in0=blk(XL, j).bitcast(F32), scalar=ALPHA, in1=PS[bank][:, :],
                                                   op0=ALU.mult, op1=ALU.add), tok)
        free[bank] = d
        return DV.op(lambda e: e.scalar_tensor_tensor(out=y, in0=blk(XH, j).bitcast(F32), scalar=ALPHA, in1=yl,
                                                      op0=ALU.mult, op1=ALU.add))

    def layer_norm(nb, g, b, final=None, post=None):
        r = stats(nb, EPS5, True)
        ts = [nb[n][:, :] for n in ("T1", "T2", "RS")]
        tfree = [None] * 3
        for j in range(8):
            y, t = blk(YH, j), ts[j % 3]
            DV.op(lambda e: e.tensor_tensor(t, PS[5][:, :], y, ALU.subtract), r, tfree[j % 3], marks() if j == 0 else None)
            free[5] = free[6] = d = DV.op(lambda e: e.tensor_tensor(t, t, PS[6][:, :], ALU.mult))
            x = final(j) if final else t
            a = AC.op(lambda e: e.activation(x, t, ACT.Identity, bias=col(b, j), scale=NG[g][:, j:j + 1]), d)
            if post:
                tfree[j % 3] = a
                post(j, a)
            else:
                tfree[j % 3] = xtok[j] = split(x, blk(XH, j), blk(XL, j), a, rest=PO)

    NG = {}
    for i, g in enumerate(("ln_attn_g0", "ln_ffn_g0", "ln_attn_g1", "ln_ffn_g1")):
        o = TN[:, 8 * i:8 * i + 8]
        NG[g] = o
    XHk, XLk, XTk = (lambda k: blk(XH, k)), (lambda k: blk(XL, k)), (lambda k: xtok[k])

    def staggered(items, stages, lags):
        for n in range(len(items) + lags[-1]):
            for s in reversed(range(len(stages))):
                if 0 <= n - lags[s] < len(items):
                    yield from stages[s](items[n - lags[s]])

    def fox():
        o = R0
        V = at("aV", 4096, F32, o); o += 16 * K
        OT = at("aO", 4096, F32, o); o += 16 * K
        QK = at("aQK", 2048, F32, o); o += 8 * K
        L = at("aL", 1024, F32, o); o += 4 * K
        P = at("aP", 1024, F32, o); o += 4 * K
        PT = at("aPT", 1024, F32, o); o += 4 * K
        NB = at("aNB", 1024, F32, o); o += 4 * K
        OH = at("aOH", 4096, F32R, o); o += 16 * K
        OL = at("aOL", 4096, F32R, o); o += 16 * K
        FZ = at("aFZ", 2560, F32, o, 16); o += 10 * K
        NC = at("aNC", 512, F32R, o, 48); o += 2 * K
        MX = at("aMX", 64, F32, o); o += 256
        NM = at("aNM", 64, F32, o); o += 256
        SU = at("aSU", 64, F32, o); o += 256
        RC = at("aRC", 64, F32, o); o += 256
        (fb, ft), = lin_fm([("f", 0)], XHk, XLk, XTk, widths=(16,))
        start = marks()
        z, e1, l1, c1, n1 = (FZ[:, 512 * i:512 * i + 512] for i in range(5))
        def gates():
            d = DV.op(lambda e: e.tensor_scalar(z, PS[fb][0:16, :], col("bf")[0:16, :], None, ALU.add), ft, start, SMALL)
            free[fb] = d
            a = AC.op(lambda e: e.activation(e1, z, ACT.Abs), d)
            a = AC.op(lambda e: e.activation(e1, e1, ACT.Exp, scale=-1.0), a)
            yield
            a = AC.op(lambda e: e.activation(l1, e1, ACT.Ln, bias=1.0), a)
            yield
            d = DV.op(lambda e: e.tensor_scalar(z, z, 0.0, None, ALU.min), a)
            d = DV.op(lambda e: e.tensor_tensor(z, z, l1, ALU.subtract))
            yield
            d = DV.op(lambda e: e.tensor_tensor_scan(c1, ONE512[0:16, :], z, 0.0, ALU.mult, ALU.add), INP)
            d = DV.op(lambda e: e.tensor_scalar(n1, c1, -8.0, None, ALU.mult))
            yield
            ncd.append(split_rows(NC, n1, d))

        ncd = []

        vtok = [None] * 4
        def vunit(i):
            def evac(c, ps, tok):
                dst = V[:, 1024 * c + 256 * i:1024 * c + 256 * i + 256]
                vtok[i] = AC.op(lambda e: e.activation(dst, ps[:, 0:256], ACT.Copy), tok)
                return vtok[i]
            lin_tm(("av", i), XHk, XLk, XTk, evac)

        qkfree = [None, None]
        qktok = [None, None]
        def qkunit(hp):
            r = lin_fm([("aqk", hp)], XHk, XLk, XTk)
            s = hp % 2
            (b0, t0), (b1, t1) = r
            q, k = QK[:, 1024 * s:1024 * s + 512], QK[:, 1024 * s + 512:1024 * s + 1024]
            a = AC.op(lambda e: e.activation(q, PS[b0][:, :], ACT.Copy), t0, qkfree[s])
            d = DV.op(lambda e: e.tensor_copy(k, PS[b1][:, :]), t1, qkfree[s])
            free[b0], free[b1] = a, d
            qktok[s] = [a, d]

        nbfree = [None, None]
        nbt = [None, None]
        ptfree = [None, None]
        pfree = [None, None]
        lfree = [None, None]
        ohtok = [None] * 8
        state = {}
        units = {"q": 0, "v": 0}
        done = [0]

        def ap(t, h):
            s, r = (h // 2) % 2, slice(64 * (h % 2), 64 * (h % 2) + 64)
            return QK[r, 1024 * s + 512 * t:1024 * s + 512 * t + 512]

        def scores(it):
            h, i = it
            while units["q"] <= h // 2 or units["v"] <= h // 4 or not ncd:
                yield
            if i == 0:
                nb = blk(NB, h % 2)
                tb = tbank()
                t = mm(PS[tb][:, :], SEL[0:48, h:h + 1].to_broadcast([48, 128]), NC[:, :], True, True, free[tb], ncd, CONST, inc=True)
                nbt[h % 2] = free[tb] = AC.op(lambda e: e.activation(nb, PS[tb][:, :], ACT.Copy), t, nbfree[h % 2])
            bank, kl, n = 2 + (4 * h + i) % 2, 128 * (i + 1), 4 * h + i
            mm(PS[bank][:, 0:kl], ap(0, h)[:, 128 * i:128 * i + 128], ap(1, h)[:, 0:kl], True, False,
               free[bank], qktok[(h // 2) % 2])
            t = mm(PS[bank][:, 128 * i:kl], IDB, CAUS, False, True, CONST, inc=True)
            if i == 3:
                qkfree[(h // 2) % 2] = t
            u = n % 2
            l, p, nb = blk(L, u)[:, 0:kl], blk(P, u), blk(NB, h % 2)
            mx, nm, su = MX[:, n:n + 1], NM[:, n:n + 1], SU[:, n:n + 1]
            d = DV.op(lambda e: e.tensor_tensor_reduce(
                l, PS[bank][:, 0:kl], nb[:, 0:kl], 0.125, -3.0e38, ALU.add, ALU.max, mx), t, nbt[h % 2], lfree[u], start)
            free[bank] = nbfree[h % 2] = d
            d = DV.op(lambda e: e.tensor_scalar(nm, mx, -1.0, None, ALU.mult))
            state[n] = lfree[u] = AC.op(lambda e: e.activation(p[:, 0:kl], l, ACT.Exp, bias=nm, accum_out=su), d, pfree[u])
            yield

        def flip(it):
            h, i = it
            n, kl = 4 * h + i, 128 * (i + 1)
            u, tb = n % 2, tbank()
            p, pt = blk(P, u), blk(PT, u)
            for kb in range(i + 1):
                t = tr(PS[tb][:, 128 * kb:128 * kb + 128], p[:, 128 * kb:128 * kb + 128], IDN,
                       state[n], free[tb], inc=(kb == i))
            pfree[u] = t
            if i % 2:
                c = AC.op(lambda e: e.activation(pt[:, 0:kl], PS[tb][:, 0:kl], ACT.Copy), t, ptfree[u])
            else:
                c = DV.op(lambda e: e.tensor_copy(pt[:, 0:kl], PS[tb][:, 0:kl]), t, ptfree[u])
            state[n] = free[tb] = c
            yield

        def values(it):
            h, i = it
            n = 4 * h + i
            pt, ob = blk(PT, n % 2), 6 + h % 2
            for kb in range(i + 1):
                t = mm(PS[ob][:, 64 * i:64 * i + 64], pt[:, 128 * kb:128 * kb + 128],
                       V[:, 1024 * kb + 64 * h:1024 * kb + 64 * h + 64], kb == 0, kb == i,
                       state[n], free[ob], vtok[h // 4], inc=(kb == i))
            ptfree[n % 2] = t
            if i == 3:
                rc = RC[:, 4 * h:4 * h + 4]
                DV.op(lambda e: e.reciprocal(rc, SU[:, 4 * h:4 * h + 4]), AC.last())
                dst = OT[:, :].rearrange("p (c n) -> p c n", c=4)[:, :, 64 * h:64 * h + 64]
                d = DV.op(lambda e: e.tensor_tensor(dst, PS[ob][:, 0:256].rearrange("p (c n) -> p c n", c=4),
                                                    rc.unsqueeze(2).to_broadcast([128, 4, 64]), ALU.mult), t)
                free[ob] = state["o"] = d
                done[0] = h + 1
            yield

        def turn(it):
            h, i = it
            if h % 2 and i == 3:
                j, tb = h // 2, tbank()
                for c in range(4):
                    t = tr(PS[tb][:, 128 * c:128 * c + 128], OT[:, 1024 * c + 128 * j:1024 * c + 128 * j + 128], IDN,
                           free[tb], state["o"], inc=(c == 3))
                free[tb] = ohtok[j] = split(PS[tb][:, :], blk(OH, j), blk(OL, j), t)
                yield

        tbn = [0]

        def tbank():
            tbn[0] += 1
            return 4 + tbn[0] % 2

        items = [(h, i) for h in range(16) for i in range(4)]
        qkunit(0)
        units["q"] = 1
        lin_bank[1] = [0, 1]
        chores.append(gates())
        constants()
        alongside(staggered(items, [scores, flip, values, turn], LAGS), RATES[0])
        for kind, i in [("v", 0), ("q", 1), ("v", 1), ("q", 2), ("q", 3), ("v", 2), ("q", 4), ("q", 5), ("v", 3),
                        ("q", 6), ("q", 7)]:
            if kind == "q":
                if i >= 2:
                    until(lambda: done[0] >= 2 * i - 2)
                qkunit(i)
            else:
                vunit(i)
            units[kind] = i + 1
        drain()
        lin_bank[1] = [0, 1, 2, 3, 4, 7]
        return (lambda k: blk(OH, k)), (lambda k: blk(OL, k)), (lambda k: ohtok[k]), o

    def attn_out(name, oh, ol, ot, g, b):
        nb = norm_bufs(R0)
        for i in range(4):
            for j, (bank, tok) in enumerate(lin_fm([(name, i)], oh, ol, ot)):
                d = residual_tile(2 * i + j, bank, [tok, marks()] if i == 0 and j == 0 else tok)
                acc_step(nb, 2 * i + j, blk(YH, 2 * i + j), d, True)
        layer_norm(nb, g, b)

    def ffn_up(names, conv, hh, hl, tmp, act_fn):
        htok = [None] * FF
        tfree = [None] * 2
        start = marks()
        for j in range(FF):
            (bg, tg), (bv, tv) = lin_fm([(names, j)], XHk, XLk, XTk, together=(j == 0))
            u = j % 2
            g, v = tmp[:, 1024 * u:1024 * u + 512], tmp[:, 1024 * u + 512:1024 * u + 1024]
            if conv is None:
                a = AC.op(lambda e: e.activation(g, PS[bg][:, :], ACT.Silu), tg, tfree[u], start)
                free[bg] = a
                d = DV.op(lambda e: e.tensor_tensor(g, g, PS[bv][:, :], ALU.mult), a, tv)
                free[bv] = d
            else:
                for x, bank, tok, f in ((g, bg, tg, j), (v, bv, tv, FF + j)):
                    w = [col(f"cw{conv}{t}", f) for t in range(3)]
                    a = AC.op(lambda e, x=x, w=w, bank=bank, f=f: e.activation(
                        x, PS[bank][:, :], ACT.Identity, bias=col(f"cb{conv}", f), scale=w[2]), tok, tfree[u], start)
                    for t in (1, 2):
                        d = DV.op(lambda e, x=x, w=w, bank=bank, t=t: e.scalar_tensor_tensor(
                            out=x[:, t:512], in0=PS[bank][:, 0:512 - t], scalar=w[2 - t], in1=x[:, t:512],
                            op0=ALU.mult, op1=ALU.add), a)
                    free[bank] = d
                a = AC.op(lambda e: e.activation(g, g, ACT.Silu), d)
                d = PO.op(lambda e: e.tensor_tensor(g, g, v, ALU.mult), a, d)
            htok[j] = split(g, blk(hh, j), blk(hl, j), d)
            tfree[u] = htok[j]
        return htok

    def ffn_down(name, hh, hl, htok, evac):
        for i in range(4):
            r = lin_long([(name, i, p) for p in range(3)], lambda k: blk(hh, k), lambda k: blk(hl, k), lambda k: htok[k])
            for j, (bank, tok) in enumerate(r):
                evac(2 * i + j, bank, tok)

    def ffn_layer(lay, g, b):
        hh = at(f"HH{lay}", 512 * FF, F32R, R0)
        hl = at(f"HL{lay}", 512 * FF, F32R, R0 + 44 * K)
        tmp = at(f"UT{lay}", 2048, F32, R0 + 88 * K)
        nb = norm_bufs(R0 + 88 * K)
        htok = ffn_up("up" + lay, int(lay), hh, hl, tmp, None)
        st = marks()
        nb["tok"] = st

        def evac(j, bank, tok):
            d = residual_tile(j, bank, [tok, st])
            acc_step(nb, j, blk(YH, j), d, True)
        ffn_down("dn" + lay, hh, hl, htok, evac)
        return nb

    def rotate(src, dst, rot, t1, cos, sin, tok, dfree, tfree, done):
        for n, (a_, b_) in enumerate(((0, 32), (32, 0), (64, 96), (96, 64))):
            a = AC.op(lambda e, a_=a_, b_=b_: e.activation(rot[a_:a_ + 32, :], src[b_:b_ + 32, :], ACT.Copy), tok, tfree)
            if n == 1:
                yield
        d = DV.op(lambda e: e.tensor_tensor(t1, src, cos, ALU.mult), a, tfree, TABLES)
        p = PO.op(lambda e: e.tensor_tensor(rot, rot, sin, ALU.mult), a, TABLES)
        yield
        done(PO.op(lambda e: e.tensor_tensor(dst, t1, rot, ALU.add), d, dfree))

    def diff():
        o = R0
        V = at("bV", 4096, F32, o); o += 16 * K
        OB = at("bO", 4096, F32, o); o += 16 * K
        QK = at("bQK", 3072, F32, o); o += 12 * K
        TQ = at("bTQ", 1024, F32, o); o += 4 * K
        ROT = at("bROT", 2048, F32, o); o += 8 * K
        P = at("bP", 2048, F32, o); o += 8 * K
        PT = at("bPT", 1024, F32, o); o += 4 * K
        OH = at("bOH", 4096, F32R, o); o += 16 * K
        OL = at("bOL", 4096, F32R, o); o += 16 * K
        TT = at("bTT", 512, F32, o); o += 2 * K
        ST = at("bST", 512, F32, o); o += 2 * K
        start = marks()
        MX, NM, SU, RC = (ST[:, 64 * i:64 * i + 64] for i in range(4))
        MS = ST[:, 256:288]
        lt, lm = TN[:, 64:128], LAMT
        for i in range(2):
            DV.op(lambda e, i=i: e.tensor_tensor(lt, col("lam", 128 * i, 64), col("lam", 128 * i + 64, 64), ALU.mult))
            d = DV.op(lambda e, i=i: e.tensor_reduce(lm[:, i:i + 1], lt, AX, ALU.add))
        a = AC.op(lambda e: e.activation(lm[:, 2:4], lm[:, 0:2], ACT.Exp), d)
        d = DV.op(lambda e: e.tensor_tensor(lm[:, 4:5], lm[:, 2:3], lm[:, 3:4], ALU.subtract), a)
        d = DV.op(lambda e: e.tensor_scalar(lm[:, 5:6], lm[:, 4:5], LAM_INIT, None, ALU.add))
        gs = lm[:, 8:9]
        DV.op(lambda e: e.tensor_scalar(gs, col("subln"), 1.0 - LAM_INIT, None, ALU.mult))

        vtok = [None] * 4
        def vunit(i):
            def evac(c, ps, tok):
                dst = V[:, 1024 * c + 256 * i:1024 * c + 256 * i + 256]
                vtok[i] = AC.op(lambda e: e.activation(dst, ps[:, 0:256], ACT.Copy), tok, start)
                return vtok[i]
            lin_tm(("bv", i), XHk, XLk, XTk, evac)

        qkfree, qktok, rfree = [None] * 3, [None] * 3, [None, None]
        def qkunit(h):
            s = h % 3
            r = lin_fm([("bqk", h)], XHk, XLk, XTk, together=(h == 0))
            toks = []

            def work(x, tok):
                dst = QK[:, 1024 * s + 512 * x:1024 * s + 512 * x + 512]
                rot, t1 = ROT[:, 1024 * x:1024 * x + 512], ROT[:, 1024 * x + 512:1024 * x + 1024]

                def done(p):
                    rfree[x] = p
                    toks.append(p)
                    if x:
                        qktok[s] = toks
                yield from rotate(blk(TQ, x), dst, rot, t1, COSA, SINA, tok, qkfree[s], rfree[x], done)
                if x:
                    for _ in range(AHEAD):
                        yield
                    units["q"] = h + 1
            for x, (bank, tok) in enumerate(r):
                free[bank] = AC.op(lambda e, x=x, bank=bank: e.activation(blk(TQ, x), PS[bank][:, :], ACT.Copy),
                                   tok, start, rfree[x])
                chores.append(work(x, free[bank]))

        ptfree = [None, None]
        pfree = [None, None]
        ohtok = [None] * 8
        state = {}
        units = {"q": 0, "v": 0}
        sent = [0]
        ttfree = [None]

        def scores(it):
            h, i = it
            while units["q"] <= h:
                yield
            s, kl, n = h % 3, 128 * (i + 1), 4 * h + i
            u, c0 = n % 2, 2 * n
            st = []
            for m in range(2):
                b, rows = 2 + 2 * u + m, slice(64 * m, 64 * m + 64)
                q = QK[rows, 1024 * s + 128 * i:1024 * s + 128 * i + 128]
                k = QK[rows, 1024 * s + 512:1024 * s + 512 + kl]
                mm(PS[b][:, 0:kl], q, k, True, False, free[b], qktok[s])
                st.append(mm(PS[b][:, 128 * i:kl], IDB, CHNK, False, True, CONST, inc=True))
            if i == 3:
                qkfree[s] = st[1]
                sent[0] = h + 1
            for m in range(2):
                b = 2 + 2 * u + m
                DV.op(lambda e: e.tensor_reduce(MX[:, c0 + m:c0 + m + 1], PS[b][:, 0:kl], AX, ALU.max), st[m], start)
            d = DV.op(lambda e: e.tensor_scalar(NM[:, c0:c0 + 2], MX[:, c0:c0 + 2], -0.125, None, ALU.mult))
            for m in range(2):
                b, p = 2 + 2 * u + m, P[:, 1024 * u + 512 * m:1024 * u + 512 * m + kl]
                a = AC.op(lambda e: e.activation(
                    p, PS[b][:, 0:kl], ACT.Exp, bias=NM[:, c0 + m:c0 + m + 1], scale=0.125,
                    accum_out=SU[:, c0 + m:c0 + m + 1]), d, pfree[u])
                free[b] = a
            state[n] = a
            yield

        def mix(it):
            h, i = it
            kl, n = 128 * (i + 1), 4 * h + i
            u, c0 = n % 2, 2 * n
            p1, p2 = P[:, 1024 * u:1024 * u + kl], P[:, 1024 * u + 512:1024 * u + 512 + kl]
            DV.op(lambda e: e.reciprocal(RC[:, c0:c0 + 2], SU[:, c0:c0 + 2]), state[n])
            DV.op(lambda e: e.tensor_scalar(p2, p2, RC[:, c0 + 1:c0 + 2], LAMT[:, 5:6], ALU.mult, ALU.mult))
            state[n] = DV.op(lambda e: e.scalar_tensor_tensor(out=p1, in0=p1, scalar=RC[:, c0:c0 + 1], in1=p2,
                                                              op0=ALU.mult, op1=ALU.subtract))
            yield

        def flip(it):
            h, i = it
            kl, n = 128 * (i + 1), 4 * h + i
            u, d = n % 2, state[n]
            for kb in range(i + 1):
                t = tr(PS[6][:, 128 * kb:128 * kb + 128], P[:, 1024 * u + 128 * kb:1024 * u + 128 * kb + 128], IDN,
                       d, free[6], inc=(kb == i))
            pfree[u] = t
            pt = blk(PT, u)
            if i % 2:
                c = AC.op(lambda e: e.activation(pt[:, 0:kl], PS[6][:, 0:kl], ACT.Copy), t, ptfree[u])
            else:
                c = DV.op(lambda e: e.tensor_copy(pt[:, 0:kl], PS[6][:, 0:kl]), t, ptfree[u])
            state[n] = free[6] = c
            yield

        def values(it):
            h, i = it
            while units["v"] <= h // 2:
                yield
            n = 4 * h + i
            pt = blk(PT, n % 2)
            for kb in range(i + 1):
                t = mm(PS[7][:, 128 * i:128 * i + 128], pt[:, 128 * kb:128 * kb + 128],
                       V[:, 1024 * kb + 128 * h:1024 * kb + 128 * h + 128], kb == 0, kb == i,
                       state[n], free[7], vtok[h // 2], inc=(kb == i))
            ptfree[n % 2] = t
            if i == 3:
                ob = OB[:, :].rearrange("p (c n) -> p c n", c=4)[:, :, 128 * h:128 * h + 128]
                a = AC.op(lambda e: e.activation(ob, PS[7][:, :].rearrange("p (c n) -> p c n", c=4), ACT.Copy), t, start)
                free[7] = a
                tt = TT[:, :].rearrange("p (c n) -> p c n", c=4)
                p = PO.op(lambda e: e.tensor_tensor(tt, ob, ob, ALU.mult), a, ttfree[0])

                def sums():
                    yield
                    yield
                    state["o", h] = DV.op(lambda e: e.tensor_reduce(MS[:, 4 * h:4 * h + 4], tt, AX, ALU.add), p)
                    ttfree[0] = state["o", h]
                chores.append(sums())
            yield

        def turns(h0, h1):
            while ("o", h1 - 1) not in state:
                yield
            ms = MS[:, 4 * h0:4 * h1]
            a = AC.op(lambda e: e.activation(ms, ms, ACT.Sqrt, bias=EPS5, scale=1.0 / 128), state["o", h1 - 1])
            d = DV.op(lambda e: e.reciprocal(ms, ms), a)
            x4 = [OB[:, :].rearrange("p (c n) -> p c n", c=4)[:, :, 128 * h:128 * h + 128] for h in range(8)]

            def scale(h):
                return DV.op(lambda e: e.tensor_tensor(
                    x4[h], x4[h], MS[:, 4 * h:4 * h + 4].unsqueeze(2).to_broadcast([128, 4, 128]), ALU.mult))
            sc = scale(h0)
            yield
            for h in range(h0, h1):
                for c in range(4):
                    t = tr(PS[6][:, 128 * c:128 * c + 128], OB[:, 1024 * c + 128 * h:1024 * c + 128 * h + 128], IDN,
                           free[6], sc, inc=(c == 3))
                if h + 1 < h1:
                    sc = scale(h + 1)
                f = DV.op(lambda e: e.tensor_scalar(TT[:, :], PS[6][:, :], gs, None, ALU.mult), t, ttfree[0])
                free[6] = f
                ohtok[h] = ttfree[0] = split(TT[:, :], blk(OH, h), blk(OL, h), f)
                yield

        def turn(it):
            if it in ((3, 3), (5, 3), (7, 3)):
                yield from turns({3: 0, 5: 4, 7: 6}[it[0]], it[0] + 1)

        lin_bank[1] = [0, 1]
        items = [(h, i) for h in range(8) for i in range(4)]
        qkunit(0)
        alongside(staggered(items, [scores, mix, flip, values, turn], LAGD), RATES[1])
        for kind, i in [("v", 0), ("q", 1), ("q", 2), ("q", 3), ("v", 1), ("q", 4), ("q", 5), ("v", 2), ("q", 6),
                        ("q", 7), ("v", 3)]:
            if kind == "q":
                if i >= 3:
                    until(lambda: sent[0] >= i - 2)
                qkunit(i)
            else:
                vunit(i)
                units["v"] = i + 1
        drain()
        lin_bank[1] = [0, 1, 2, 3, 4, 7]
        return (lambda k: blk(OH, k)), (lambda k: blk(OL, k)), (lambda k: ohtok[k]), o

    def rms_apply(nb, src, tok, gain):
        r = stats(nb, EPS6, False)
        ts = [nb[n][:, :] for n in ("T1", "T2", "RS")]
        tfree = [None] * 3
        for j in range(8):
            t = ts[j % 3]
            free[6] = d = DV.op(lambda e: e.scalar_tensor_tensor(
                out=t, in0=blk(src, j), scalar=col(gain, j), in1=PS[6][:, :], op0=ALU.mult, op1=ALU.mult),
                r, tfree[j % 3], marks() if j == 0 else None)
            tfree[j % 3] = xtok[j] = split(t, blk(XH, j), blk(XL, j), d, rest=PO)

    def second(XR, nb0):
        O0 = R0 + 16 * K
        rms_apply(nb0, XR, None, "n1pre")
        o = O0
        OTH = at("cOTH", 2048, F32R, o); o += 8 * K
        OTL = at("cOTL", 2048, F32R, o); o += 8 * K
        DT = at("cDT", 128, F32, o); o += 512
        ADT = at("cADT", 128, F32, o); o += 512
        ACS = at("cACS", 128, F32, o); o += 512
        NAC = at("cNAC", 128, F32, o); o += 512
        EAC = at("cEAC", 128, F32, o); o += 512
        TOT = at("cTOT", 128, F32, o); o += 512
        DSD = at("cDSD", 128, F32, o); o += 512
        CD = at("cCD", 128, F32, o); o += 512
        EA = at("cEA", 32, F32, o); o += 128
        SS = at("cSS", 32, F32, o); o += 128
        E0 = o
        QQ = at("cQ", 2560, F32, o); o += 10 * K
        V = at("cV", 512, F32, o); o += 2 * K
        OT = at("cO", 2048, F32, o); o += 8 * K
        P = at("cP", 1024, F32, o); o += 4 * K
        PT = at("cPT", 1024, F32, o); o += 4 * K
        ROT = at("cROT", 2560, F32, o); o += 10 * K
        ST = at("cST", 128, F32, o); o += 512
        start = marks()
        MX, NM, SU, RC = (ST[:, 32 * i:32 * i + 32] for i in range(4))
        vt = []

        def evac(c, ps, tok):
            a = AC.op(lambda e: e.activation(V[:, 128 * c:128 * c + 128], ps[:, 0:128], ACT.Copy), tok, start)
            d = DV.op(lambda e: e.tensor_tensor(DT[:, 32 * c:32 * c + 32], ps[:, 128:160], col("dtb", 0, 32), ALU.add), a)
            vt.append(a)
            return d
        SQ5 = [blk(OT, n) for n in range(4)] + [blk(P, 0)]
        qt, sqt = [None] * 5, [None] * 5

        def qk_units(key, n0, widths=(128, 128), together=False):
            for j, (bank, tok) in enumerate(lin_fm([key], XHk, XLk, XTk, widths=widths, together=together)):
                n = n0 + j
                sqt[n] = AC.op(lambda e: e.activation(SQ5[n], PS[bank][:, :], ACT.Square), tok, start)
                free[bank] = DV.op(lambda e: e.tensor_copy(blk(QQ, n), PS[bank][:, :]), tok, sqt[n])

        acs = {}

        def prep():
            rfree = [start, start]
            for n in (4, 0, 1, 2, 3):
                while sqt[n] is None:
                    yield
                u, q = n % 2, blk(QQ, n)
                b = 5 + u
                rot, t1 = ROT[:, 1024 * u:1024 * u + 512], ROT[:, 1024 * u + 512:1024 * u + 1024]
                rs = TN[:, 48 + 8 * n:56 + 8 * n]
                for c in range(4):
                    m = mm(PS[b][:, 2 * c:2 * c + 2], SQ5[n][:, 128 * c:128 * c + 128], BLK[:, 0:65:64], True, True,
                           sqt[n], free[b], inc=(c == 3))
                free[b] = AC.op(lambda e: e.activation(rs, PS[b][:, 0:8], ACT.Sqrt, bias=EPS6), m)
                d = DV.op(lambda e: e.reciprocal(rs, rs), free[b])
                yield
                for c in range(4):
                    for i in range(2):
                        r = rs[:, 2 * c + i:2 * c + i + 1].to_broadcast([128, 64])
                        t = mm(PS[b][64 * i:64 * i + 64, 128 * c:128 * c + 128], r, IDN, True, True, d, free[b],
                               inc=(c == 3 and i == 1))
                x = free[b] = DV.op(lambda e: e.scalar_tensor_tensor(
                    out=q, in0=q, scalar=col("kn" if n == 4 else "qn"), in1=PS[b][:, :], op0=ALU.mult, op1=ALU.mult), t)
                yield

                def done(p, n=n, u=u):
                    qt[n] = rfree[u] = p
                yield from rotate(q, q, rot, t1, COSB, SINB, x, None, rfree[u], done)
                yield
            while not dtraw:
                yield
            a = AC.op(lambda e: e.activation(ADT[:, :], DT[:, :], ACT.Abs), dtraw)
            a = AC.op(lambda e: e.activation(ADT[:, :], ADT[:, :], ACT.Exp, scale=-1.0))
            a = AC.op(lambda e: e.activation(ADT[:, :], ADT[:, :], ACT.Ln, bias=1.0))
            a = AC.op(lambda e: e.activation(EA[:, :], col("alog", 0, 32), ACT.Exp))
            DV.op(lambda e: e.tensor_scalar(DT[:, :], DT[:, :], 0.0, None, ALU.max), a)
            DV.op(lambda e: e.tensor_tensor(DT[:, :], DT[:, :], ADT[:, :], ALU.add))
            v3 = lambda t: t[:, :].rearrange("p (c n) -> p c n", c=4)
            DV.op(lambda e: e.tensor_tensor(v3(ADT), v3(DT), EA[:, :].unsqueeze(1).to_broadcast([128, 4, 32]), ALU.mult))
            dtd = DV.op(lambda e: e.tensor_scalar(ADT[:, :], ADT[:, :], -1.0, None, ALU.mult))
            yield
            for c in range(4):
                mm(PS[5][:, 32 * c:32 * c + 16], UPP, ADT[:, 32 * c:32 * c + 16], True, True, dtd, free[5])
                mm(PS[5][:, 32 * c + 16:32 * c + 32], LOW, ADT[:, 32 * c + 16:32 * c + 32], True, True)
            for c in range(4):
                t = mm(PS[5][:, 128 + 32 * c:160 + 32 * c], ONE, ADT[:, 32 * c:32 * c + 32], True, True, inc=(c == 3))
            DV.op(lambda e: e.tensor_copy(ACS[:, :], PS[5][:, 0:128]), t)
            acs["nac"] = DV.op(lambda e: e.tensor_scalar(NAC[:, :], ACS[:, :], -1.0, None, ALU.mult))
            free[5] = DV.op(lambda e: e.tensor_copy(TOT[:, :], PS[5][:, 128:256]))
            d = DV.op(lambda e: e.tensor_tensor(DSD[:, :], TOT[:, :], ACS[:, :], ALU.subtract))
            AC.op(lambda e: e.activation(DSD[:, :], DSD[:, :], ACT.Exp), d)
            AC.op(lambda e: e.activation(EAC[:, :], ACS[:, :], ACT.Exp))
            a = AC.op(lambda e: e.activation(CD[:, :], TOT[:, :], ACT.Exp))
            acs["dec"] = DV.op(lambda e: e.tensor_tensor(DSD[:, :], DSD[:, :], DT[:, :], ALU.mult), a)
            yield

        pfree, ptfree = [None, None], [None, None]
        ohtok = [None] * 4
        state = {}

        def scores(it):
            h, i = it
            n, rows = 4 * h + i, slice(64 * (h // 4), 64 * (h // 4) + 64)
            u, bank = n % 2, 2 + n % 2
            q, k = QQ[rows, 512 * (h % 4) + 128 * i:512 * (h % 4) + 128 * i + 128], QQ[rows, 2048:2560]
            t = mm(PS[bank][:, :], q, k, True, True, free[bank], qt[h % 4], qt[4], inc=True)
            DV.op(lambda e: e.tensor_reduce(MX[:, n:n + 1], PS[bank][:, :], AX, ALU.max), t, start)
            d = DV.op(lambda e: e.tensor_scalar(NM[:, n:n + 1], MX[:, n:n + 1], -0.125, None, ALU.mult))
            state[n] = free[bank] = AC.op(lambda e: e.activation(
                blk(P, u), PS[bank][:, :], ACT.Exp, bias=NM[:, n:n + 1], scale=0.125, accum_out=SU[:, n:n + 1]), d, pfree[u])
            yield

        def flip(it):
            h, i = it
            n = 4 * h + i
            u, tb = n % 2, 4 + n % 2
            p, pt = blk(P, u), blk(PT, u)
            for kb in range(4):
                t = tr(PS[tb][:, 128 * kb:128 * kb + 128], p[:, 128 * kb:128 * kb + 128], IDN, state[n], free[tb], inc=(kb == 3))
            pfree[u] = t
            if i % 4:
                c = AC.op(lambda e: e.activation(pt, PS[tb][:, :], ACT.Copy), t, ptfree[u])
            else:
                c = DV.op(lambda e: e.tensor_copy(pt, PS[tb][:, :]), t, ptfree[u])
            state[n] = free[tb] = c
            yield

        def values(it):
            h, i = it
            n, kv = 4 * h + i, h // 4
            pt = blk(PT, n % 2)
            for kb in range(4):
                t = mm(PS[7][:, 64 * i:64 * i + 64], pt[:, 128 * kb:128 * kb + 128],
                       V[:, 128 * kb + 64 * kv:128 * kb + 64 * kv + 64], kb == 0, kb == 3, state[n], free[7], vt, inc=(kb == 3))
            ptfree[n % 2] = t
            if i == 3:
                rc = RC[:, 4 * h:4 * h + 4]
                DV.op(lambda e: e.reciprocal(rc, SU[:, 4 * h:4 * h + 4]), AC.last())
                dst = OT[:, :].rearrange("p (c n) -> p c n", c=4)[:, :, 64 * h:64 * h + 64]
                d = DV.op(lambda e: e.tensor_tensor(dst, PS[7][:, 0:256].rearrange("p (c n) -> p c n", c=4),
                                                    rc.unsqueeze(2).to_broadcast([128, 4, 64]), ALU.mult), t)
                free[7] = state["o"] = d
            yield

        def turn(it):
            h, i = it
            if h % 2 and i == 3:
                j = h // 2
                for c in range(4):
                    t = tr(PS[6][:, 128 * c:128 * c + 128], OT[:, 512 * c + 128 * j:512 * c + 128 * j + 128], IDN,
                           free[6], state["o"], inc=(c == 3))
                free[6] = ohtok[j] = split(PS[6][:, :], blk(OTH, j), blk(OTL, j), t)
                yield

        o2 = o
        BC = at("cBC", 2048, F32, o2); o2 += 8 * K
        BT = at("cBT", 1024, F32, o2); o2 += 4 * K
        XS = at("cXS", 4096, F32, o2); o2 += 16 * K
        CVT = at("cCVT", 1024, F32, o2); o2 += 4 * K
        CTH = FP[:, 1152:2176]
        thfree = [None, None]
        hw, hn = sm["sw0"][0], 72
        DV.op(lambda e: e.tensor_scalar(SM[:, hw:hw + hn], SM[:, hw:hw + hn], 0.5, None, ALU.mult))
        cfree = [None, None]
        xst = [None] * 8
        bct = [None] * 4
        btt = [None] * 2

        CU = [FP[:, 2176:2688], FP[:, 2688:3200]]
        cufree = [None, None]
        turns = []

        def xbc(i):
            r = lin_fm([("cx", i)], XHk, XLk, XTk)
            until(lambda: all(qt))
            while turns:
                xturn(*turns.pop(0))
            for jj, (bank, tok) in enumerate(r):
                j = 2 * i + jj
                free[bank] = AC.op(lambda e, j=j, bank=bank: e.activation(CU[j % 2], PS[bank][:, :], ACT.Copy),
                                   tok, cufree[j % 2], qt)
                chores.append(xconv(j, free[bank]))

        def xconv(j, a):
            u, y = CU[j % 2], blk(CVT, j % 2)
            a = AC.op(lambda e: e.activation(y, u, ACT.Identity, bias=col("sb", j), scale=col("sw2", j)),
                      a, cfree[j % 2], start)
            yield
            for t in (0, 1, 3, 4):
                s = t - 2
                oa, ob_ = max(0, -s), 512 - max(0, s)
                d = DV.op(lambda e, t=t, s=s, oa=oa, ob_=ob_: e.scalar_tensor_tensor(
                    out=y[:, oa:ob_], in0=u[:, oa + s:ob_ + s], scalar=col(f"sw{t}", j), in1=y[:, oa:ob_],
                    op0=ALU.mult, op1=ALU.add), a)
                yield
            cufree[j % 2] = d
            th = blk(CTH, j % 2)
            a = AC.op(lambda e: e.activation(th, y, ACT.Tanh), d, thfree[j % 2])
            yield
            src = y if j < 8 else blk(BC, j - 8)
            a = thfree[j % 2] = DV.op(lambda e: e.scalar_tensor_tensor(
                out=src, in0=th, scalar=1.0, in1=y, op0=ALU.add, op1=ALU.mult), a)
            if j >= 8:
                cfree[j % 2] = bct[j - 8] = a
            if j < 10:
                turns.append((j, src, a))

        def xturn(j, src, a):
            for c in range(4):
                t = tr(PS[6][:, 128 * c:128 * c + 128], src[:, 128 * c:128 * c + 128], IDN, a, free[6], inc=(c == 3))
            if j < 8:
                cfree[j % 2] = t
                dst = XS[:, :].rearrange("p (c n) -> p c n", c=4)[:, :, 128 * j:128 * j + 128]
            else:
                dst = BT[:, :].rearrange("p (c n) -> p c n", c=4)[:, :, 128 * (j - 8):128 * (j - 8) + 128]
            f = AC.op(lambda e: e.activation(dst, PS[6][:, :].rearrange("p (c n) -> p c n", c=4), ACT.Copy), t, start)
            free[6] = f
            if j < 8:
                xst[j] = f
            else:
                btt[j - 8] = f

        dtraw = []
        lin_bank[1] = [0, 1]
        def attention():
            for _ in prep():
                for _ in range(SLOW):
                    yield
            yield from staggered([(h, i) for h in range(8) for i in range(4)], [scores, flip, values, turn], LAGS)
        alongside(attention(), RATES[4])
        qk_units(("ck", 0), 4, (128,), together=True)
        qk_units(("cq", 0), 0)
        qk_units(("cq", 1), 2)
        lin_tm(("cv", 0), XHk, XLk, XTk, evac)
        dtraw += [vt[-1], DV.last()]
        beside[1] = RATES[2]
        for i in range(6):
            xbc(i)
        drain()

        start2 = marks()
        o = E0
        Y = at("cY", 4096, F32, o); o += 16 * K
        CB = at("cCB", 1024, F32, o); o += 4 * K
        RF = at("cRF", 1024, F32R, o, 48); o += 4 * K
        EM = at("cEM", 2048, F32, o); o += 8 * K
        XD = at("cXD", 1024, F32, o); o += 4 * K
        assert o <= E0 + 36 * K
        o = o2 - 4 * K
        PRV = FP[:, 1152:3200]
        XW = at("cXW", 1024, F32, o); o += 4 * K
        YT_ = at("cYT", 512, F32, E0 + 36 * K)

        nacd, dec = acs["nac"], acs["dec"]
        for dr in range(2):
            for c in range(4):
                t = tr(PS[4 + dr][0:16, 128 * c:128 * c + 128], ACS[:, 32 * c + 16 * dr:32 * c + 16 * dr + 16], IDN,
                       nacd, free[4 + dr], start2, inc=(c == 3))
            rfd = split_rows(RF[:, 512 * dr:512 * dr + 512], PS[4 + dr][0:16, :], t)
            free[4 + dr] = rfd
        for g in range(2):
            for c in range(4):
                s = slice(512 * g + 128 * c, 512 * g + 128 * c + 128)
                s2 = slice(1024 + 512 * g + 128 * c, 1024 + 512 * g + 128 * c + 128)
                t = mm(PS[6][:, 128 * c:128 * c + 128], BC[:, s], BC[:, s2], True, True, bct, free[6], inc=(c == 3))
            cbd = DV.op(lambda e, g=g: e.tensor_copy(blk(CB, g), PS[6][:, :]), t)
            free[6] = cbd
        yv = Y[:, :].rearrange("p (c n) -> p c n", c=4)
        for c in range(4):
            src = XS[:, 1024 * c:1024 * c + 1024].rearrange("p (h n) -> p h n", h=16)
            dst = Y[:, 1024 * c:1024 * c + 1024].rearrange("p (h n) -> p h n", h=16)
            yt0 = PO.op(lambda e, src=src, dst=dst: e.tensor_tensor(
                dst, src, col("dskip", 0, 16).unsqueeze(2).to_broadcast([128, 16, 64]), ALU.mult), xst, start2)

        emfree = [None, None]
        xdfree = [None, None]

        def shead(h):
            g, u = h // 8, h % 2
            em = [EM[:, 1024 * u + 512 * dr:1024 * u + 512 * dr + 512] for dr in range(2)]
            xd = [XD[:, 512 * u + 256 * dr:512 * u + 256 * dr + 256] for dr in range(2)]
            mt = []
            for dr in range(2):
                bank = 2 + dr + 2 * u
                mm(PS[bank][:, :], SEL[0:48, h:h + 1].to_broadcast([48, 128]), RF[:, 512 * dr:512 * dr + 512], True, False,
                   rfd, free[bank])
                t = mm(PS[bank][:, :], IDB, MF if dr == 0 else MB, False, True, inc=True)
                for c in range(4):
                    n = 32 * c + 16 * dr + h
                    a = AC.op(lambda e, c=c, n=n, dr=dr, bank=bank: e.activation(
                        em[dr][:, 128 * c:128 * c + 128], PS[bank][:, 128 * c:128 * c + 128], ACT.Exp,
                        bias=NAC[:, n:n + 1]), t, nacd, emfree[u])
                free[bank] = a
                mt.append(DV.op(lambda e, dr=dr: e.tensor_tensor(em[dr], em[dr], blk(CB, g), ALU.mult), a))
                xs = XS[:, :].rearrange("p (c n) -> p c n", c=4)[:, :, 64 * h:64 * h + 64]
                dt = DT[:, :].rearrange("p (c n) -> p c n", c=4)[:, :, 16 * dr + h:16 * dr + h + 1]
                mt.append(PO.op(lambda e, dr=dr, xs=xs, dt=dt: e.tensor_tensor(
                    xd[dr].rearrange("p (c n) -> p c n", c=4), xs, dt.to_broadcast([128, 4, 64]), ALU.mult),
                    xst, xdfree[u], start2))
            state["m", h] = mt
            yield

        def syvals(h):
            u = h % 2
            em = [EM[:, 1024 * u + 512 * dr:1024 * u + 512 * dr + 512] for dr in range(2)]
            xd = [XD[:, 512 * u + 256 * dr:512 * u + 256 * dr + 256] for dr in range(2)]
            mt = state["m", h]
            for c in range(4):
                for dr in range(2):
                    t = mm(PS[7][:, 64 * c:64 * c + 64], em[dr][:, 128 * c:128 * c + 128], xd[dr][:, 64 * c:64 * c + 64],
                           dr == 0, dr == 1, mt, free[7], inc=(c == 3 and dr == 1))
            emfree[u] = xdfree[u] = t
            dst = yv[:, :, 64 * h:64 * h + 64]
            d = DV.op(lambda e: e.tensor_tensor(dst, PS[7][:, 0:256].rearrange("p (c n) -> p c n", c=4), dst, ALU.add), t, yt0)
            free[7] = d
            sdone[0] = h + 1
            yield

        sdone = [0]

        def states(dr):
            cs = (0, 1, 2, 3) if dr == 0 else (3, 2, 1, 0)
            prv = PRV[:, 1024 * dr:1024 * dr + 1024]
            h8 = lambda t: t.rearrange("p (h n) -> p h n", h=8)
            read = [None, None]
            for idx, c in enumerate(cs):
                at_c = 32 * c + 16 * dr
                if idx:
                    for g in range(2):
                        b = pick()
                        t = mm(PS[b][:, :], BC[:, 1024 + 512 * g + 128 * c:1024 + 512 * g + 128 * c + 128],
                               blk(prv, g), True, True, free[b], bct, prv_t[dr], inc=True)
                        read[g] = t
                        sc = EAC[:, at_c + 8 * g:at_c + 8 * g + 8]
                        free[b] = DV.op(lambda e, b=b, sc=sc: e.tensor_tensor(
                            h8(YT_[:, :]), h8(PS[b][:, :]), sc.unsqueeze(2).to_broadcast([128, 8, 64]), ALU.mult),
                            t, dec, start2)
                        dst = Y[:, 1024 * c + 512 * g:1024 * c + 512 * g + 512]
                        DV.op(lambda e, dst=dst: e.tensor_tensor(dst, dst, YT_[:, :], ALU.add), yt0)
                    yield
                if idx < 3:
                    for g in range(2):
                        xw = blk(XW, dr)
                        sc = DSD[:, at_c + 8 * g:at_c + 8 * g + 8]
                        p = PO.op(lambda e, g=g, sc=sc: e.tensor_tensor(
                            h8(xw), h8(XS[:, 1024 * c + 512 * g:1024 * c + 512 * g + 512]),
                            sc.unsqueeze(2).to_broadcast([128, 8, 64]), ALU.mult), dec, xst, xwfree[dr], start2)
                        if idx:
                            cd = CD[:, at_c + 8 * g:at_c + 8 * g + 8]
                            dcy = PO.op(lambda e, g=g, cd=cd: e.tensor_tensor(
                                h8(blk(prv, g)), h8(blk(prv, g)), cd.unsqueeze(2).to_broadcast([128, 8, 64]), ALU.mult),
                                read[g], prv_t[dr])
                        yield
                        b = pick()
                        t = xwfree[dr] = mm(PS[b][:, :], BT[:, 256 * c + 128 * g:256 * c + 128 * g + 128], xw, True, True,
                                            free[b], p, btt, inc=True)
                        if idx == 0:
                            d = DV.op(lambda e, g=g, b=b: e.tensor_copy(blk(prv, g), PS[b][:, :]), t, start2)
                        else:
                            d = DV.op(lambda e, g=g, b=b: e.tensor_tensor(blk(prv, g), blk(prv, g), PS[b][:, :], ALU.add),
                                      t, dcy)
                        free[b] = d
                    prv_t[dr] = d
            finished[dr] = True

        prv_t, xwfree, finished = [None, None], [None, None], [False, False]

        def scans():
            left = [states(0), states(1)]
            for n, _ in enumerate(staggered(list(range(16)), [shead, syvals], [0, 2])):
                yield
                for i in range(PACE):
                    next(left[(PACE * n + i) % 2], None)
        alongside(scans(), RATES[3])
        until(lambda: sdone[0] >= 4 and all(finished))
        for i in range(4):
            def evac(c, ps, tok):
                if c == 0:
                    until(lambda: sdone[0] >= 4 * i + 4)
                z, z2 = XW[:, 512 * (c % 2):512 * (c % 2) + 256], XW[:, 512 * (c % 2) + 256:512 * (c % 2) + 512]
                y = Y[:, 1024 * c + 256 * i:1024 * c + 256 * i + 256]
                a = AC.op(lambda e: e.activation(z, ps[:, 0:256], ACT.Tanh, scale=0.5), tok, zfree[c % 2], z0)
                d = DV.op(lambda e: e.scalar_tensor_tensor(out=z2, in0=z, scalar=1.0, in1=ps[:, 0:256],
                                                           op0=ALU.add, op1=ALU.mult), a)
                zfree[c % 2] = DV.op(lambda e: e.tensor_tensor(y, y, z2, ALU.mult), d)
                return d
            zfree, z0 = [None, None], marks()
            lin_tm(("cz", i), XHk, XLk, XTk, evac)
        drain()
        lin_bank[1] = [0, 1, 2, 3, 4, 7]
        st = st_a = marks()
        for c in range(4):
            a = AC.op(lambda e, c=c: e.activation(XS[:, 0:1024], Y[:, 1024 * c:1024 * c + 1024], ACT.Square,
                                                  accum_out=SS[:, c:c + 1]), st)
        a = AC.op(lambda e: e.activation(SS[:, 4:8], SS[:, 0:4], ACT.Sqrt, bias=EPS6, scale=0.25 / D))
        d = DV.op(lambda e: e.reciprocal(SS[:, 8:12], SS[:, 4:8]), a)
        for c in range(4):
            d = DV.op(lambda e, c=c: e.tensor_scalar(Y[:, 1024 * c:1024 * c + 1024], Y[:, 1024 * c:1024 * c + 1024],
                                                     SS[:, 8 + c:9 + c], 0.5, ALU.mult, ALU.mult))
        SG = FP[:, 1152:3200]
        mtok = [None] * 8
        sgf = [None, None]

        def mix_a(i):
            ga = lin_fm([("cga", i)], XHk, XLk, XTk)
            ta = []
            for j, (bank, tok) in enumerate(ga):
                x = SG[:, 1024 * j:1024 * j + 512]
                a = AC.op(lambda e: e.activation(x, PS[bank][:, :], ACT.Sigmoid), tok, sgf[j], st_a)
                free[bank] = a
                ta.append(a)
            pa = lin_fm([("cpa", i)], lambda k: blk(OTH, k), lambda k: blk(OTL, k), lambda k: ohtok[k])
            for j, (bank, tok) in enumerate(pa):
                x = SG[:, 1024 * j:1024 * j + 512]
                d = DV.op(lambda e: e.tensor_tensor(x, x, PS[bank][:, :], ALU.mult), tok, ta)
                free[bank] = d

        def mix_b(i):
            gsr = lin_fm([("cgs", i)], XHk, XLk, XTk)
            tb = []
            for j, (bank, tok) in enumerate(gsr):
                x = SG[:, 1024 * j + 512:1024 * j + 1024]
                a = AC.op(lambda e: e.activation(x, PS[bank][:, :], ACT.Sigmoid), tok, sgf[j])
                free[bank] = a
                tb.append(a)
            psr = lin_fm([("cps", i)], lambda k: blk(YTH, k), lambda k: blk(YTL, k), lambda k: ytt[k])
            for j, (bank, tok) in enumerate(psr):
                x, x2 = SG[:, 1024 * j:1024 * j + 512], SG[:, 1024 * j + 512:1024 * j + 1024]
                d = DV.op(lambda e: e.tensor_tensor(x2, x2, PS[bank][:, :], ALU.mult), tok, tb)
                free[bank] = d
                p = PO.op(lambda e: e.tensor_tensor(x, x, x2, ALU.add), d)
                sgf[j] = mtok[2 * i + j] = split(x, blk(MIX[0], 2 * i + j), blk(MIX[1], 2 * i + j), p)
        MIX = []
        mix_a(0)
        st = marks()
        yo = E0 + 16 * K
        YTH = at("cYTH", 4096, F32R, yo)
        YTL = at("cYTL", 4096, F32R, yo + 16 * K)
        TT = at("cTT", 1024, F32, yo + 32 * K)
        ytt = [None] * 8
        for j in range(8):
            b = pick()
            for c in range(4):
                t = tr(PS[b][:, 128 * c:128 * c + 128], Y[:, 1024 * c + 128 * j:1024 * c + 128 * j + 128], IDN,
                       free[b], st, inc=(c == 3))
            tt = blk(TT, j % 2)
            f = DV.op(lambda e: e.tensor_scalar(tt, PS[b][:, :], col("ssdn", j), None, ALU.mult), t, ytt[j - 2] if j > 1 else None, st)
            free[b] = f
            ytt[j] = split(tt, blk(YTH, j), blk(YTL, j), f)
        MIXH = at("cMXH", 4096, F32R, yo + 36 * K)
        MIXL = at("cMXL", 4096, F32R, E0)
        MIX += [MIXH, MIXL]
        st = marks()
        for i in range(4):
            if i:
                mix_a(i)
            mix_b(i)
        st = marks()
        nb = norm_bufs(yo)
        nb["tok"] = st

        def evac_y(j, bank, tok, first):
            y = blk(YH, j)
            a = AC.op(lambda e: e.activation(y, PS[bank][:, :], ACT.Copy), tok, first)
            free[bank] = a
            acc_step(nb, j, y, a, False)
        for i in range(4):
            for j, (bank, tok) in enumerate(lin_fm([("co", i)], lambda k: blk(MIXH, k), lambda k: blk(MIXL, k), lambda k: mtok[k])):
                evac_y(2 * i + j, bank, tok, st)
        r = stats(nb, EPS6, False)
        nb2 = norm_bufs(yo + 14 * K)
        nb2["tok"] = st
        for j in range(8):
            y, x = blk(YH, j), blk(XR, j)
            DV.op(lambda e: e.scalar_tensor_tensor(out=y, in0=y, scalar=col("n1post", j), in1=PS[6][:, :],
                                                   op0=ALU.mult, op1=ALU.mult), r)
            free[6] = DV.last()
            d = DV.op(lambda e: e.tensor_tensor(x, x, y, ALU.add))
            acc_step(nb2, j, x, d, False)
        rms_apply(nb2, XR, None, "n2pre")
        st = marks()
        hh = at("HH2", 512 * FF, F32R, O0)
        hl = at("HL2", 512 * FF, F32R, O0 + 44 * K)
        tmp = FP[:, 1152:3200]
        htok = ffn_up_2(hh, hl, tmp, st)
        nb = {n: FP[:, 1152 + 512 * i:1664 + 512 * i] for i, n in enumerate(("SQ", "A1", "A2", "MS"))}
        st = marks()
        nb["tok"] = st

        def evac(j, bank, tok):
            y = blk(YH, j)
            a = AC.op(lambda e: e.activation(y, PS[bank][:, :], ACT.Copy), tok, st)
            free[bank] = a
            acc_step(nb, j, y, a, False)
        ffn_down("dn2", hh, hl, htok, evac)
        r = stats(nb, EPS6, False)
        outs = []
        for j in range(8):
            y, x = blk(YH, j), blk(XR, j)
            DV.op(lambda e: e.scalar_tensor_tensor(out=y, in0=y, scalar=col("n2post", j), in1=PS[6][:, :],
                                                   op0=ALU.mult, op1=ALU.mult), r)
            d = (PO if j % 2 else DV).op(lambda e: e.tensor_tensor(x, x, y, ALU.add), DV.last())
            sp(lambda e, j=j, x=x: e.dma_start(outT[:, 512 * j:512 * j + 512], x).then_inc(s_out, 16), d)

    def ffn_up_2(hh, hl, tmp, st):
        return ffn_up("up2", None, hh, hl, tmp, st)

    oh, ol, ot, _ = fox()
    attn_out("ao", oh, ol, ot, "ln_attn_g0", "ln_attn_b0")
    nb = ffn_layer("0", "", "")
    layer_norm(nb, "ln_ffn_g0", "ln_ffn_b0")
    oh, ol, ot, _ = diff()
    attn_out("bo", oh, ol, ot, "ln_attn_g1", "ln_attn_b1")
    nb = ffn_layer("1", "", "")
    XR = at("XR", 4096, F32, R0)
    nb0 = norm_bufs(R0 + 40 * K)
    layer_norm(nb, "ln_ffn_g1", "ln_ffn_b1", final=lambda j: blk(XR, j),
               post=lambda j, a: acc_step(nb0, j, blk(XR, j), a, False))
    second(XR, nb0)
    if turn == "sp":
        engine.wait_ge(s_out, 16 * 8)
    return used


def whole(nc, *args):
    mem = {}
    order = program(nc, *args, None, mem, None, None)
    with nc.Block() as block:
        @block.sync
        def _(e):
            program(nc, *args, order, mem, "sp", e)

        @block.tensor
        def _(e):
            program(nc, *args, order, mem, "pe", e)

        @block.scalar
        def _(e):
            program(nc, *args, order, mem, "act", e)

        @block.vector
        def _(e):
            program(nc, *args, order, mem, "dve", e)

        @block.gpsimd
        def _(e):
            program(nc, *args, order, mem, "pool", e)


def kernel(**inputs):
    import concourse.bacc as bacc
    from concourse.bass_utils import run_bass_kernel_spmd

    a = {k: np.asarray(v) for k, v in inputs.items()}
    w = {"a_w_in": a["a_w_in"][0], "a_w_out": a["a_w_out"][0], "kv_w": a["kv_w"], "b_w_q": a["b_w_q"][0],
         "b_w_out": a["b_w_out"][0], "w_in_2": a["w_in_2"][0], "w_attn_proj_2": a["w_attn_proj_2"][0],
         "w_ssd_proj_2": a["w_ssd_proj_2"][0], "w_out_2": a["w_out_2"][0], "w_gate_up_2": a["w_gate_up_2"][0],
         "w_down_2": a["w_down_2"][0]}
    for i in range(2):
        w[f"ffn_w_in{i}"], w[f"ffn_w_out{i}"] = a["ffn_w_in"][i], a["ffn_w_out"][i]
    places, total = unit_places()
    wall = np.empty(total, np.float32)
    for key, parts in unit_table().items():
        off, kt, n = places[key]
        m = np.concatenate([w[s][128 * k0:128 * (k0 + kk)][:, c] for s, k0, kk, c in parts], axis=1)
        wall[off:off + 128 * kt * n] = m.reshape(kt, 128, n).transpose(1, 0, 2).reshape(-1)

    sm, nsm = small_table()
    small = np.zeros((128, nsm), np.float32)

    def put(name, v, rep=False):
        o, n = sm[name]
        v = np.asarray(v)
        small[:, o:o + n] = np.broadcast_to(v.reshape(1, n), (128, n)) if rep else v.reshape(n, 128).T

    for i in range(2):
        put(f"ln_attn_g{i}", a["ln_attn_g"][i])
        put(f"ln_attn_b{i}", a["ln_attn_b"][i])
        put(f"ln_ffn_g{i}", a["ln_ffn_g"][i])
        put(f"ln_ffn_b{i}", a["ln_ffn_b"][i])
        for t in range(3):
            put(f"cw{i}{t}", a["ffn_conv_w"][i, t])
        put(f"cb{i}", a["ffn_conv_b"][i])
    for t in range(5):
        put(f"sw{t}", a["conv_w_2"][0, t])
    put("sb", a["conv_b_2"][0])
    for n, s in (("n1pre", "norm1_pre_2"), ("n1post", "norm1_post_2"), ("n2pre", "norm2_pre_2"),
                 ("n2post", "norm2_post_2"), ("ssdn", "ssd_norm_2")):
        put(n, a[s][0])
    t64 = turned(0)
    put("qn", np.concatenate([a["q_norm_2"][0][t64]] * 2))
    put("kn", np.concatenate([a["k_norm_2"][0][t64]] * 2))
    small[0:16, sm["bf"][0]] = a["a_b_f"][0]
    put("subln", a["b_subln_g"][0])
    put("lam", a["b_lambda"][0].reshape(-1), True)
    put("dtb", np.concatenate([a["dt_bias_f_2"][0], a["dt_bias_b_2"][0]]), True)
    put("alog", np.concatenate([a["a_log_f_2"][0], a["a_log_b_2"][0]]), True)
    put("dskip", a["d_skip_2"][0], True)
    fp, masks = const_arrays()
    xT = np.ascontiguousarray(a["x"][0].T.reshape(8, 128, S).transpose(1, 0, 2).reshape(128, 8 * S))
    arrays = {"xT": xT, "wall": wall, "small": small, "cfp": fp, "cmask": masks}

    nc = bacc.Bacc("TRN2", target_bir_lowering=False, num_devices=1)
    aps = [nc.dram_tensor(k, v.shape, mybir.dt.from_np(v.dtype), kind="ExternalInput").ap() for k, v in arrays.items()]
    out = nc.dram_tensor("outT", (128, 8 * S), F32, kind="ExternalOutput").ap()
    whole(nc, *aps, out)
    r = run_bass_kernel_spmd(nc, [arrays], core_ids=[0])
    o = r.results[0]["outT"]
    return np.ascontiguousarray(o.reshape(128, 8, S).transpose(1, 0, 2).reshape(D, S).T).reshape(1, S, D)
```
